# Optimizing a Trainium2 kernel written in Bass

```python
import math, functools
import jax, jax.numpy as jnp
from jax import lax
import numpy as np

D_MODEL = 2048
BATCH = 1
SEQ = 512
DEPTH = 1
DEC_BATCH = 8
DEC_SEQ = 1
PAST_LEN = 2048
PAGE_SIZE = 128

N_META = 16
D_SSM = D_MODEL // 2
SSM_GROUP = 16
N_GROUPS = D_SSM // SSM_GROUP
N_STATE = 64
DT_MIN = 1e-3
DT_MAX = 1e-1
D_ATT = D_MODEL - D_SSM
V_HEAD = 128
N_HEADS = D_ATT // V_HEAD
QK_NOPE = 128
QK_ROPE = 64
KV_LORA = 512
Q_LORA = 768
ROPE_THETA = 10000.0
SOFTMAX_SCALE = (QK_NOPE + QK_ROPE) ** -0.5
Q_BLOCK = 128
EPS = 1e-6
SPLIT_IDX = (D_SSM, 2 * D_SSM, 2 * D_SSM + Q_LORA, 2 * D_SSM + Q_LORA + KV_LORA,
             2 * D_SSM + Q_LORA + KV_LORA + QK_ROPE)
D_IN_PROJ = 2 * D_SSM + Q_LORA + KV_LORA + QK_ROPE + D_ATT

kernel_name = "hymba_s5_mla_decode_step"

def rmsnorm(x, g):
    xf = x.astype(jnp.float32)
    y = xf * lax.rsqrt(jnp.mean(xf * xf, axis=-1, keepdims=True) + EPS)
    return (y * g.astype(jnp.float32)).astype(x.dtype)

def rope(x, pos):
    half = QK_ROPE // 2
    inv = ROPE_THETA ** (-jnp.arange(half, dtype=jnp.float32) / half)
    ang = pos.astype(jnp.float32)[:, None] * inv[None, :]
    ang = ang.reshape((ang.shape[0],) + (1,) * (x.ndim - 3) + (half,))
    cos, sin = jnp.cos(ang), jnp.sin(ang)
    xf = x.astype(jnp.float32)
    x1, x2 = xf[..., :half], xf[..., half:]
    return jnp.concatenate([x1 * cos - x2 * sin, x1 * sin + x2 * cos], axis=-1).astype(x.dtype)

def ssm_discretize(a_re, a_im, log_dt, b_re, b_im):
    dt = jnp.exp(log_dt.astype(jnp.float32))[:, None]
    ar, ai = a_re.astype(jnp.float32), a_im.astype(jnp.float32)
    mag = jnp.exp(dt * ar)
    abr, abi = mag * jnp.cos(dt * ai), mag * jnp.sin(dt * ai)
    den = ar * ar + ai * ai
    nr, ni = abr - 1.0, abi
    f_re = (nr * ar + ni * ai) / den
    f_im = (ni * ar - nr * ai) / den
    br, bi = b_re.astype(jnp.float32), b_im.astype(jnp.float32)
    bbr = f_re[..., None] * br - f_im[..., None] * bi
    bbi = f_re[..., None] * bi + f_im[..., None] * br
    return abr, abi, bbr, bbi

def _ssm_combine(e1, e2):
    a1r, a1i, b1r, b1i = e1
    a2r, a2i, b2r, b2i = e2
    return (a1r * a2r - a1i * a2i,
            a1r * a2i + a1i * a2r,
            a2r * b1r - a2i * b1i + b2r,
            a2r * b1i + a2i * b1r + b2i)

def ssm_scan(u, h0r, h0i, abr, abi, bbr, bbi, c_re, c_im):
    bu_r = jnp.einsum('gnc,blgc->blgn', bbr, u)
    bu_i = jnp.einsum('gnc,blgc->blgn', bbi, u)
    bu_r = bu_r.at[:, 0].add(abr * h0r - abi * h0i)
    bu_i = bu_i.at[:, 0].add(abr * h0i + abi * h0r)
    a_r = jnp.broadcast_to(abr, bu_r.shape)
    a_i = jnp.broadcast_to(abi, bu_i.shape)
    _, _, hr, hi = lax.associative_scan(_ssm_combine, (a_r, a_i, bu_r, bu_i), axis=1)
    y = (jnp.einsum('gcn,blgn->blgc', c_re.astype(jnp.float32), hr)
         - jnp.einsum('gcn,blgn->blgc', c_im.astype(jnp.float32), hi))
    return y, hr[:, -1], hi[:, -1]

def mla_prompt_attn(q_abs, q_pe, c, k_pe, w_uv):
    bsz, seq = q_abs.shape[0], q_abs.shape[1]
    nb = -(-seq // Q_BLOCK)
    padded = nb * Q_BLOCK
    pad = ((0, 0), (0, padded - seq), (0, 0), (0, 0))
    qa, qp = jnp.pad(q_abs, pad), jnp.pad(q_pe, pad)
    kpos = jnp.arange(seq)

    def block(i):
        start = i * Q_BLOCK
        qa_b = lax.dynamic_slice_in_dim(qa, start, Q_BLOCK, axis=1)
        qp_b = lax.dynamic_slice_in_dim(qp, start, Q_BLOCK, axis=1)
        sc = (jnp.einsum('bqhr,bkr->bhqk', qa_b, c).astype(jnp.float32)
              + jnp.einsum('bqhe,bke->bhqk', qp_b, k_pe).astype(jnp.float32)) * SOFTMAX_SCALE
        qpos = start + jnp.arange(Q_BLOCK)
        sc = jnp.where(kpos[None, :] <= qpos[:, None], sc, -jnp.inf)
        w = jax.nn.softmax(sc, axis=-1).astype(c.dtype)
        o_lat = jnp.einsum('bhqk,bkr->bqhr', w, c)
        return jnp.einsum('bqhr,rhv->bqhv', o_lat, w_uv)

    o = lax.map(block, jnp.arange(nb))
    o = o.transpose(1, 0, 2, 3, 4).reshape(bsz, padded, N_HEADS, V_HEAD)
    return o[:, :seq]

def mla_sample_attn(q_abs, q_pe, c_new, kpe_new, c_pool, kpe_pool, page_table, w_uv):
    dbs, sq = q_abs.shape[0], q_abs.shape[1]
    c_past = c_pool[page_table].reshape(dbs, -1, KV_LORA)
    kpe_past = kpe_pool[page_table].reshape(dbs, -1, QK_ROPE)
    n_past = c_past.shape[1]
    s_past = (jnp.einsum('bqhr,bkr->bhqk', q_abs, c_past).astype(jnp.float32)
              + jnp.einsum('bqhe,bke->bhqk', q_pe, kpe_past).astype(jnp.float32)) * SOFTMAX_SCALE
    s_new = (jnp.einsum('bqhr,bkr->bhqk', q_abs, c_new).astype(jnp.float32)
             + jnp.einsum('bqhe,bke->bhqk', q_pe, kpe_new).astype(jnp.float32)) * SOFTMAX_SCALE
    causal = jnp.tril(jnp.ones((sq, sq), dtype=bool))
    s_new = jnp.where(causal, s_new, -jnp.inf)
    w = jax.nn.softmax(jnp.concatenate([s_past, s_new], axis=-1), axis=-1).astype(c_new.dtype)
    o_lat = (jnp.einsum('bhqk,bkr->bqhr', w[..., :n_past], c_past)
             + jnp.einsum('bhqk,bkr->bqhr', w[..., n_past:], c_new))
    return jnp.einsum('bqhr,rhv->bqhv', o_lat, w_uv)

def mixer(xn, pos, h0r, h0i, attend, w_in, a_re, a_im, log_dt, b_re, b_im, c_re, c_im,
          d_skip, w_glu, b_glu, g_qn, w_uq, g_kvn, w_uk, w_out):
    bsz, seq, _ = xn.shape
    proj = xn @ w_in
    u, zs, cq, ckv, kpe, za = jnp.split(proj, SPLIT_IDX, axis=-1)
    uf = u.astype(jnp.float32)
    abr, abi, bbr, bbi = ssm_discretize(a_re, a_im, log_dt, b_re, b_im)
    ys, hr, hi = ssm_scan(uf.reshape(bsz, seq, N_GROUPS, SSM_GROUP), h0r.astype(jnp.float32),
                          h0i.astype(jnp.float32), abr, abi, bbr, bbi, c_re, c_im)
    ys = ys.reshape(bsz, seq, D_SSM) + d_skip.astype(jnp.float32) * uf
    ys = jax.nn.gelu(ys).astype(xn.dtype)
    ys = ys * jax.nn.sigmoid(ys @ w_glu + b_glu)
    ssm_out = ys * jax.nn.silu(zs)
    q = (rmsnorm(cq, g_qn) @ w_uq).reshape(bsz, seq, N_HEADS, QK_NOPE + QK_ROPE)
    q_nope, q_pe = q[..., :QK_NOPE], rope(q[..., QK_NOPE:], pos)
    q_abs = jnp.einsum('blhd,rhd->blhr', q_nope, w_uk)
    c = rmsnorm(ckv, g_kvn)
    k_pe = rope(kpe, pos)
    o = attend(q_abs, q_pe, c, k_pe)
    att_out = o.reshape(bsz, seq, D_ATT) * jax.nn.silu(za)
    y = jnp.concatenate([ssm_out, att_out], axis=-1) @ w_out
    return y, c, k_pe, hr, hi

def setup_inputs(seed: int = 0) -> dict:
    key = jax.random.key(seed)
    ks = jax.random.split(key, 28)
    f32 = jnp.float32
    n_pages = PAST_LEN // PAGE_SIZE
    n_pool = (DEC_BATCH * n_pages * 5) // 4

    def nrm(k, shape, std):
        return jax.random.normal(k, shape, f32) * std

    page_table = jax.random.permutation(ks[6], n_pool)[: DEC_BATCH * n_pages]
    page_table = page_table.reshape(DEC_BATCH, n_pages).astype(jnp.int32)
    n_idx = jnp.arange(N_STATE, dtype=f32)
    return {
        'x_prompt': nrm(ks[0], (BATCH, SEQ, D_MODEL), 1.0),
        'x_sample': nrm(ks[1], (DEC_BATCH, DEC_SEQ, D_MODEL), 1.0),
        'cache_ckv': nrm(ks[2], (DEPTH, n_pool, PAGE_SIZE, KV_LORA), 1.0),
        'cache_kpe': nrm(ks[3], (DEPTH, n_pool, PAGE_SIZE, QK_ROPE), 1.0),
        'state_ssm_re': nrm(ks[4], (DEPTH, DEC_BATCH, N_GROUPS, N_STATE), 0.1),
        'state_ssm_im': nrm(ks[5], (DEPTH, DEC_BATCH, N_GROUPS, N_STATE), 0.1),
        'page_table': page_table,
        'meta_tokens': nrm(ks[7], (N_META, D_MODEL), 1.0),
        'g_norm': 1.0 + nrm(ks[8], (DEPTH, D_MODEL), 0.02),
        'w_in': nrm(ks[9], (DEPTH, D_MODEL, D_IN_PROJ), D_MODEL ** -0.5),
        'ssm_a_re': -0.5 + nrm(ks[10], (DEPTH, N_GROUPS, N_STATE), 0.01),
        'ssm_a_im': jnp.pi * n_idx + nrm(ks[11], (DEPTH, N_GROUPS, N_STATE), 0.01),
        'ssm_log_dt': jax.random.uniform(ks[12], (DEPTH, N_GROUPS), f32,
                                         math.log(DT_MIN), math.log(DT_MAX)),
        'ssm_b_re': nrm(ks[13], (DEPTH, N_GROUPS, N_STATE, SSM_GROUP), (2 * SSM_GROUP) ** -0.5),
        'ssm_b_im': nrm(ks[14], (DEPTH, N_GROUPS, N_STATE, SSM_GROUP), (2 * SSM_GROUP) ** -0.5),
        'ssm_c_re': nrm(ks[15], (DEPTH, N_GROUPS, SSM_GROUP, N_STATE), N_STATE ** -0.5),
        'ssm_c_im': nrm(ks[16], (DEPTH, N_GROUPS, SSM_GROUP, N_STATE), N_STATE ** -0.5),
        'ssm_d': nrm(ks[17], (DEPTH, D_SSM), 1.0),
        'w_glu': nrm(ks[18], (DEPTH, D_SSM, D_SSM), D_SSM ** -0.5),
        'b_glu': nrm(ks[19], (DEPTH, D_SSM), 0.02),
        'g_q_norm': 1.0 + nrm(ks[20], (DEPTH, Q_LORA), 0.02),
        'w_uq': nrm(ks[21], (DEPTH, Q_LORA, N_HEADS * (QK_NOPE + QK_ROPE)), Q_LORA ** -0.5),
        'g_kv_norm': 1.0 + nrm(ks[22], (DEPTH, KV_LORA), 0.02),
        'w_uk': nrm(ks[23], (DEPTH, KV_LORA, N_HEADS, QK_NOPE), KV_LORA ** -0.5),
        'w_uv': nrm(ks[24], (DEPTH, KV_LORA, N_HEADS, V_HEAD), KV_LORA ** -0.5),
        'w_out': nrm(ks[25], (DEPTH, D_MODEL, D_MODEL), D_MODEL ** -0.5),
        'g_final': 1.0 + nrm(ks[26], (D_MODEL,), 0.02),
    }

def reference(x_prompt, x_sample, cache_ckv, cache_kpe, state_ssm_re, state_ssm_im, page_table,
              meta_tokens, g_norm, w_in, ssm_a_re, ssm_a_im, ssm_log_dt, ssm_b_re, ssm_b_im,
              ssm_c_re, ssm_c_im, ssm_d, w_glu, b_glu, g_q_norm, w_uq, g_kv_norm, w_uk, w_uv,
              w_out, g_final):
    bsz = x_prompt.shape[0]
    meta = jnp.broadcast_to(meta_tokens.astype(x_prompt.dtype)[None], (bsz, N_META, D_MODEL))
    hp = jnp.concatenate([meta, x_prompt], axis=1)
    pos_p = jnp.arange(hp.shape[1], dtype=jnp.int32)
    hs = x_sample
    past_len = page_table.shape[1] * cache_ckv.shape[2]
    pos_s = past_len + jnp.arange(hs.shape[1], dtype=jnp.int32)
    zero_state = jnp.zeros((bsz, N_GROUPS, N_STATE), jnp.float32)

    ckv_p, kpe_p, sre_p, sim_p = [], [], [], []
    ckv_s, kpe_s, sre_s, sim_s = [], [], [], []
    for l in range(DEPTH):
        lw = (w_in[l], ssm_a_re[l], ssm_a_im[l], ssm_log_dt[l], ssm_b_re[l], ssm_b_im[l],
              ssm_c_re[l], ssm_c_im[l], ssm_d[l], w_glu[l], b_glu[l], g_q_norm[l], w_uq[l],
              g_kv_norm[l], w_uk[l], w_out[l])
        attend_p = functools.partial(mla_prompt_attn, w_uv=w_uv[l])
        yp, cp, kp, hrp, hip = mixer(rmsnorm(hp, g_norm[l]), pos_p, zero_state, zero_state,
                                     attend_p, *lw)
        hp = hp + yp
        attend_s = functools.partial(mla_sample_attn, c_pool=cache_ckv[l], kpe_pool=cache_kpe[l],
                                     page_table=page_table, w_uv=w_uv[l])
        ysm, cs, kse, hrs, his = mixer(rmsnorm(hs, g_norm[l]), pos_s, state_ssm_re[l],
                                       state_ssm_im[l], attend_s, *lw)
        hs = hs + ysm
        ckv_p.append(cp); kpe_p.append(kp)
        sre_p.append(hrp.astype(state_ssm_re.dtype)); sim_p.append(hip.astype(state_ssm_im.dtype))
        ckv_s.append(cs); kpe_s.append(kse)
        sre_s.append(hrs.astype(state_ssm_re.dtype)); sim_s.append(his.astype(state_ssm_im.dtype))

    y_prompt = rmsnorm(hp, g_final)[:, N_META:]
    y_sample = rmsnorm(hs, g_final)
    return (y_prompt, y_sample,
            jnp.stack(ckv_p), jnp.stack(kpe_p), jnp.stack(sre_p), jnp.stack(sim_p),
            jnp.stack(ckv_s), jnp.stack(kpe_s), jnp.stack(sre_s), jnp.stack(sim_s))


_drawn_inputs = setup_inputs


def setup_inputs(seed=0):
    import zlib

    import numpy as np

    out = dict(_drawn_inputs(seed))
    spreads = {}
    factors = {'cache_ckv': 3.566,
     'cache_kpe': 7.017,
     'g_norm': 2.699,
     'ssm_a_re': 16.827,
     'ssm_c_re': 3.615,
     'ssm_c_im': 4.122,
     'b_glu': 25.669,
     'g_q_norm': 8.0,
     'g_kv_norm': 2.799,
     'g_final': 8.306}
    for name, (base, spread) in spreads.items():
        noise = np.random.default_rng([zlib.crc32(name.encode()), seed]).standard_normal(out[name].shape)
        drawn = base * np.exp(spread * noise) if base else spread * noise
        out[name] = __import__('jax').numpy.asarray(drawn.astype(out[name].dtype))
    for name, factor in factors.items():
        out[name] = (out[name] * factor).astype(out[name].dtype)
    return out
```

```python
import math
from contextlib import ExitStack

import numpy as np

import concourse.bass as bass
from concourse import mybir

F32 = mybir.dt.float32
F32R = mybir.dt.float32r
ALU = mybir.AluOpType
ACT = mybir.ActivationFunctionType
AX = mybir.AxisListType
ds = bass.ds

P = 128
D_MODEL, SEQ, N_META, N_SAMPLE = 2048, 512, 16, 8
D_SSM, GROUP, N_STATE = 1024, 16, 64
N_GROUPS = D_SSM // GROUP
N_HEADS, V_HEAD, QK_NOPE, QK_ROPE = 8, 128, 128, 64
KV_LORA, Q_LORA = 512, 768
PAGE, PAST = 128, 2048
N_PAGES = PAST // PAGE
ROPE_THETA = 10000.0
EPS = 1e-6
SCALE = (QK_NOPE + QK_ROPE) ** -0.5
NEG = -1.0e30

T_PROMPT = N_META + SEQ
T = T_PROMPT + N_SAMPLE
HALVES = ((0, 264), (264, 272))
TILES = tuple((t, min(P, T - t)) for t in range(0, T, P))
KD = D_MODEL // P
CHUNK = P // GROUP
N_CHUNK = T_PROMPT // CHUNK
YCOLS = N_SAMPLE + N_CHUNK
PAIRS = N_GROUPS // 2
ENTRIES = N_SAMPLE + 1 + N_CHUNK + N_SAMPLE
COL_ZS, COL_LAT = D_SSM, 2 * D_SSM
COL_ZA = 2 * D_SSM + Q_LORA + KV_LORA + QK_ROPE

B_LAT, B_U, B_ZS, B_ZA, B_GLU, B_QN, B_QR, B_K, B_V, B_OUT, B_END = 0, 11, 19, 27, 35, 43, 51, 55, 63, 65, 81


RUNS = (B_LAT, B_U, B_ZS, B_ZA, B_GLU, B_QN, B_QR, B_K, B_V, B_OUT, B_END)


def block_width(n):
    if n < B_GLU:
        return KD * P
    if n < B_QN:
        return D_SSM
    if n < B_K:
        return Q_LORA
    if n < B_V:
        return KV_LORA
    return KV_LORA // P * 512 if n < B_OUT else KD * P


def build(nc, d):
    es = ExitStack()
    base = 16512
    used = {}

    def at(name, offset, shape, dt=F32):
        assert base + offset + math.prod(shape[1:]) * 4 <= 229344, name
        return nc.alloc_sbuf_tensor_at(name, shape, dt, offset=base + offset)

    with es:
        def sem(name):
            return es.enter_context(nc.semaphore(name))

        ROW = T * 4
        xh = at("xh", 0, [P, KD, T], F32R)
        xl = at("xl", KD * ROW, [P, KD, T], F32R)
        o = 2 * KD * ROW
        w_raw = at("w_raw", o, [P, 2, 2048])
        w_hi = at("w_hi", o + 16384, [P, 2, 2048], F32R)
        w_lo = at("w_lo", o + 32768, [P, 2, 2048], F32R)
        W_AREA = o
        o += 49152
        ident = at("ident", o, [P, P])
        ones = at("ones", o + 512, [P, P])
        causal = at("causal", o + 1024, [P, P])
        rot = at("rot", o + 1536, [P, P])
        vecs = at("vecs", o + 2048, [P, 64])
        stat = at("stat", o + 2304, [P, 64])
        o += 4096
        ev = at("ev", o, [P, 2, T])
        o += 2 * ROW
        A0 = o

        xtok = at("xtok", A0, [P, 5, D_MODEL])
        gbc = at("gbc", A0 + 40960, [P, D_MODEL])
        junk = at("junk", A0 + 49152, [P, D_MODEL])
        states = at("states", A0, [P, ENTRIES, 2, PAIRS])
        XA = A0 + ENTRIES * 256
        xgrp = at("xgrp", XA, [P, N_GROUPS, 82])
        o = XA + N_GROUPS * 82 * 4
        tmp = at("tmp", o, [P, 4, 512])
        o += 8192
        wst = at("wst", o, [P, 2, 2, 4, CHUNK, GROUP])
        bst = at("bst", o + 8192, [P, 2, 4, P])
        kall = at("kall", o + 12288, [P, D_SSM])
        cast = at("cast", o, [P, 2, 2, 4, 2, CHUNK, GROUP])
        o += 16384
        powers = at("powers", o, [P, 2, 9, PAIRS])
        coef = at("coef", o + 2304, [P, 24, PAIRS])
        bbar = at("bbar", o + 5376, [P, 2, PAIRS, GROUP])
        cbd = at("cbd", o + 9472, [P, 2, PAIRS, 2, GROUP])
        snew = at("snew", o + 17664, [P, 2, N_SAMPLE, PAIRS])
        o += 17664 + 2048
        anat = at("anat", A0 + 57344, [P, 3, P])
        snat = at("snat", A0 + 58880, [P, 2, 2, P])
        cnat = at("cnat", A0 + 60928, [P, 4, 2, P])
        vnat = at("vnat", A0 + 65024, [P, P])
        ldt = at("ldt", A0 + 65536, [P, 2])
        ychunk = at("ychunk", 0, [P, 2, CHUNK, P])
        ug = at("ug", 8192, [P, 2, T])
        yg = at("yg", 8192 + 2 * ROW, [P, 2, T])
        ys = at("ys", 8 * ROW, [P, 8, T])
        ys_hi = at("ys_hi", A0, [P, 8, T], F32R)
        ys_lo = at("ys_lo", A0 + 8 * ROW, [P, 8, T], F32R)
        ptmp = at("ptmp", 2 * KD * ROW + 49152 + 4096, [P, 4, 256])
        gate = at("gate", A0 + 16 * ROW, [P, 2, T])
        sig = at("sig", A0 + 18 * ROW, [P, 2, T])
        comb_hi, comb_lo = xh, xl
        sout = at("sout", A0 + 20 * ROW, [P, 6, P])
        A1 = A0 + 46592
        latq = at("latq", A1, [P, 6, T])
        latc = at("latc", A1 + 6 * ROW, [P, 4, T])
        sq = at("sq", A1 + 10 * ROW, [P, 2, T])
        rs = at("rs", A1 + 12 * ROW, [P, 2, T])
        vout = at("vout", A1 + 14 * ROW, [P, 2, 512])
        cos = at("cos", A1 + 14 * ROW + 4096, [P, T])
        sin = at("sin", A1 + 15 * ROW + 4096, [P, T])
        rp = at("rp", A1, [P, 5, T])
        cout = at("cout", A1 + 10 * ROW, [P, 2, KV_LORA])
        kout = at("kout", A0 + 42880, [P, 5, QK_ROPE])
        qn_hi = at("qn_hi", A0, [P, 6, T], F32R)
        qn_lo = at("qn_lo", A0 + 6 * ROW, [P, 6, T], F32R)
        cn_hi = at("cn_hi", A0 + 12 * ROW, [P, 4, T], F32R)
        cn_lo = at("cn_lo", A0 + 16 * ROW, [P, 4, T], F32R)
        hraw = at("hraw", A0, [P, 2, 3, T])
        hh = at("hh", A0 + 6 * ROW, [P, 2, 3, T], F32R)
        hl = at("hl", A0 + 12 * ROW, [P, 2, 3, T], F32R)
        kp_hi = at("kp_hi", A0 + 18 * ROW, [P, T], F32R)
        kp_lo = at("kp_lo", A0 + 19 * ROW, [P, T], F32R)
        o = A0 + 20 * ROW
        vraw = at("vraw", o, [P, 2, 5, V_HEAD])
        vh = at("vh", o + 5120, [P, 2, 5, V_HEAD], F32R)
        vl = at("vl", o + 10240, [P, 2, 5, V_HEAD], F32R)
        pt_hi = at("pt_hi", o + 15360, [P, 5, T_PROMPT], F32R)
        pt_lo = at("pt_lo", o + 15360 + 5 * T_PROMPT * 4, [P, 5, T_PROMPT], F32R)
        za = at("za", W_AREA, [P, 2, T])
        otmp = at("otmp", W_AREA + 2 * ROW, [P, 2, T])
        prob = at("prob", W_AREA + 4 * ROW, [P, 2, T_PROMPT])
        kp_raw = at("kp_raw", W_AREA + 6 * ROW, [P, T])
        ckv = at("ckv", A0, [P, 2 * N_PAGES, KV_LORA])
        kpe = at("kpe", A0 + 65536, [P, 2 * N_PAGES, QK_ROPE])
        KEYS = PAST + N_SAMPLE
        sc = [at("sc0", A0 + 73728, [P, KEYS]), at("sc1", W_AREA + 40704, [P, KEYS])]
        kt_hi = at("kt_hi", A0 + 81952, [P, 2, P], F32R)
        kt_lo = at("kt_lo", A0 + 82976, [P, 2, P], F32R)
        half2 = at("half2", A0 + 84000, [P, 512])
        ct_hi = at("ct_hi", W_AREA, [P, 2, 4, 2 * P], F32R)
        ct_lo = at("ct_lo", W_AREA + 8192, [P, 2, 4, 2 * P], F32R)
        cp_hi = at("cp_hi", W_AREA + 16384, [P, 2, 2, KV_LORA], F32R)
        cp_lo = at("cp_lo", W_AREA + 24576, [P, 2, 2, KV_LORA], F32R)
        wuk = at("wuk", W_AREA + 16384, [P, 4, N_HEADS * QK_NOPE])
        wuk_t = at("wuk_t", W_AREA, [P, N_HEADS, KV_LORA])
        cnew_hi = at("cnew_hi", W_AREA + 32768, [P, KV_LORA], F32R)
        cnew_lo = at("cnew_lo", W_AREA + 34816, [P, KV_LORA], F32R)
        olat = at("olat", W_AREA + 36864, [P, KV_LORA])
        olat_t = at("olat_t", W_AREA + 38912, [P, 4, N_HEADS, N_SAMPLE])
        qs = at("qs", W_AREA + 39936, [P, N_HEADS, N_SAMPLE])
        qps = at("qps", W_AREA + 40192, [P, N_HEADS, N_SAMPLE])
        kpn_raw = at("kpn_raw", W_AREA + 40448, [P, N_SAMPLE])
        EV0 = 2 * KD * ROW + 49152 + 4096
        p_t = at("p_t", EV0, [P, N_PAGES + 1, 40], F32R)
        qa = at("qa", EV0 + 2720, [P, 6, N_SAMPLE, N_HEADS])
        C0 = 2 * KD * ROW + 49152
        ptab = nc.alloc_sbuf_tensor_at("ptab", [1, N_SAMPLE * N_PAGES], mybir.dt.int32, offset=base + C0 + 1536)
        q_st = at("q_st", C0 + 2560, [P, 6, 40], F32R)
        cnt_hi = at("cnt_hi", C0 + 3520, [P, 4, N_SAMPLE], F32R)
        cnt_lo = at("cnt_lo", C0 + 3648, [P, 4, N_SAMPLE], F32R)
        not_own = at("not_own", C0 + 3776, [N_SAMPLE, N_SAMPLE, N_SAMPLE])
        kpn_hi = at("kpn_hi", C0 + 4032, [P, N_SAMPLE], F32R)
        kpn_lo = at("kpn_lo", C0 + 4064, [P, N_SAMPLE], F32R)
        wuv = at("wuv", A0, [P, 4, N_HEADS * V_HEAD])
        yt = at("yt", A0 + 16384, [P, 4, D_MODEL])
        ysm = at("ysm", A0 + 49152, [P, D_MODEL])
        gfin = at("gfin", A0 + 57344, [P, D_MODEL])
        yb = at("yb", A0 + 65536, [P, 2, SEQ + N_SAMPLE])
        junk2 = at("junk2", A0 + 69696, [P, D_MODEL])
        oh = at("oh", A0 + 77888, [P, N_HEADS * V_HEAD])
        zas = at("zas", A0 + 81984, [P, N_HEADS, N_SAMPLE])
        oz = at("oz", A0 + 82240, [P, N_HEADS, N_SAMPLE])
        toep = at("toep", KD * ROW, [P, CHUNK, D_SSM])

        def psum(name):
            return es.enter_context(nc.psum_tensor(name, [P, 512], F32))

        gemm = [psum(f"gemm{i}") for i in range(4)]
        misc = [psum(f"misc{i}") for i in range(4)]

        x_loaded = [sem(f"x_loaded{t}") for t in range(5)]
        g_loaded = sem("g_loaded")
        prep_loaded = sem("prep_loaded")
        cnat_loaded = sem("cnat_loaded")
        filled = sem("filled")
        const_ready = sem("const_ready")
        x_squared = sem("x_squared")
        var_ready = sem("var_ready")
        std_ready = sem("std_ready")
        rstd_ready = sem("rstd_ready")
        x_scaled = sem("x_scaled")
        xt_ready = sem("xt_ready")
        xh_done = sem("xh_done")
        xl_done = sem("xl_done")
        w_loaded = [sem("w_loaded0"), sem("w_loaded1")]
        w_hi_ready = sem("w_hi_ready")
        w_lo_ready = sem("w_lo_ready")
        gemm_done = sem("gemm_done")
        gemm_read = sem("gemm_read")
        ev_stored = [sem("ev_stored0"), sem("ev_stored1")]
        ldt_spread = sem("ldt_spread")
        prep_t_ready = sem("prep_t_ready")
        prep_t_read = sem("prep_t_read")
        dve_step = sem("dve_step")
        dt_ready = sem("dt_ready")
        mag_ready = sem("mag_ready")
        angle_ready = sem("angle_ready")
        sin_ready = sem("sin_ready")
        coef_ready = sem("coef_ready")
        xgrp_loaded = sem("xgrp_loaded")
        wst_built = sem("wst_built")
        mul_done = sem("mul_done")
        bt_ready = sem("bt_ready")
        k_ready = sem("k_ready")
        bt_re_copied = sem("bt_re_copied")
        bt_im_copied = sem("bt_im_copied")
        k_copied = sem("k_copied")
        s_ready = sem("s_ready")
        s_re_copied = sem("s_re_copied")
        s_im_copied = sem("s_im_copied")
        scan_step = sem("scan_step")
        sample_step = sem("sample_step")
        toep_zeroed = sem("toep_zeroed")
        toep_loaded = sem("toep_loaded")
        ca_built = sem("ca_built")
        ca_built_pool = sem("ca_built_pool")
        pool_step = sem("pool_step")
        y_ready = sem("y_ready")
        y_copied = sem("y_copied")
        yt_ready = sem("yt_ready")
        yt_added = sem("yt_added")
        ug_loaded = [sem("ug_loaded0"), sem("ug_loaded1")]
        gelu_done = sem("gelu_done")
        ys_hi_done = sem("ys_hi_done")
        ys_lo_done = sem("ys_lo_done")
        state_t_ready = sem("state_t_ready")
        state_copied = sem("state_copied")
        state_stored = sem("state_stored")
        gate_loaded = [sem("gate_loaded0"), sem("gate_loaded1")]
        sig_done = sem("sig_done")
        gated = sem("gated")
        lat_loaded = sem("lat_loaded")
        rope_loaded = sem("rope_loaded")
        sums_ready = sem("sums_ready")
        squared = sem("squared")
        c_scaled = sem("c_scaled")
        normed = sem("normed")
        n_hi_done = sem("n_hi_done")
        n_lo_done = sem("n_lo_done")
        c_t_ready = sem("c_t_ready")
        c_t_copied = sem("c_t_copied")
        c_stored = [sem("c_stored0"), sem("c_stored1")]
        rotated = sem("rotated")
        rope_step = sem("rope_step")
        rope_done = sem("rope_done")
        kpe_copied = sem("kpe_copied")
        kpe_stored = sem("kpe_stored")
        v_ready = sem("v_ready")
        v_copied = sem("v_copied")
        v_stored = [sem("v_stored0"), sem("v_stored1")]
        kp_loaded = sem("kp_loaded")
        kp_hi_done = sem("kp_hi_done")
        kp_lo_done = sem("kp_lo_done")
        v_loaded = [sem("v_loaded0"), sem("v_loaded1")]
        head_loaded = [sem("head_loaded0"), sem("head_loaded1")]
        head_hi_done = sem("head_hi_done")
        head_lo_done = sem("head_lo_done")
        scores_ready = sem("scores_ready")
        max_ready = sem("max_ready")
        max_step = sem("max_step")
        sum_step = sem("sum_step")
        exp_done = sem("exp_done")
        prob_ready = sem("prob_ready")
        pt_ready = sem("pt_ready")
        pt_hi_done = sem("pt_hi_done")
        pt_lo_done = sem("pt_lo_done")
        pv_done = sem("pv_done")
        o_gated = sem("o_gated")
        cnt_saved = sem("cnt_saved")
        table_loaded = sem("table_loaded")
        page_loaded = [[sem(f"page_loaded{u}{g}") for g in range(4)] for u in range(2)]
        sample_loaded = sem("sample_loaded")
        wuk_t_ready = sem("wuk_t_ready")
        wuk_t_copied = sem("wuk_t_copied")
        qa_ready = sem("qa_ready")
        new_hi_done = sem("new_hi_done")
        new_lo_done = sem("new_lo_done")
        q_hi_done = sem("q_hi_done")
        q_lo_done = sem("q_lo_done")
        t_ready = sem("t_ready")
        t_hi_done = sem("t_hi_done")
        t_lo_done = sem("t_lo_done")
        p_hi_done = sem("p_hi_done")
        p_lo_done = sem("p_lo_done")
        pv_pair_done = sem("pv_pair_done")
        sc_ready = sem("sc_ready")
        half_copied = sem("half_copied")
        sc_added = sem("sc_added")
        sc_step = sem("sc_step")
        smax_ready = sem("smax_ready")
        sexp_done = sem("sexp_done")
        spt_ready = sem("spt_ready")
        spt_hi_done = sem("spt_hi_done")
        spt_lo_done = sem("spt_lo_done")
        opv_done = sem("opv_done")
        ohalf_copied = sem("ohalf_copied")
        olat_step = sem("olat_step")
        ot_ready = sem("ot_ready")
        ot_copied = sem("ot_copied")
        wuv_loaded = sem("wuv_loaded")
        os_step = sem("os_step")
        oh_copied = sem("oh_copied")
        res_loaded = sem("res_loaded")
        out_t_ready = sem("out_t_ready")
        out_added = sem("out_added")
        y_stored = sem("y_stored")
        comb_hi_done = sem("comb_hi_done")
        comb_lo_done = sem("comb_lo_done")

        lat_d, u_d, z_d = d["lat_d"], d["u_d"], d["z_d"]
        w_in = d["w_in"].rearrange("l (k p) n -> p (l k) n", p=P)
        w_glu = d["w_glu"].rearrange("l (k p) n -> p (l k) n", p=P)
        w_uq = d["w_uq"].rearrange("l (k p) n -> p (l k) n", p=P)
        w_uk = d["w_uk"].rearrange("l (k p) h n -> p (l k) (h n)", p=P)
        w_uv = d["w_uv"].rearrange("l (k p) h n -> p (l k) (h n)", p=P)
        q_d, qp_d, k_d, v_d = d["q_d"], d["qp_d"], d["k_d"], d["v_d"]
        x_prompt = d["x_prompt"].rearrange("b s m -> (b s) m")
        x_sample = d["x_sample"].rearrange("b s m -> (b s) m")

        def blocks(eng, first, count, body, between=None):
            alike = block_width(first + count) == block_width(first) and first + count not in (B_QR, B_OUT, B_END)
            looped = (count if alike else count - 2) // 2
            with eng.Fori(0, looped) as i:
                for n in (first, first + 1):
                    body(i * 2 + n, i + n // 2, n % 2, first)
            if between is not None:
                between()
            for n in range(first + 2 * looped, first + count):
                body(n, n // 2, n % 2, n + 2 if n + 2 < B_OUT or B_OUT <= n < B_END - 2 else None)

        def with_first_pass(eng, body, first_pass):
            for n in (B_ZS, B_ZS + 1):
                body(n, n // 2, n % 2, B_ZS)
            with eng.Fori(0, 3) as i:
                for u in range(2):
                    n = B_ZS + 2 + u
                    first_pass(i * 2 + u)
                    body(i * 2 + n, i + n // 2, n % 2, B_ZS)
            for b in (6, 7):
                first_pass(b)

        bias_glu = vecs[:, 10:18]
        EV_STORES = (18 + 4 + 4, 17 + 4 + 4)
        SQ_STEPS = 5 + 3
        NORM_OUT = (d["o_ckv_p"].rearrange("l b t r -> (l b t) r"), d["o_ckv_s"].rearrange("l b t r -> (l b t) r"))
        KPE_OUT = (d["o_kpe_p"].rearrange("l b t r -> (l b t) r"), d["o_kpe_s"].rearrange("l b t r -> (l b t) r"))

        def gate_count(n, r, slot):
            return (r - (B_GLU + 1 - slot) // 2 + 1) * 16 if slot == 0 else (r - B_GLU // 2 + 1) * 16

        SBANK = [(gemm[0], gemm[1], gemm[2], misc[1])[k] for k in (0, 1, 2, 0, 1, 2, 0, 1, 2, 3)]
        EXTRA = slice(272, 288)

        def head_pairs(eng, body):
            with eng.Fori(0, N_HEADS // 2 - 1) as i:
                for u in range(2):
                    body(i, u, False)
            for u in range(2):
                body(N_HEADS // 2 - 1, u, True)

        def samples(eng, step):
            step(0, 0, 0)
            step(1, 1, 0)
            with eng.Fori(0, N_SAMPLE // 2 - 2) as i:
                for u in range(2):
                    step(i * 2 + (2 + u), u, i + 1)
            for s in range(N_SAMPLE - 2, N_SAMPLE + 1):
                step(s, s % 2, s // 2)

        block = es.enter_context(nc.Block())

        @block.sync
        def _(sp):
            for t, (t0, rows) in enumerate(TILES):
                if t == 0:
                    sp.dma_start(xtok[0:N_META, 0, :], d["meta_tokens"]).then_inc(x_loaded[0], 16)
                    sp.dma_start(xtok[N_META:P, 0, :], x_prompt[0:P - N_META, :]).then_inc(x_loaded[0], 16)
                elif t < 4:
                    sp.dma_start(xtok[:, t, :], x_prompt[t0 - N_META:t0 - N_META + P, :]).then_inc(x_loaded[t], 16)
                else:
                    sp.dma_start(xtok[0:N_META, t, :], x_prompt[t0 - N_META:SEQ, :]).then_inc(x_loaded[t], 16)
                    sp.dma_start(xtok[N_META:rows, t, :], x_sample).then_inc(x_loaded[t], 16)

            def load(n, slot, col):
                sp.dma_start(w_raw[:, slot, :].rearrange("p (k n) -> p k n", k=KD),
                             w_in[:, :, ds(col, P)]).then_inc(w_loaded[slot], 16)

            for n in range(2):
                load(n, n, COL_LAT + n * P)

            def run(first, count, col):
                with sp.Fori(0, count // 2) as i:
                    for u in range(2):
                        sp.wait_ge(w_lo_ready, i * 2 + (first + u - 1))
                        load(None, (first + u) % 2, i * (2 * P) + (col + u * P))
                if count % 2:
                    n = first + count - 1
                    sp.wait_ge(w_lo_ready, n - 1)
                    load(n, n % 2, col + (count - 1) * P)

            run(2, B_U - 2, COL_LAT + 2 * P)
            run(B_U, 8, 0)
            run(B_ZS, 8, COL_ZS)
            run(B_ZA, 8, COL_ZA)

            def load_glu(n, slot, col):
                sp.dma_start(w_raw[:, slot, 0:D_SSM].rearrange("p (k n) -> p k n", k=8),
                             w_glu[:, :, ds(col, P)]).then_inc(w_loaded[slot], 16)

            for n in (B_GLU, B_GLU + 1):
                sp.wait_ge(w_lo_ready, n - 1)
                load_glu(n, n % 2, (n - B_GLU) * P)
            sp.wait_ge(toep_zeroed, 1)
            sp.wait_ge(coef_ready, 4)
            sp.wait_ge(k_copied, 9)
            for i in range(CHUNK):
                sp.dma_start(toep[(CHUNK - 1 - i) * GROUP:P, i, :], kall[0:(i + 1) * GROUP, :]).then_inc(toep_loaded, 16)
            for b in range(8):
                if b >= 2:
                    sp.wait_ge(yt_added, 2 * (b - 1))
                sp.dma_start(ug[:, b % 2, :], u_d[b * P:(b + 1) * P, :]).then_inc(ug_loaded[b % 2], 16)
            sp.wait_ge(y_ready, 16)

            def load_gate(n, slot):
                sp.dma_start(gate[:, slot, :], z_d[ds((n - B_GLU) * P, P), :]).then_inc(gate_loaded[slot], 16)
            load_gate(B_GLU, B_GLU % 2)
            load_gate(B_GLU + 1, (B_GLU + 1) % 2)

            def next_glu(k, ku):
                sp.wait_ge(w_lo_ready, k + (B_GLU + 2))
                load_glu(None, (B_GLU + 3 + ku) % 2, k * P + 3 * P)

            def next_gate(k, ku):
                sp.wait_ge(comb_lo_done, k + 3)
                load_gate(k + (B_GLU + 2), (B_GLU + ku) % 2)

            next_glu(-1, -1)
            with sp.Fori(0, 2) as i:
                for u in range(2):
                    next_glu(i * 2 + u, u)
                    next_gate(i * 2 + u, u)
            next_glu(4, 4)
            next_gate(4, 4)
            next_gate(5, 5)
            sp.wait_ge(state_copied, 6)
            for c, o_d in enumerate((d["o_ssm_re_s"], d["o_ssm_im_s"])):
                rows = o_d.rearrange("l b (q t) n -> (l b q) (t n)", t=2)
                for h in range(2):
                    sp.dma_start(rows[h * P:(h + 1) * P, :], sout[:, 2 * h + c, :]).then_inc(state_stored, 16)
            for c, o_d in enumerate((d["o_ssm_re_p"], d["o_ssm_im_p"])):
                sp.dma_start(o_d.rearrange("l b (q t) n -> (l b q) (t n)", t=2), sout[0:PAIRS, 4 + c, :]).then_inc(state_stored, 16)

            def load_w(n, slot, src, width):
                sp.dma_start(w_raw[:, slot, 0:width].rearrange("p (k n) -> p k n", k=src.shape[1]), src).then_inc(w_loaded[slot], 16)

            HD = QK_NOPE + QK_ROPE
            with sp.Fori(0, 4) as i:
                for u in range(2):
                    sp.wait_ge(w_lo_ready, i * 2 + (B_QN + u - 1))
                    load_w(None, (B_QN + u) % 2, w_uq[:, :, ds(i * (2 * HD) + u * HD, P)], Q_LORA)
            with sp.Fori(0, 2) as i:
                for u in range(2):
                    sp.wait_ge(w_lo_ready, i * 2 + (B_QR + u - 1))
                    slot = (B_QR + u) % 2
                    dst = w_raw[:, slot, 0:Q_LORA].rearrange("p (k n) -> p k n", k=Q_LORA // P)
                    for t in range(2):
                        c0 = i * (4 * HD) + ((2 * u + t) * HD + QK_NOPE)
                        sp.dma_start(dst[:, :, t * QK_ROPE:(t + 1) * QK_ROPE], w_uq[:, :, ds(c0, QK_ROPE)]).then_inc(w_loaded[slot], 16)
            with sp.Fori(0, 4) as i:
                for u in range(2):
                    sp.wait_ge(w_lo_ready, i * 2 + (B_K + u - 1))
                    load_w(None, (B_K + u) % 2, w_uk[:, :, ds(i * (2 * P) + u * P, P)], KV_LORA)
            for u in range(2):
                sp.wait_ge(w_lo_ready, B_V + u - 1)
                load_w(None, (B_V + u) % 2, w_uv[:, :, u * 512:(u + 1) * 512], 2048)
            sp.wait_ge(state_stored, 16 * 6)
            def load_qk(h, slot):
                sp.dma_start(hraw[:, slot, 0, :], q_d[ds(h * P, P), :]).then_inc(head_loaded[slot], 16)
                sp.dma_start(hraw[:, slot, 1, :], k_d[ds(h * P, P), :]).then_inc(head_loaded[slot], 16)

            def load_qp(h, slot):
                sp.dma_start(hraw[0:QK_ROPE, slot, 2, :], qp_d[ds(h * QK_ROPE, QK_ROPE), :]).then_inc(head_loaded[slot], 16)

            def load_v(h, slot):
                sp.dma_start(vraw[:, slot, 0:4, :], v_d[0:SEQ, ds(h * V_HEAD, V_HEAD)].rearrange("(t p) c -> p t c", p=P)
                             ).then_inc(v_loaded[slot], 16)
                sp.dma_start(vraw[0:N_META, slot, 4, :], v_d[SEQ:T_PROMPT, ds(h * V_HEAD, V_HEAD)]).then_inc(v_loaded[slot], 16)

            def load_za(h, slot):
                sp.dma_start(za[:, slot, :], z_d[ds(h * P + D_SSM, P), :]).then_inc(ug_loaded[slot], 16)

            sp.wait_ge(gemm_done, B_V)
            for u in range(2):
                sp.wait_ge(ev_stored[u], 16 * (1 + EV_STORES[u]))
            for u in range(2):
                load_qk(u, u)
            sp.wait_ge(v_ready, 10)
            for u in range(2):
                sp.wait_ge(ev_stored[u], 16 * (1 + EV_STORES[u] + 3 - u))
            sp.dma_start(kp_raw[0:QK_ROPE, :], qp_d[4 * P:4 * P + QK_ROPE, :]).then_inc(kp_loaded, 16)
            for u in range(2):
                load_qp(u, u)
            for u in range(2):
                sp.wait_ge(v_stored[u], 16 * 5)
            sp.wait_ge(kpe_stored, 16 * 3)
            for u in range(2):
                load_v(u, u)
                load_za(u, u)
            for u in range(2):
                sp.wait_ge(c_stored[u], 16 * (4 - 2 * u))
            sp.wait_ge(rotated, 5)
            sp.dma_start(ptab[:], d["page_table"].rearrange("b j -> (b j)").unsqueeze(0)).then_inc(table_loaded, 16)
            sp.dma_start(wuk[:], w_uk).then_inc(sample_loaded, 16)
            sp.dma_start(qs[:], q_d.rearrange("(h e) t -> e h t", e=QK_NOPE)[:, :, T_PROMPT:T]).then_inc(sample_loaded, 16)
            for half in range(2):
                sp.dma_start(qps[half * QK_ROPE:(half + 1) * QK_ROPE],
                             qp_d[0:4 * P, :].rearrange("(h e) t -> e h t", e=QK_ROPE)[:, :, T_PROMPT:T]).then_inc(sample_loaded, 16)
            sp.dma_start(kpn_raw[0:QK_ROPE], qp_d[4 * P:4 * P + QK_ROPE, T_PROMPT:T]).then_inc(sample_loaded, 16)
            sp.dma_start(half2[0:N_SAMPLE], NORM_OUT[1]).then_inc(sample_loaded, 16)
            with sp.Fori(0, N_HEADS // 2 - 1) as i:
                for u in range(2):
                    sp.wait_ge(head_lo_done, i * 4 + (2 * u + 2))
                    load_qk(i * 2 + (u + 2), u)
                    load_qp(i * 2 + (u + 2), u)
                    load_v(i * 2 + (u + 2), u)
                    sp.wait_ge(o_gated, i * 2 + (u + 2))
                    load_za(i * 2 + (u + 2), u)
            sp.wait_ge(table_loaded, 16)
            sp.wait_ge(comb_lo_done, 18)

            def load_pages(s, u, g):
                pages = [sp.value_load(ptab[0:1, ds(s * N_PAGES + (4 * g + j), 1)], min_val=0, max_val=d["cache_ckv"].shape[1] - 1)
                         for j in range(4)]
                if not isinstance(s, int):
                    sp.wait_ge(p_lo_done, s * 8 + (2 * g + 2 - 16))
                for j, page in enumerate(pages):
                    k = u * N_PAGES + 4 * g + j
                    sp.dma_start(ckv[:, k, :], d["cache_ckv"][0, ds(page, 1)].rearrange("a k r -> (a k) r")).then_inc(page_loaded[u][g], 16)
                    sp.dma_start(kpe[:, k, :], d["cache_kpe"][0, ds(page, 1)].rearrange("a k r -> (a k) r")).then_inc(page_loaded[u][g], 16)

            for b in range(2):
                for g in range(4):
                    load_pages(b, b, g)
            with sp.Fori(0, N_SAMPLE // 2 - 1) as i:
                for u in range(2):
                    for g in range(4):
                        load_pages(i * 2 + (2 + u), u, g)
            sp.wait_ge(p_lo_done, 8 * 7)
            sp.dma_start(wuv[:], w_uv).then_inc(wuv_loaded, 16)

            w_out = d["w_out"].rearrange("l (k p) n -> p (l k) n", p=P)

            def load_out(j, slot):
                sp.dma_start(w_raw[:, slot, :].rearrange("p (k n) -> p k n", k=KD),
                             w_out[:, :, ds(j * P, P)]).then_inc(w_loaded[slot], 16)

            sp.wait_ge(sc_ready, 5 * 8)
            for j in range(2):
                load_out(j, j)
            sp.wait_ge(p_lo_done, 8 * 8)
            sp.wait_ge(ot_copied, 9)
            sp.dma_start(zas[:], z_d[D_SSM:2 * D_SSM, :].rearrange("(h e) t -> e h t", e=P)[:, :, T_PROMPT:T]).then_inc(res_loaded, 16)
            for t in range(4):
                sp.dma_start(yt[:, t, :], x_prompt[t * P:(t + 1) * P, :]).then_inc(res_loaded, 16)
            sp.dma_start(ysm[0:N_SAMPLE, :], x_sample).then_inc(res_loaded, 16)
            sp.dma_start(gfin[:], d["g_final"].partition_broadcast(P)).then_inc(res_loaded, 16)
            with sp.Fori(0, 7) as i:
                for u in range(2):
                    sp.wait_ge(w_lo_ready, i * 2 + (B_OUT + 1 + u))
                    load_out(i * 2 + (2 + u), u)
            for t in range(4):
                sp.wait_ge(x_scaled, t + 6)
                sp.dma_start(d["o_y_p"].rearrange("b s m -> (b s) m")[t * P:(t + 1) * P, :], yt[:, t, :]).then_inc(y_stored, 16)
            sp.wait_ge(x_scaled, 10)
            sp.dma_start(d["o_y_s"].rearrange("b s m -> (b s) m"), ysm[0:N_SAMPLE, :]).then_inc(y_stored, 16)
            sp.wait_ge(y_stored, 16 * 5)

        @block.gpsimd
        def _(pool):
            pool.memset(ident[:], 0.0).then_inc(filled, 1)
            pool.memset(rot[:], 0.0).then_inc(filled, 1)
            pool.memset(causal[:], 0.0).then_inc(filled, 1)
            pool.memset(ones[:], 1.0).then_inc(const_ready, 1)
            pool.wait_ge(filled, 3)
            pool.affine_select(out=ident[:], in_=ident[:], compare_op=ALU.not_equal, fill=1.0, base=0,
                               pattern=[[-1, P]], channel_multiplier=1).then_inc(const_ready, 1)
            pool.affine_select(out=causal[:], in_=causal[:], compare_op=ALU.is_ge, fill=NEG, base=0,
                               pattern=[[-1, P]], channel_multiplier=1).then_inc(const_ready, 1)
            rv = rot[:].rearrange("p (a h i) -> p a h i", a=2, h=2)
            for h, off in ((0, -32), (1, 0)):
                v = rv[:, :, h, :]
                pool.affine_select(out=v, in_=v, compare_op=ALU.not_equal, fill=1.0, base=off,
                                   pattern=[[-64, 2], [-1, 32]], channel_multiplier=1).then_inc(const_ready, 1)

            def build_out(b):
                if b >= 2:
                    pool.wait_ge(y_ready, 2 * b - 2)
                for q in (2, 3):
                    g = 4 * b + q
                    n = 2 * b + q - 2
                    for c in range(2):
                        t2 = [ptmp[:, 2 * c + i].rearrange("p (t l c) -> p t l c", t=2, l=CHUNK) for i in range(2)]
                        for i in range(2):
                            pw = powers[:, (c + i) % 2, 1:9, g].unsqueeze(1).to_broadcast([P, 2, CHUNK])
                            pw = pw.unsqueeze(3).to_broadcast([P, 2, CHUNK, GROUP])
                            cc = cbd[:, i, g].unsqueeze(2).to_broadcast([P, 2, CHUNK, GROUP])
                            last = pool.tensor_tensor(t2[i], pw, cc, ALU.mult)
                        last.then_inc(pool_step, 1)
                    for c in range(2):
                        t2 = [ptmp[:, 2 * c + i].rearrange("p (t l c) -> p t l c", t=2, l=CHUNK) for i in range(2)]
                        pool.wait_ge(pool_step, 2 * n + 1 + c)
                        if c == 0:
                            last = pool.tensor_tensor(cast[:, b % 2, c, q], t2[0], t2[1], ALU.add)
                        else:
                            last = pool.tensor_tensor(cast[:, b % 2, c, q], t2[1], t2[0], ALU.subtract)
                    last.then_inc(ca_built_pool, 1)
                    pool.wait_ge(ca_built_pool, n + 1)

            pool.wait_ge(gemm_done, B_GLU)
            pool.memset(toep[:, 0:4], 0.0).then_inc(toep_zeroed, 1)
            pool.wait_ge(ev_stored[0], 16 * 19)
            pool.wait_ge(ev_stored[1], 16 * 18)
            build_out(0)
            pool.wait_ge(toep_loaded, 16 * CHUNK)
            for b in range(1, 8):
                build_out(b)
            pool.wait_ge(state_t_ready, 2)
            pool.dma_start(latq[:], lat_d[0:Q_LORA, :].rearrange("(k p) t -> p k t", p=P)).then_inc(lat_loaded, 16)
            pool.dma_start(latc[:], lat_d[Q_LORA:Q_LORA + KV_LORA, :].rearrange("(k p) t -> p k t", p=P)).then_inc(lat_loaded, 16)
            pool.dma_start(cos[:], d["rope_cos"]).then_inc(rope_loaded, 16)
            pool.dma_start(sin[:], d["rope_sin"]).then_inc(rope_loaded, 16)
            for k in range(1, 10):
                if k == 6:
                    continue
                pool.wait_ge(squared, k + 1)
                i = k // 6
                pool.tensor_tensor(sq[:, i], sq[:, i], rs[:, k % 2], ALU.add).then_inc(pool_step, 1)
                pool.wait_ge(pool_step, 32 + k - i)
            for k in range(10):
                if k in (0, 6):
                    pool.wait_ge(rstd_ready, 6 + k // 6)
                buf = latq[:, k] if k < 6 else latc[:, k - 6]
                pool.tensor_tensor(buf, buf, rs[:, k // 6], ALU.mult).then_inc(normed, 1)
            pool.wait_ge(n_lo_done, 6)
            for h in range(2):
                pool.dma_start(rp[h * QK_ROPE:(h + 1) * QK_ROPE, 4, :],
                               lat_d[Q_LORA + KV_LORA:Q_LORA + KV_LORA + QK_ROPE, :]).then_inc(rope_loaded, 16)

            pool.wait_ge(c_t_ready, 6)
            for u in range(2):
                pool.wait_ge(c_stored[u], 16 * (4 - 2 * u))
            for z in (pt_hi, pt_lo):
                pool.memset(z[:, 1, 0:P].bitcast(F32), 0.0).then_inc(filled, 1)
                pool.memset(z[:, 3, 2 * P:3 * P].bitcast(F32), 0.0).then_inc(filled, 1)

            def head_lo(h, u):
                pool.wait_ge(head_hi_done, h * 2 + 1)
                pool.tensor_tensor(hl[:, u, 0:2], hraw[:, u, 0:2], hh[:, u, 0:2].bitcast(F32), ALU.subtract)
                pool.tensor_tensor(hl[0:QK_ROPE, u, 2], hraw[0:QK_ROPE, u, 2], hh[0:QK_ROPE, u, 2].bitcast(F32), ALU.subtract).then_inc(head_lo_done, 1)
                pool.wait_ge(head_hi_done, h * 2 + 2)
                pool.tensor_tensor(vl[0:N_META, u, 4], vraw[0:N_META, u, 4], vh[0:N_META, u, 4].bitcast(F32), ALU.subtract)
                pool.tensor_tensor(vl[:, u, 0:4], vraw[:, u, 0:4], vh[:, u, 0:4].bitcast(F32), ALU.subtract).then_inc(head_lo_done, 1)

            with pool.Fori(0, N_HEADS // 2) as i:
                for u in range(2):
                    head_lo(i * 2 + u, u)

            pool.memset(not_own[:], NEG).then_inc(filled, 1)
            pool.wait_ge(filled, 8)
            pool.affine_select(out=not_own[:], in_=not_own[:], compare_op=ALU.not_equal, fill=0.0, base=0,
                               pattern=[[1, N_SAMPLE], [-1, N_SAMPLE]], channel_multiplier=0).then_inc(filled, 1)
            pool.memset(q_st[:].bitcast(F32), 0.0).then_inc(filled, 1)
            pool.memset(p_t[:].bitcast(F32), 0.0).then_inc(filled, 1)
            pool.memset(qa[:, 4:6], 0.0).then_inc(filled, 1)

            def page_lo(b, u, hg):
                pool.wait_ge(p_hi_done, b * 8 + (hg + 1))
                k = u * N_PAGES + 2 * hg
                pool.tensor_tensor(cp_lo[:, hg % 2], ckv[:, k:k + 2], cp_hi[:, hg % 2].bitcast(F32), ALU.subtract).then_inc(p_lo_done, 1)

            with pool.Fori(0, N_SAMPLE // 2) as i:
                for u in range(2):
                    for hg in range(8):
                        page_lo(i * 2 + u, u, hg)

        @block.scalar
        def _(act):
            act.dma_start(gbc[:], d["g_norm"].partition_broadcast(P).rearrange("p l m -> p (l m)")).then_inc(g_loaded, 16)
            act.dma_start(anat[0:PAIRS, 0, :], d["ssm_a_re"].rearrange("l (q t) n -> (l q) (t n)", t=2)).then_inc(prep_loaded, 16)
            act.dma_start(anat[0:PAIRS, 1, :], d["ssm_a_im"].rearrange("l (q t) n -> (l q) (t n)", t=2)).then_inc(prep_loaded, 16)
            act.dma_start(ldt[0:PAIRS, :], d["ssm_log_dt"].rearrange("l (q t) -> (l q) t", t=2)).then_inc(prep_loaded, 16)
            for c, s in enumerate((d["state_ssm_re"], d["state_ssm_im"])):
                rows = s.rearrange("l b (q t) n -> (l b q) (t n)", t=2)
                for h in range(2):
                    act.dma_start(snat[:, h, c, :], rows[h * P:(h + 1) * P, :]).then_inc(prep_loaded, 16)
            for c, b in enumerate((d["ssm_b_re"], d["ssm_b_im"])):
                act.dma_start(bbar[:, c], b.rearrange("l (q t) n c -> (l t n) q c", t=2)).then_inc(prep_loaded, 16)
            row = 0
            for v in (d["g_q_norm"], d["g_kv_norm"], d["b_glu"], d["ssm_d"]):
                v = v.rearrange("l (k p) -> (l k) p", p=P)
                act.dma_start(vnat[row:row + v.shape[0], :], v).then_inc(prep_loaded, 16)
                row += v.shape[0]
            for c, cc in enumerate((d["ssm_c_re"], d["ssm_c_im"])):
                v = cc.rearrange("l (b q t) c n -> t (l b) q c n", b=4, t=2)
                for b in range(4):
                    for t in range(2):
                        act.dma_start(cnat[:, b, c, t * N_STATE:(t + 1) * N_STATE],
                                      v[t, b]).then_inc(cnat_loaded, 16)

            def square(t):
                t0, rows = TILES[t]
                act.wait_ge(x_loaded[t], 32 if t in (0, 4) else 16)
                act.activation(junk[0:rows], xtok[0:rows, t], ACT.Square,
                               accum_out=stat[0:rows, t:t + 1]).then_inc(x_squared, 1)
                act.wait_ge(var_ready, t + 1)
                act.activation(stat[0:rows, 16 + t:17 + t], stat[0:rows, 8 + t:9 + t],
                               ACT.Sqrt).then_inc(std_ready, 1)

            def split_hi(n, r, slot, ahead):
                if ahead is not None:
                    width = block_width(ahead)
                    more = 0 if ahead < B_QR else r + 2 - (B_QR + 1 - slot) // 2 if ahead < B_K else 2
                    act.wait_ge(w_loaded[slot], (r + 2 + more) * 16)
                    act.wait_ge(gemm_done, n + 1)
                    act.activation(w_hi[:, slot, 0:width], w_raw[:, slot, 0:width], ACT.Copy).then_inc(w_hi_ready, 1)

            square(0)
            square(1)
            for g in range(20):
                t, q = divmod(g, 4)
                t0, rows = TILES[t]
                act.wait_ge(xt_ready, g + 1)
                act.activation(xh[:, 4 * q:4 * q + 4, t0:t0 + rows],
                               misc[g % 4][:].rearrange("p (k t) -> p k t", k=4)[:, :, 0:rows],
                               ACT.Copy).then_inc(xh_done, 1)
                if q == 3 and t < 3:
                    square(t + 2)
                if q == 3 and t in (2, 3):
                    act.wait_ge(w_loaded[t - 2], 16)
                    act.activation(w_hi[:, t - 2, :], w_raw[:, t - 2, :], ACT.Copy).then_inc(w_hi_ready, 1)

            act.wait_ge(prep_t_read, 1)
            act.activation(coef[:, 3], coef[:, 2], ACT.Exp).then_inc(dt_ready, 1)
            act.wait_ge(dve_step, 1)
            act.activation(coef[:, 5], coef[:, 4], ACT.Exp).then_inc(mag_ready, 1)
            act.wait_ge(angle_ready, 1)
            act.activation(coef[:, 10:12], coef[:, 8:10], ACT.Sin).then_inc(sin_ready, 1)

            def store(dst):
                def body(n, r, slot, ahead):
                    split_hi(n, r, slot, ahead)
                    act.wait_ge(gemm_read, n + 3)
                    act.dma_start(dst(n), ev[:, slot, :]).then_inc(ev_stored[slot], 16)
                return body

            blocks(act, B_LAT, 11, store(lambda n: lat_d[ds(n * P, P), :]))
            blocks(act, B_U, 8, store(lambda n: u_d[ds((n - B_U) * P, P), :]))

            act.wait_ge(coef_ready, 3)
            act.wait_ge(ev_stored[0], 16 + 16 * (B_ZS // 2 + B_ZS % 2))
            act.wait_ge(ev_stored[1], 16 + 16 * (B_ZS // 2))
            for lag in range(CHUNK):
                j = CHUNK - 1 - lag
                rows = xgrp[lag * GROUP:(lag + 1) * GROUP]
                act.dma_start(rows[:, :, N_SAMPLE:YCOLS],
                              u_d.rearrange("(g c) t -> c g t", c=GROUP)[:, :, j * N_CHUNK:(j + 1) * N_CHUNK]
                              ).then_inc(xgrp_loaded, 16)
            for lag, col in ((0, YCOLS), (CHUNK - 1, 0)):
                act.dma_start(xgrp[lag * GROUP:(lag + 1) * GROUP, :, col:col + N_SAMPLE],
                              u_d.rearrange("(g c) t -> c g t", c=GROUP)[:, :, T_PROMPT:T]).then_inc(xgrp_loaded, 16)

            def first_pass(b):
                act.wait_ge(bt_ready, b + 1)
                act.activation(bst[:, 0], misc[0][:].rearrange("p (q m) -> p q m", q=4), ACT.Copy).then_inc(bt_re_copied, 1)
                act.wait_ge(k_ready, b + 1)
                act.activation(kall[:, ds(b * P, P)], misc[2][:, 0:P], ACT.Copy).then_inc(k_copied, 1)
                act.wait_ge(s_ready, b + 1)
                act.activation(states[:, N_SAMPLE + 1:ENTRIES, 0, ds(b * 4, 4)],
                               misc[3][:, 0:4 * YCOLS].rearrange("p (q e) -> p e q", q=4), ACT.Copy).then_inc(s_re_copied, 1)

            def silu_store(first):
                def body(n, r, slot, ahead):
                    split_hi(n, r, slot, ahead)
                    act.wait_ge(gemm_done, n + 1)
                    act.wait_ge(ev_stored[slot], (r + 1) * 16)
                    for h, (h0, hw) in enumerate(HALVES):
                        last = act.activation(ev[:, slot, h0:h0 + hw], gemm[2 * slot + h][:, 0:hw], ACT.Silu)
                    last.then_inc(gemm_read, 1)
                    act.wait_ge(gemm_read, n + 3)
                    act.dma_start(z_d[ds((n - B_ZS) * P, P), :], ev[:, slot, :]).then_inc(ev_stored[slot], 16)
                return body

            with_first_pass(act, silu_store(B_ZS), first_pass)
            blocks(act, B_ZA, 8, silu_store(B_ZA))

            act.wait_ge(gemm_done, B_GLU)
            def gelu(b):
                act.wait_ge(yt_added, 2 * b + 2)
                act.activation(ys[:, b], yg[:, b % 2], ACT.Gelu_apprx_tanh).then_inc(gelu_done, 1)

            for b in range(8):
                act.wait_ge(y_ready, 2 * b + 1)
                if b >= 2:
                    act.wait_ge(yt_ready, 2 * b - 2)
                act.activation(ychunk[0:YCOLS, b % 2, :, 0:64].rearrange("p i (g c) -> p g i c", c=GROUP),
                               misc[0][0:YCOLS, :].rearrange("p (g i c) -> p g i c", g=4, c=GROUP), ACT.Copy).then_inc(y_copied, 1)
                if b >= 1:
                    gelu(b - 1)
            gelu(7)

            act.wait_ge(state_t_ready, 2)
            act.wait_ge(gelu_done, 8)
            for k in range(8):
                act.activation(ys_hi[:, k], ys[:, k], ACT.Copy).then_inc(ys_hi_done, 1)

            def glu(n, r, slot, ahead):
                split_hi(n, r, slot, ahead)
                act.wait_ge(gemm_done, n + 1)
                act.wait_ge(comb_lo_done, n - (B_GLU - 1))
                for h, (h0, hw) in enumerate(HALVES):
                    last = act.activation(sig[:, slot, h0:h0 + hw], gemm[2 * slot + h][:, 0:hw], ACT.Sigmoid,
                                          bias=bias_glu[:, ds(n - B_GLU, 1)])
                last.then_inc(sig_done, 1)
                act.wait_ge(gated, n - (B_GLU - 1))
                act.activation(comb_hi[:, ds(n - B_GLU, 1), :].rearrange("p a t -> p (a t)"), gate[:, slot], ACT.Copy).then_inc(comb_hi_done, 1)

            act.wait_ge(lat_loaded, 32)
            for k in range(10):
                if k >= 3 and k != 6:
                    act.wait_ge(pool_step, 32 + (k - 2 if k < 8 else k - 3))
                src = latq[:, k] if k < 6 else latc[:, k - 6]
                act.activation(sq[:, k // 6] if k in (0, 6) else rs[:, k % 2], src, ACT.Square).then_inc(squared, 1)

            def roots():
                for i in range(2):
                    act.wait_ge(var_ready, i + 6)
                    act.activation(rs[:, i], rs[:, i], ACT.Sqrt).then_inc(std_ready, 1)

            blocks(act, B_GLU, 8, glu, roots)

            act.wait_ge(comb_lo_done, 10)
            for k in range(10):
                if k < 6:
                    act.wait_ge(normed, k + 1)
                    act.activation(qn_hi[:, k], latq[:, k], ACT.Copy, scale=vecs[:, k:k + 1]).then_inc(n_hi_done, 1)
                else:
                    act.wait_ge(c_scaled, k - 5)
                    act.activation(cn_hi[:, k - 6], latc[:, k - 6], ACT.Copy).then_inc(n_hi_done, 1)

            def store_q(dst, first, count0, stored, before):
                def body(n, r, slot, ahead):
                    split_hi(n, r, slot, ahead)
                    act.wait_ge(gemm_read, n + 3)
                    act.dma_start(dst[ds((n - first) * P, P), :], ev[:, slot, :]).then_inc(stored[slot], 16)
                return body

            blocks(act, B_QN, 8, store_q(q_d, B_QN, 0, ev_stored, 0))

            def store_c(t):
                act.wait_ge(c_t_copied, t + 1)
                t0, rows = TILES[t]
                if t < 4:
                    act.dma_start(NORM_OUT[0][t0:t0 + P, :], cout[:, t % 2, :]).then_inc(c_stored[t % 2], 16)
                else:
                    act.dma_start(NORM_OUT[0][t0:T_PROMPT, :], cout[0:N_META, 0, :]).then_inc(c_stored[0], 16)
                    act.dma_start(NORM_OUT[1], cout[N_META:rows, 0, :]).then_inc(c_stored[0], 16)

            blocks(act, B_QR, 4, split_hi)
            blocks(act, B_K, 8, store_q(k_d, B_K, 0, ev_stored, 0))
            for v in range(10):
                j, t = divmod(v, 5)
                t0, rows = TILES[t]
                act.wait_ge(v_copied, v + 1)
                act.dma_start(v_d[t0:t0 + rows, j * 512:(j + 1) * 512], vout[0:rows, v % 2, :]).then_inc(v_stored[v % 2], 16)
                if v < 5:
                    act.wait_ge(rope_done, v + 1)
                    act.dma_start(qp_d[v * P:(v + 1) * P, :], ev[:, v % 2, :]).then_inc(ev_stored[v % 2], 16)
                else:
                    act.wait_ge(c_t_ready, t + 1)
                    if t >= 2:
                        act.wait_ge(c_stored[t % 2], 16 * (t // 2))
                    act.activation(cout[0:rows, t % 2, :], misc[t % 2][0:rows, :], ACT.Copy).then_inc(c_t_copied, 1)
                    store_c(t)
            act.wait_ge(n_lo_done, 10)
            act.activation(cnt_hi[:], cn_hi[:, :, T_PROMPT:T].bitcast(F32), ACT.Copy)
            act.activation(cnt_lo[:], cn_lo[:, :, T_PROMPT:T].bitcast(F32), ACT.Copy).then_inc(cnt_saved, 1)
            act.wait_ge(cnt_saved, 1)
            act.wait_ge(kpe_copied, 1)
            kv = kout[:].rearrange("p t r -> p t r")
            act.dma_start(KPE_OUT[0][0:512, :].rearrange("(t p) r -> p t r", p=P), kv[:, 0:4, :]).then_inc(kpe_stored, 16)
            act.dma_start(KPE_OUT[0][512:T_PROMPT, :], kv[0:N_META, 4, :]).then_inc(kpe_stored, 16)
            act.dma_start(KPE_OUT[1], kv[N_META:N_META + N_SAMPLE, 4, :]).then_inc(kpe_stored, 16)

            NM, SM, RS = 0, 12, 24
            def head_hi(u, count):
                act.wait_ge(head_loaded[u], (count + 1) * 48)
                act.activation(hh[:, u, 0:2], hraw[:, u, 0:2], ACT.Copy)
                act.activation(hh[0:QK_ROPE, u, 2], hraw[0:QK_ROPE, u, 2], ACT.Copy).then_inc(head_hi_done, 1)

            def values_hi(u, count):
                act.wait_ge(v_loaded[u], (count + 1) * 32)
                act.activation(vh[:, u, 0:4], vraw[:, u, 0:4], ACT.Copy)
                act.activation(vh[0:N_META, u, 4], vraw[0:N_META, u, 4], ACT.Copy).then_inc(head_hi_done, 1)

            def exponential(n, m):
                i = m % 5
                rows = P if i < 4 else N_META
                width = P * min(i + 1, 4)
                act.wait_ge(max_ready, n + 1)
                if not isinstance(n, int) or n >= 2:
                    act.wait_ge(pt_ready, n)
                last = act.activation(prob[0:rows, m % 2, 0:width], SBANK[m][0:rows, 0:width], ACT.Exp, scale=SCALE,
                                      bias=stat[0:rows, NM + m:NM + m + 1], accum_out=stat[0:rows, SM + m:SM + m + 1])
                if i == 4:
                    last = act.activation(prob[0:rows, m % 2, width:T_PROMPT], misc[0][0:rows, EXTRA], ACT.Exp, scale=SCALE,
                                          bias=stat[0:rows, NM + m:NM + m + 1], accum_out=stat[0:rows, 40 + m // 5:41 + m // 5])
                last.then_inc(exp_done, 1)

            def pt_high(n, m):
                i = m % 5
                rows = P if i < 4 else N_META
                act.wait_ge(pt_ready, n + 2)
                q0 = i * P
                src = misc[2 + m % 2][:, 0:5 * rows if i == 4 else (i + 1) * P].rearrange("p (j q) -> p j q", q=rows)
                last = act.activation(pt_hi[:, 0:min(i + 1, 4), q0:q0 + rows], src[:, 0:min(i + 1, 4)], ACT.Copy)
                if i == 4:
                    last = act.activation(pt_hi[0:rows, 4, q0:q0 + rows], src[0:rows, 4], ACT.Copy)
                last.then_inc(pt_hi_done, 1)

            def comb_high(h, u):
                act.wait_ge(o_gated, h + 2)
                act.activation(comb_hi[:, ds(h + 8, 1), 0:T_PROMPT].rearrange("p a t -> p (a t)"), otmp[:, u, 0:T_PROMPT], ACT.Copy).then_inc(comb_hi_done, 1)

            act.wait_ge(kp_loaded, 16)
            act.activation(kp_hi[0:QK_ROPE], kp_raw[0:QK_ROPE], ACT.Copy).then_inc(kp_hi_done, 1)
            head_hi(0, 0)
            exponential(0, 0)
            values_hi(0, 0)
            head_hi(1, 0)
            values_hi(1, 0)

            def head_act(pair, u, last):
                for i in range(5):
                    m = 5 * u + i
                    n = pair * 10 + m
                    if not (last and m == 9):
                        exponential(pair * 10 + (m + 1), (m + 1) % 10)
                    if i == 0:
                        act.wait_ge(pv_done, pair * 2 + (u + 1))
                    pt_high(n, m)
                    if i == 3 and not last:
                        act.wait_ge(scores_ready, pair * 10 + (5 * u + 5))
                        head_hi(u, pair + 1)
                comb_high(pair * 2 + u, u)
                if not last:
                    values_hi(u, pair + 1)

            head_pairs(act, head_act)

            SUM, RSUM, PART, SMAX = 48, 50, 52, 58
            act.wait_ge(filled, 12)
            act.wait_ge(sample_loaded, 16 * 6)
            act.activation(kpn_hi[0:QK_ROPE], kpn_raw[0:QK_ROPE], ACT.Copy)
            act.activation(cnew_hi[0:N_SAMPLE], half2[0:N_SAMPLE], ACT.Copy).then_inc(new_hi_done, 1)
            for h in range(N_HEADS):
                act.wait_ge(wuk_t_ready, h + 1)
                act.activation(wuk_t[:, h], misc[h % 4][:], ACT.Copy).then_inc(wuk_t_copied, 1)
            act.wait_ge(qa_ready, 1)
            act.activation(qa[:, 0:4].rearrange("p k b h -> p k h b"), gemm[3][:, 0:256].rearrange("p (k h b) -> p k h b", k=4, h=8), ACT.Copy)
            for half in range(2):
                rows = slice(half * QK_ROPE, (half + 1) * QK_ROPE)
                last = act.activation(qa[rows, 4 + half].rearrange("p b h -> p h b"), qps[rows], ACT.Copy)
            last.then_inc(wuk_t_copied, 1)
            act.wait_ge(wuk_t_copied, 9)

            def turn_hi(g, hg):
                act.wait_ge(t_ready, g + 1)
                for j in range(2):
                    act.activation(ct_hi[:, hg % 2, :, j * P:(j + 1) * P], misc[(hg % 2) * 2 + j][:].rearrange("p (k c) -> p k c", k=4), ACT.Copy)
                act.activation(kt_hi[:, hg % 2], gemm[0][:, 0:P], ACT.Copy).then_inc(t_hi_done, 1)

            def second_half(s, k):
                width = 512 if k else N_SAMPLE
                act.wait_ge(sc_ready, s * 5 + (k + 1))
                act.wait_ge(sc_added, s * 5 + k)
                act.activation(half2[0:N_HEADS, 0:width], gemm[2][32:40, 0:width], ACT.Copy).then_inc(half_copied, 1)

            def last_half(b):
                act.wait_ge(opv_done, b + 1)
                act.activation(half2[0:N_HEADS, 0:KV_LORA], gemm[3][32:40, :], ACT.Copy).then_inc(ohalf_copied, 1)

            def page_hi(hg, v):
                k = v * N_PAGES + 2 * hg
                act.activation(cp_hi[:, hg % 2], ckv[:, k:k + 2], ACT.Copy).then_inc(p_hi_done, 1)

            def sample_act(s, u, half):
                static = isinstance(s, int)
                if not static or s < N_SAMPLE:
                    act.wait_ge(sc_ready, s * 5)
                    act.activation(q_st[:, :, 0:N_HEADS], qa[:, :, ds(s, 1), :].rearrange("p k b h -> p k (b h)"), ACT.Copy).then_inc(q_hi_done, 1)
                    second_half(s, 0)
                for hg in range(8):
                    if not static or s < N_SAMPLE - (1 if hg == 7 else 0):
                        turn_hi(s * 8 + (hg + 1), (hg + 1) % 8)
                    if hg == 0 and (not static or s >= 1):
                        act.wait_ge(smax_ready, s)
                        v = 1 - u
                        act.activation(sc[v][0:N_HEADS, :], sc[v][0:N_HEADS, :], ACT.Exp, scale=SCALE, bias=stat[0:N_HEADS, SMAX + v:SMAX + v + 1],
                                       accum_out=stat[0:N_HEADS, SUM + v:SUM + v + 1]).then_inc(sexp_done, 1)
                    if hg == 0 and (not static or s >= 2):
                        act.wait_ge(sc_added, s * 5 + 1 if not static or s < N_SAMPLE else s * 5)
                        last_half(s - 2)
                    if hg == 0 and (not static or s >= 1):
                        act.wait_ge(spt_ready, s)
                        act.activation(p_t[:, 0:N_PAGES, 0:N_HEADS], gemm[1][:, 0:P].rearrange("p (j h) -> p j h", h=N_HEADS), ACT.Copy)
                        act.activation(p_t[0:N_SAMPLE, N_PAGES, 0:N_HEADS], gemm[1][0:N_SAMPLE, P:P + N_HEADS], ACT.Copy).then_inc(spt_hi_done, 1)
                    if static and s == 0:
                        if hg == 7:
                            page_hi(0, 0)
                    elif hg < 7:
                        if not (static and s == 1 and hg == 0):
                            act.wait_ge(pv_pair_done, s * 8 + (hg - 8))
                        page_hi(hg + 1, 1 - u)
                    elif not static or s < N_SAMPLE:
                        act.wait_ge(pv_pair_done, s * 8 - 1)
                        page_hi(0, u)
                    if hg % 2 and (not static or s < N_SAMPLE):
                        second_half(s, (hg + 1) // 2)

            turn_hi(0, 0)
            samples(act, sample_act)
            act.wait_ge(olat_step, 3 * 7)
            last_half(7)

            act.wait_ge(os_step, 6)
            act.activation(comb_hi[:, 8:16, T_PROMPT:T], oz[:], ACT.Copy).then_inc(os_step, 1)

            def out_hi(j, slot, r):
                act.wait_ge(w_loaded[slot], (r + (B_OUT + 1 - slot) // 2 + 3) * 16)
                if not isinstance(j, int) or j >= 2:
                    act.wait_ge(gemm_done, j + (B_V - 1))
                act.activation(w_hi[:, slot, :], w_raw[:, slot, :], ACT.Copy).then_inc(w_hi_ready, 1)

            def out_copy(j, slot):
                act.wait_ge(gemm_done, j + (B_V + 1))
                act.wait_ge(out_t_ready, j + 1)
                for h in range(2):
                    last = act.activation(yb[:, slot, h * 260:(h + 1) * 260], gemm[2 * slot + h][:, 0:260], ACT.Copy)
                last.then_inc(gemm_read, 1)

            out_hi(0, 0, 0)
            out_hi(1, 1, 0)
            with act.Fori(0, 7) as i:
                for u in range(2):
                    out_copy(i * 2 + u, u)
                    out_hi(i * 2 + (2 + u), u, i + 1)
            out_copy(14, 0)
            out_copy(15, 1)
            for t in range(5):
                y, rows = (yt[:, t], P) if t < 4 else (ysm[0:N_SAMPLE], N_SAMPLE)
                act.wait_ge(out_added, 18)
                act.activation(junk2[0:rows], y, ACT.Square, accum_out=stat[0:rows, t:t + 1]).then_inc(x_squared, 1)
                act.wait_ge(var_ready, t + 8)
                act.activation(stat[0:rows, 16 + t:17 + t], stat[0:rows, 8 + t:9 + t], ACT.Sqrt).then_inc(std_ready, 1)

        @block.vector
        def _(dve):
            dve.sem_inc(gemm_read, 2)
            dve.sem_inc(ev_stored[0], 16)
            dve.sem_inc(ev_stored[1], 16)

            def scale(t):
                t0, rows = TILES[t]
                dve.wait_ge(x_squared, t + 1)
                dve.tensor_scalar(stat[0:rows, 8 + t:9 + t], stat[0:rows, t:t + 1], 1.0 / D_MODEL, EPS,
                                  ALU.mult, ALU.add).then_inc(var_ready, 1)
                dve.wait_ge(std_ready, t + 1)
                dve.reciprocal(stat[0:rows, 24 + t:25 + t], stat[0:rows, 16 + t:17 + t]).then_inc(rstd_ready, 1)
                dve.wait_ge(rstd_ready, t + 1)
                if t == 0:
                    dve.wait_ge(g_loaded, 16)
                dve.scalar_tensor_tensor(out=xtok[0:rows, t], in0=xtok[0:rows, t], scalar=stat[0:rows, 24 + t:25 + t],
                                         in1=gbc[0:rows], op0=ALU.mult, op1=ALU.mult).then_inc(x_scaled, 1)

            def split_lo(n, slot, ahead):
                if ahead is not None:
                    width = block_width(ahead)
                    dve.wait_ge(w_hi_ready, n + 3)
                    dve.tensor_tensor(w_lo[:, slot, 0:width], w_raw[:, slot, 0:width],
                                      w_hi[:, slot, 0:width].bitcast(F32), ALU.subtract).then_inc(w_lo_ready, 1)

            scale(0)
            scale(1)
            for g in range(20):
                t, q = divmod(g, 4)
                t0, rows = TILES[t]
                dve.wait_ge(xh_done, g + 1)
                dve.tensor_tensor(xl[:, 4 * q:4 * q + 4, t0:t0 + rows],
                                  misc[g % 4][:].rearrange("p (k t) -> p k t", k=4)[:, :, 0:rows],
                                  xh[:, 4 * q:4 * q + 4, t0:t0 + rows].bitcast(F32), ALU.subtract).then_inc(xl_done, 1)
                if q == 3 and t < 3:
                    scale(t + 2)
                if q == 3 and t in (2, 3):
                    split_lo(t - 4, t - 2, B_LAT)
                if g == 0:
                    dve.wait_ge(prep_loaded, 16 * 13)
                    dve.tensor_copy(anat[0:PAIRS, 2, :].rearrange("p (t n) -> p t n", t=2),
                                    ldt[0:PAIRS, :].unsqueeze(2).to_broadcast([PAIRS, 2, N_STATE])).then_inc(ldt_spread, 1)

            dve.wait_ge(prep_t_ready, 1)
            dve.tensor_copy(coef[:, 0:3], misc[0][:, 0:3 * PAIRS].rearrange("p (a q) -> p a q", a=3)).then_inc(prep_t_read, 1)
            dve.tensor_copy(vecs[:, 0:26], misc[0][:, P:P + 26]).then_inc(prep_t_read, 1)
            dve.wait_ge(prep_t_ready, 2)
            for h in range(2):
                for c in range(2):
                    dve.tensor_copy(states[:, 4 * h:4 * h + 4, c, :],
                                    misc[1][:].rearrange("p (h c b q) -> p h c b q", h=2, c=2, b=4)[:, h, c]).then_inc(prep_t_read, 1)
            dve.memset(cbd[:], 0.0).then_inc(prep_t_read, 1)
            dve.wait_ge(prep_t_read, 7)
            dve.wait_ge(prep_t_ready, 3)
            for c in range(2):
                for t in range(2):
                    rows = slice(t * N_STATE, (t + 1) * N_STATE)
                    dve.tensor_scalar(cbd[rows, c, :, t, :], misc[2 + c][rows, :].rearrange("p (q c) -> p q c", c=GROUP),
                                      -1.0 if c else 1.0, None, ALU.mult).then_inc(prep_t_read, 1)

            step = [0]

            def link(ins):
                step[0] += 1
                ins.then_inc(dve_step, 1)
                dve.wait_ge(dve_step, step[0])

            AR, AI, DT, XR, MAG, TH, ROT, R, SN, CS, DEN, NR, FR, FI, U1, U2 = 0, 1, 3, 4, 5, 8, 12, 8, 10, 11, 6, 7, 16, 17, 18, 19
            c_ = lambda k: coef[:, k]
            tt = dve.tensor_tensor
            dve.wait_ge(dt_ready, 1)
            link(tt(c_(XR), c_(DT), c_(AR), ALU.mult))
            link(tt(c_(TH), c_(DT), c_(AI), ALU.mult))
            link(dve.tensor_scalar(c_(TH + 1), c_(TH), math.pi / 2, None, ALU.add))
            big_ = float(3 << 22)
            c1 = 6.28125
            c2 = 2 * math.pi - c1
            link(dve.tensor_scalar(coef[:, ROT:ROT + 2], coef[:, TH:TH + 2], 1 / (2 * math.pi), big_, ALU.mult, ALU.add))
            link(dve.tensor_scalar(coef[:, ROT:ROT + 2], coef[:, ROT:ROT + 2], -big_, None, ALU.add))
            link(dve.scalar_tensor_tensor(out=coef[:, R:R + 2], in0=coef[:, ROT:ROT + 2], scalar=-c1, in1=coef[:, R:R + 2],
                                          op0=ALU.mult, op1=ALU.add))
            link(dve.scalar_tensor_tensor(out=coef[:, R:R + 2], in0=coef[:, ROT:ROT + 2], scalar=-c2, in1=coef[:, R:R + 2],
                                          op0=ALU.mult, op1=ALU.add))
            dve.tensor_scalar(coef[:, R:R + 2], coef[:, R:R + 2], 3.1415925, -3.1415925, ALU.min, ALU.max).then_inc(angle_ready, 1)
            dve.wait_ge(sin_ready, 1)
            dve.wait_ge(mag_ready, 1)
            re, im = powers[:, 0], powers[:, 1]
            link(dve.memset(re[:, 0], 1.0))
            link(dve.memset(im[:, 0], 0.0))
            link(tt(re[:, 1], c_(MAG), c_(CS), ALU.mult))
            link(tt(im[:, 1], c_(MAG), c_(SN), ALU.mult))
            for k in (1, 2, 4):
                by = lambda z: z[:, k:k + 1].to_broadcast([P, k, PAIRS])
                t = [tmp[:, i, 0:k * PAIRS].rearrange("p (k q) -> p k q", k=k) for i in range(4)]
                link(tt(t[0], re[:, 1:k + 1], by(re), ALU.mult))
                link(tt(t[1], im[:, 1:k + 1], by(im), ALU.mult))
                link(tt(t[2], re[:, 1:k + 1], by(im), ALU.mult))
                link(tt(t[3], im[:, 1:k + 1], by(re), ALU.mult))
                link(tt(re[:, k + 1:2 * k + 1], t[0], t[1], ALU.subtract))
                link(tt(im[:, k + 1:2 * k + 1], t[2], t[3], ALU.add))
            link(tt(c_(U1), c_(AR), c_(AR), ALU.mult))
            link(tt(c_(U2), c_(AI), c_(AI), ALU.mult))
            link(tt(c_(DEN), c_(U1), c_(U2), ALU.add))
            link(dve.reciprocal(c_(DEN), c_(DEN)))
            link(dve.tensor_scalar(c_(NR), re[:, 1], -1.0, None, ALU.add))
            link(tt(c_(U1), c_(NR), c_(AR), ALU.mult))
            link(tt(c_(U2), im[:, 1], c_(AI), ALU.mult))
            link(tt(c_(U1), c_(U1), c_(U2), ALU.add))
            link(tt(c_(FR), c_(U1), c_(DEN), ALU.mult))
            link(tt(c_(U1), im[:, 1], c_(AR), ALU.mult))
            link(tt(c_(U2), c_(NR), c_(AI), ALU.mult))
            link(tt(c_(U1), c_(U1), c_(U2), ALU.subtract))
            link(tt(c_(FI), c_(U1), c_(DEN), ALU.mult))
            t = [tmp[:, i, :].rearrange("p (q c) -> p q c", c=GROUP) for i in range(4)]
            wide = lambda z: z.unsqueeze(2).to_broadcast([P, PAIRS, GROUP])
            link(tt(t[0], bbar[:, 0], wide(c_(FR)), ALU.mult))
            link(tt(t[1], bbar[:, 1], wide(c_(FI)), ALU.mult))
            link(tt(t[2], bbar[:, 1], wide(c_(FR)), ALU.mult))
            link(tt(t[3], bbar[:, 0], wide(c_(FI)), ALU.mult))
            link(tt(bbar[:, 0], t[0], t[1], ALU.subtract))
            link(tt(bbar[:, 1], t[2], t[3], ALU.add))
            dve.memset(xgrp[:, :, 0:N_SAMPLE], 0.0).then_inc(coef_ready, 1)
            dve.memset(xgrp[:, :, YCOLS:82], 0.0).then_inc(coef_ready, 1)
            dve.memset(states[:, N_SAMPLE], 0.0).then_inc(coef_ready, 1)

            def copy_out(n, r, slot, ahead):
                split_lo(n, slot, ahead)
                dve.wait_ge(gemm_done, n + 1)
                dve.wait_ge(ev_stored[slot], (r + 1) * 16)
                for h, (h0, hw) in enumerate(HALVES):
                    last = dve.tensor_copy(ev[:, slot, h0:h0 + hw], gemm[2 * slot + h][:, 0:hw])
                last.then_inc(gemm_read, 1)

            def copy_u(n, r, slot, ahead):
                split_lo(n, slot, ahead)
                dve.wait_ge(gemm_done, n + 1)
                dve.wait_ge(ev_stored[slot], (r + 1) * 16)
                out = ev[:, slot, 0:T_PROMPT].rearrange("p (j k) -> p k j", k=N_CHUNK)
                for h in range(2):
                    dve.tensor_copy(out[:, 33 * h:33 * h + 33],
                                    gemm[2 * slot + h][:, 0:264].rearrange("p (k j) -> p k j", j=CHUNK))
                dve.tensor_copy(ev[:, slot, T_PROMPT:T], gemm[2 * slot + 1][:, 264:272]).then_inc(gemm_read, 1)

            blocks(dve, B_LAT, 11, copy_out)
            blocks(dve, B_U, 8, copy_u)

            re4 = lambda c, b: powers[:, c, 0:CHUNK, ds(b * 4, 4)].rearrange("p l q -> p q l")
            dve.sem_inc(s_im_copied, 1)
            dve.sem_inc(s_re_copied, 1)
            dve.sem_inc(k_copied, 1)
            dve.wait_ge(coef_ready, 3)
            def build(b, slot):
                t4 = [tmp[:, i].rearrange("p (q l c) -> p q l c", q=4, l=CHUNK) for i in range(4)]
                for i, (pc, bc) in enumerate(((0, 0), (1, 1), (0, 1), (1, 0))):
                    pw = powers[:, pc, 0:CHUNK, ds(b * 4, 4)].rearrange("p l q -> p q l").unsqueeze(3).to_broadcast([P, 4, CHUNK, GROUP])
                    bb = bbar[:, bc, ds(b * 4, 4), :].unsqueeze(2).to_broadcast([P, 4, CHUNK, GROUP])
                    last = tt(t4[i], pw, bb, ALU.mult)
                last.then_inc(mul_done, 1)
                dve.wait_ge(mul_done, b + 1)
                tt(wst[:, slot, 0], t4[0], t4[1], ALU.subtract)
                tt(wst[:, slot, 1], t4[2], t4[3], ALU.add).then_inc(wst_built, 1)
                dve.wait_ge(wst_built, b + 1)

            def first_pass(b):
                dve.wait_ge(bt_ready, b + 1)
                dve.tensor_copy(bst[:, 1], misc[1][:].rearrange("p (q m) -> p q m", q=4)).then_inc(bt_im_copied, 1)
                dve.wait_ge(s_ready, b + 1)
                dve.tensor_copy(states[:, N_SAMPLE + 1:ENTRIES, 1, ds(b * 4, 4)],
                                misc[0][:, 0:4 * YCOLS].rearrange("p (q e) -> p e q", q=4)).then_inc(s_im_copied, 1)

            for b in range(2):
                build(b, b)
            for n in (B_ZS, B_ZS + 1):
                split_lo(n, n % 2, B_ZS)
            with dve.Fori(0, 3) as i:
                for u in range(2):
                    first_pass(i * 2 + u)
                    build(i * 2 + (2 + u), u)
                    split_lo(i * 2 + (B_ZS + 2 + u), (B_ZS + u) % 2, B_ZS)
            for b in (6, 7):
                first_pass(b)

            a8 = [powers[:, c, 8].unsqueeze(1).to_broadcast([P, 2, PAIRS]) for c in range(2)]
            m1, m2 = [tmp[:, i, 0:2 * PAIRS].rearrange("p (c q) -> p c q", c=2) for i in range(2)]

            def scan(k):
                prev = states[:, ds(k + N_SAMPLE, 1)].rearrange("p e c q -> p (e c) q")
                new = states[:, ds(k + (N_SAMPLE + 1), 1)].rearrange("p e c q -> p (e c) q")
                tt(m1, prev, a8[0], ALU.mult)
                tt(m2, prev, a8[1], ALU.mult).then_inc(scan_step, 1)
                dve.wait_ge(scan_step, k * 3 + 1)
                tt(new, new, m1, ALU.add).then_inc(scan_step, 1)
                dve.wait_ge(scan_step, k * 3 + 2)
                tt(new[:, 0], new[:, 0], m2[:, 1], ALU.subtract)
                tt(new[:, 1], new[:, 1], m2[:, 0], ALU.add).then_inc(scan_step, 1)
                dve.wait_ge(scan_step, k * 3 + 3)

            dve.wait_ge(s_re_copied, 9)
            dve.wait_ge(s_im_copied, 9)
            h0, hs = states[:, 0:N_SAMPLE], states[:, ENTRIES - N_SAMPLE:ENTRIES]
            a1 = [powers[:, c, 1].unsqueeze(1).to_broadcast([P, N_SAMPLE, PAIRS]) for c in range(2)]
            m = [tmp[:, i, 0:256].rearrange("p (b q) -> p b q", q=PAIRS) for i in range(4)]
            for i, (c, e) in enumerate(((0, 0), (1, 1), (0, 1), (1, 0))):
                last = tt(m[i], h0[:, :, c], a1[e], ALU.mult)
            last.then_inc(sample_step, 1)
            dve.wait_ge(sample_step, 1)
            tt(m[0], m[0], m[1], ALU.subtract)
            tt(m[2], m[2], m[3], ALU.add).then_inc(sample_step, 1)
            dve.wait_ge(sample_step, 2)
            tt(snew[:, 0], hs[:, :, 0], m[0], ALU.add)
            tt(snew[:, 1], hs[:, :, 1], m[2], ALU.add).then_inc(sample_step, 1)
            dve.wait_ge(sample_step, 3)

            def build_out(b):
                if b >= 2:
                    dve.wait_ge(y_ready, 2 * b - 2)
                for q in range(2):
                    g = 4 * b + q
                    for c in range(2):
                        out = cast[:, b % 2, c, q]
                        t2 = [tmp[:, 2 * c + i, 0:256].rearrange("p (t l c) -> p t l c", t=2, l=CHUNK) for i in range(2)]
                        for i in range(2):
                            pw = powers[:, (c + i) % 2, 1:9, g].unsqueeze(1).to_broadcast([P, 2, CHUNK])
                            pw = pw.unsqueeze(3).to_broadcast([P, 2, CHUNK, GROUP])
                            cc = cbd[:, i, g].unsqueeze(2).to_broadcast([P, 2, CHUNK, GROUP])
                            last = tt(t2[i], pw, cc, ALU.mult)
                        last.then_inc(mul_done, 1)
                        dve.wait_ge(mul_done, 8 + 4 * b + 2 * q + c + 1)
                        if c == 0:
                            last = tt(out, t2[0], t2[1], ALU.add)
                        else:
                            last = tt(out, t2[1], t2[0], ALU.subtract)
                last.then_inc(ca_built, 1)

            dve.wait_ge(k_ready, 8)
            build_out(0)
            SCAN_FIRST = N_CHUNK % 8
            for k in range(SCAN_FIRST):
                scan(k)

            def split_and_scan(n, r, slot, ahead):
                for j in range(8):
                    scan((n - B_ZA) * 8 + (SCAN_FIRST + j))
                split_lo(n, slot, ahead)

            blocks(dve, B_ZA, 8, split_and_scan)

            dve.wait_ge(gemm_done, B_GLU)
            dve.memset(toep[:, 4:CHUNK - 1], 0.0).then_inc(coef_ready, 1)

            def add_skip(b):
                dve.wait_ge(ug_loaded[b % 2], 16 * (b // 2 + 1))
                if b >= 2:
                    dve.wait_ge(gelu_done, b - 1)
                for h in range(2):
                    dve.wait_ge(yt_ready, 2 * b + h + 1)
                    out = yg[:, b % 2, 0:T_PROMPT].rearrange("p (k j) -> p j k", j=CHUNK)[:, 4 * h:4 * h + 4]
                    src = misc[2 + h][:, 0:4 * YCOLS].rearrange("p (j k) -> p j k", j=4)
                    uu = ug[:, b % 2, 0:T_PROMPT].rearrange("p (j k) -> p j k", j=CHUNK)[:, 4 * h:4 * h + 4]
                    last = dve.scalar_tensor_tensor(out=out, in0=uu, scalar=vecs[:, 18 + b:19 + b],
                                                    in1=src[:, :, N_SAMPLE:], op0=ALU.mult, op1=ALU.add)
                    if h == 0:
                        last = dve.scalar_tensor_tensor(out=yg[:, b % 2, T_PROMPT:T], in0=ug[:, b % 2, T_PROMPT:T],
                                                        scalar=vecs[:, 18 + b:19 + b], in1=src[:, 0, 0:N_SAMPLE],
                                                        op0=ALU.mult, op1=ALU.add)
                    last.then_inc(yt_added, 1)

            dve.wait_ge(toep_loaded, 16 * CHUNK)
            build_out(1)
            for b in range(8):
                dve.wait_ge(y_ready, 2 * b + 2)
                if b >= 2:
                    dve.wait_ge(yt_ready, 2 * b - 2)
                dve.tensor_copy(ychunk[0:YCOLS, b % 2, :, 64:P].rearrange("p i (g c) -> p g i c", c=GROUP),
                                misc[1][0:YCOLS, :].rearrange("p (g i c) -> p g i c", g=4, c=GROUP)).then_inc(y_copied, 1)
                if b < 6:
                    build_out(b + 2)
                add_skip(b)
            dve.wait_ge(state_t_ready, 1)
            dve.tensor_copy(sout[:, 0:4, :], misc[0][:].rearrange("p (a m) -> p a m", a=4)).then_inc(state_copied, 4)
            dve.wait_ge(state_t_ready, 2)
            dve.tensor_copy(sout[0:PAIRS, 4:6, :], misc[1][0:PAIRS, 0:2 * P].rearrange("p (a m) -> p a m", a=2)).then_inc(state_copied, 2)
            for k in range(8):
                dve.wait_ge(ys_hi_done, k + 1)
                tt(ys_lo[:, k], ys[:, k], ys_hi[:, k].bitcast(F32), ALU.subtract).then_inc(ys_lo_done, 1)
            dve.sem_inc(comb_lo_done, 2)

            def glu(n, r, slot, ahead):
                split_lo(n, slot, ahead)
                dve.wait_ge(sig_done, n - (B_GLU - 1))
                dve.wait_ge(gate_loaded[slot], gate_count(n, r, slot))
                y = ys[:, ds(n - B_GLU, 1), :].rearrange("p a t -> p (a t)")
                tt(sig[:, slot], sig[:, slot], y, ALU.mult).then_inc(gemm_read, 1)
                dve.wait_ge(gemm_read, n + 3)
                tt(gate[:, slot], gate[:, slot], sig[:, slot], ALU.mult).then_inc(gated, 1)
                dve.wait_ge(comb_hi_done, n - (B_GLU - 1))
                lo = comb_lo[:, ds(n - B_GLU, 1), :].rearrange("p a t -> p (a t)")
                hi = comb_hi[:, ds(n - B_GLU, 1), :].rearrange("p a t -> p (a t)")
                tt(lo, gate[:, slot], hi.bitcast(F32), ALU.subtract).then_inc(comb_lo_done, 1)

            def norms():
                for i, width in enumerate((Q_LORA, KV_LORA)):
                    dve.wait_ge(sums_ready, i + 1)
                    for h, (h0, hw) in enumerate(HALVES):
                        last = dve.tensor_scalar(rs[:, i, h0:h0 + hw], misc[2 * i + h][:, 0:hw], 1.0 / width, EPS, ALU.mult, ALU.add)
                    last.then_inc(var_ready, 1)
                for i in range(2):
                    dve.wait_ge(std_ready, i + 6)
                    dve.reciprocal(rs[:, i], rs[:, i]).then_inc(rstd_ready, 1)

            blocks(dve, B_GLU, 8, glu, norms)

            dve.wait_ge(comb_lo_done, 10)
            for k in range(6):
                dve.wait_ge(n_hi_done, k + 1)
                dve.scalar_tensor_tensor(out=qn_lo[:, k], in0=latq[:, k], scalar=vecs[:, k:k + 1], in1=qn_hi[:, k].bitcast(F32),
                                         op0=ALU.mult, op1=ALU.subtract).then_inc(n_lo_done, 1)
            for k in range(4):
                dve.wait_ge(normed, k + 7)
                dve.tensor_scalar(latc[:, k], latc[:, k], vecs[:, 6 + k:7 + k], None, ALU.mult).then_inc(c_scaled, 1)
            for k in range(4):
                dve.wait_ge(n_hi_done, k + 7)
                tt(cn_lo[:, k], latc[:, k], cn_hi[:, k].bitcast(F32), ALU.subtract).then_inc(n_lo_done, 1)

            def copy_q(stores):
                def body(n, r, slot, ahead):
                    split_lo(n, slot, ahead)
                    dve.wait_ge(gemm_done, n + 1)
                    dve.wait_ge(ev_stored[slot], (stores(r, slot) + 1) * 16)
                    for h, (h0, hw) in enumerate(HALVES):
                        last = dve.tensor_copy(ev[:, slot, h0:h0 + hw], gemm[2 * slot + h][:, 0:hw])
                    last.then_inc(gemm_read, 1)
                return body

            blocks(dve, B_QN, 8, copy_q(lambda r, slot: r - 4))

            def keep_rotary(n, r, slot, ahead):
                split_lo(n, slot, ahead)
                dve.wait_ge(gemm_done, n + 1)
                for h, (h0, hw) in enumerate(HALVES):
                    last = dve.tensor_copy(rp[:, ds(n - B_QR, 1), h0:h0 + hw].rearrange("p a t -> p (a t)"), gemm[2 * slot + h][:, 0:hw])
                last.then_inc(gemm_read, 1)

            blocks(dve, B_QR, 4, keep_rotary)
            blocks(dve, B_K, 8, copy_q(lambda r, slot: r - 6))

            dve.wait_ge(rope_loaded, 64)
            for v in range(10):
                rows = TILES[v % 5][1]
                dve.wait_ge(v_ready, v + 1)
                if v >= 2:
                    dve.wait_ge(v_stored[v % 2], 16 * (v // 2))
                dve.tensor_copy(vout[0:rows, v % 2, :], gemm[v % 4][0:rows, :]).then_inc(v_copied, 1)
                if v < 5:
                    dve.wait_ge(rotated, v + 1)
                    dve.wait_ge(ev_stored[v % 2], 16 * (1 + EV_STORES[v % 2] + v // 2))
                    for h, (h0, hw) in enumerate(HALVES):
                        last = tt(ev[:, v % 2, h0:h0 + hw], misc[2 + h][:, 0:hw], sin[:, h0:h0 + hw], ALU.mult)
                    last.then_inc(rope_step, 1)
                    tt(rp[:, v], rp[:, v], cos[:], ALU.mult).then_inc(rope_step, 1)
                    dve.wait_ge(rope_step, 2 * v + 2)
                    tt(ev[:, v % 2], ev[:, v % 2], rp[:, v], ALU.add).then_inc(rope_done, 1)
            dve.wait_ge(c_t_ready, 6)
            dve.wait_ge(state_stored, 16 * 6)
            dve.tensor_copy(kout[:], misc[0][:, 0:5 * QK_ROPE].rearrange("p (t r) -> p t r", t=5)).then_inc(kpe_copied, 1)

            NM, SM, RS = 0, 12, 24
            dve.sem_inc(o_gated, 1)
            dve.sem_inc(ot_copied, 1)
            dve.wait_ge(kp_hi_done, 1)
            tt(kp_lo[0:QK_ROPE], kp_raw[0:QK_ROPE], kp_hi[0:QK_ROPE].bitcast(F32), ALU.subtract).then_inc(kp_lo_done, 1)

            def maximum(n, m, head):
                i = m % 5
                rows = P if i < 4 else N_META
                width = P * min(i + 1, 4)
                bank = SBANK[m]
                dve.wait_ge(scores_ready, n + 1)
                diag = bank[:, i * P:(i + 1) * P] if i < 4 else misc[0][0:rows, EXTRA]
                tt(diag, diag, causal[0:rows, 0:rows], ALU.add).then_inc(max_step, 1)
                dve.wait_ge(max_step, head * 11 + (2 * i + 1))
                nm = stat[0:rows, NM + m:NM + m + 1]
                if i < 4:
                    dve.reduce_max(nm, bank[0:rows, 0:width], axis=AX.X).then_inc(max_step, 1)
                else:
                    parts = stat[0:rows, 42 + 2 * (m // 5):44 + 2 * (m // 5)]
                    dve.reduce_max(parts[:, 0:1], bank[0:rows, 0:width], axis=AX.X)
                    dve.reduce_max(parts[:, 1:2], misc[0][0:rows, EXTRA], axis=AX.X).then_inc(max_step, 1)
                    dve.wait_ge(max_step, head * 11 + 10)
                    tt(nm, parts[:, 0:1], parts[:, 1:2], ALU.max).then_inc(max_step, 1)
                dve.wait_ge(max_step, head * 11 + (2 * i + 2 if i < 4 else 11))
                dve.tensor_scalar(nm, nm, -SCALE, None, ALU.mult).then_inc(max_ready, 1)

            def normalise(n, m, head):
                i = m % 5
                rows = P if i < 4 else N_META
                width = P * (i + 1) if i < 4 else T_PROMPT
                sm, r = stat[0:rows, SM + m:SM + m + 1], stat[0:rows, RS + m:RS + m + 1]
                dve.wait_ge(exp_done, n + 1)
                if i == 4:
                    tt(sm, sm, stat[0:rows, 40 + m // 5:41 + m // 5], ALU.add).then_inc(sum_step, 1)
                    dve.wait_ge(sum_step, head * 6 + 5)
                dve.reciprocal(r, sm).then_inc(sum_step, 1)
                dve.wait_ge(sum_step, head * 6 + (i + 1 if i < 4 else 6))
                p = prob[0:rows, m % 2, 0:width]
                dve.tensor_scalar(p, p, r, None, ALU.mult).then_inc(prob_ready, 1)

            def pt_low(n, m):
                i = m % 5
                rows = P if i < 4 else N_META
                q0 = i * P
                dve.wait_ge(pt_hi_done, n + 1)
                src = misc[2 + m % 2][:, 0:5 * rows if i == 4 else (i + 1) * P].rearrange("p (j q) -> p j q", q=rows)
                w = min(i + 1, 4)
                last = tt(pt_lo[:, 0:w, q0:q0 + rows], src[:, 0:w], pt_hi[:, 0:w, q0:q0 + rows].bitcast(F32), ALU.subtract)
                if i == 4:
                    last = tt(pt_lo[0:rows, 4, q0:q0 + rows], src[0:rows, 4], pt_hi[0:rows, 4, q0:q0 + rows].bitcast(F32), ALU.subtract)
                last.then_inc(pt_lo_done, 1)

            def gate_o(h, u, count):
                dve.wait_ge(ug_loaded[u], (count + 5) * 16)
                dve.wait_ge(pv_done, h + 2)
                tt(otmp[:, u, 0:256], gemm[3][:, 0:256], za[:, u, 0:256], ALU.mult)
                tt(otmp[:, u, 256:T_PROMPT], misc[0][:, 0:272], za[:, u, 256:T_PROMPT], ALU.mult).then_inc(o_gated, 1)
                dve.wait_ge(comb_hi_done, h + 9)
                tt(comb_lo[:, ds(h + 8, 1), 0:T_PROMPT].rearrange("p a t -> p (a t)"), otmp[:, u, 0:T_PROMPT],
                   comb_hi[:, ds(h + 8, 1), 0:T_PROMPT].rearrange("p a t -> p (a t)").bitcast(F32), ALU.subtract).then_inc(comb_lo_done, 1)

            maximum(0, 0, 0)
            maximum(1, 1, 0)
            normalise(0, 0, 0)
            maximum(2, 2, 0)

            def head_dve(pair, u, last):
                tile = lambda k: (pair * 10 + k, k % 10, pair * 2 + k // 5)
                for i in range(5):
                    m = 5 * u + i
                    if not (last and m == 9):
                        normalise(*tile(m + 1))
                    if i > 0 and not (last and m >= 8):
                        maximum(*tile(m + 2))
                    pt_low(pair * 10 + m, m)
                if not (last and u == 1):
                    maximum(*tile(5 * u + 7))
                gate_o(pair * 2 + u, u, pair)

            head_pairs(dve, head_dve)

            SUM, RSUM, PART, SMAX = 48, 50, 52, 58
            dve.wait_ge(new_hi_done, 1)
            tt(kpn_lo[0:QK_ROPE], kpn_raw[0:QK_ROPE], kpn_hi[0:QK_ROPE].bitcast(F32), ALU.subtract)
            tt(cnew_lo[0:N_SAMPLE], half2[0:N_SAMPLE], cnew_hi[0:N_SAMPLE].bitcast(F32), ALU.subtract).then_inc(new_lo_done, 1)

            def turn_lo(g, hg):
                dve.wait_ge(t_hi_done, g + 1)
                for j in range(2):
                    tt(ct_lo[:, hg % 2, :, j * P:(j + 1) * P], misc[(hg % 2) * 2 + j][:].rearrange("p (k c) -> p k c", k=4),
                       ct_hi[:, hg % 2, :, j * P:(j + 1) * P].bitcast(F32), ALU.subtract)
                tt(kt_lo[:, hg % 2], gemm[0][:, 0:P], kt_hi[:, hg % 2].bitcast(F32), ALU.subtract).then_inc(t_lo_done, 1)

            def add_halves(s, u, k):
                width = 512 if k else N_SAMPLE
                out = sc[u][0:N_HEADS, (k - 1) * 512:k * 512] if k else sc[u][0:N_HEADS, PAST:KEYS]
                dve.wait_ge(half_copied, s * 5 + (k + 1))
                tt(out, gemm[2][0:N_HEADS, 0:width], half2[0:N_HEADS, 0:width], ALU.add).then_inc(sc_added, 1)
                dve.wait_ge(sc_added, s * 5 + (k + 1))
                if k == 0:
                    tt(out, out, not_own[:, ds(s, 1), :].rearrange("p a b -> p (a b)"), ALU.add).then_inc(sc_step, 1)
                    dve.wait_ge(sc_step, s * 3 + 1)
                last = dve.reduce_max(stat[0:N_HEADS, PART + k:PART + k + 1], out, axis=AX.X)
                if k == 4:
                    last.then_inc(sc_step, 1)
                    dve.wait_ge(sc_step, s * 3 + 2)
                    nm = stat[0:N_HEADS, SMAX + u:SMAX + u + 1]
                    dve.reduce_max(nm, stat[0:N_HEADS, PART:PART + 5], axis=AX.X).then_inc(sc_step, 1)
                    dve.wait_ge(sc_step, s * 3 + 3)
                    dve.tensor_scalar(nm, nm, -SCALE, None, ALU.mult).then_inc(smax_ready, 1)

            def sum_latent(b, u):
                dve.wait_ge(sexp_done, b + 1)
                dve.wait_ge(ohalf_copied, b + 1)
                dve.wait_ge(ot_ready, b + 1)
                dve.reciprocal(stat[0:N_HEADS, RSUM + u:RSUM + u + 1], stat[0:N_HEADS, SUM + u:SUM + u + 1]).then_inc(olat_step, 1)
                tt(olat[0:N_HEADS], gemm[3][0:N_HEADS, :], half2[0:N_HEADS], ALU.add).then_inc(olat_step, 1)
                dve.wait_ge(olat_step, b * 3 + 2)
                dve.tensor_scalar(olat[0:N_HEADS], olat[0:N_HEADS], stat[0:N_HEADS, RSUM + u:RSUM + u + 1], None, ALU.mult).then_inc(olat_step, 1)

            def copy_ot(b):
                dve.wait_ge(ot_ready, b + 2)
                dve.tensor_copy(olat_t[:, :, :, ds(b, 1)].rearrange("p k h b -> p k (h b)"),
                                gemm[1][:, 256:288].rearrange("p (k h) -> p k h", k=4)).then_inc(ot_copied, 1)

            def sample_dve(s, u, half):
                static = isinstance(s, int)
                if not static or s < N_SAMPLE:
                    dve.wait_ge(q_hi_done, s + 1)
                    tt(q_st[:, :, 32:40], qa[:, :, ds(s, 1), :].rearrange("p k b h -> p k (b h)"), q_st[:, :, 0:N_HEADS].bitcast(F32),
                       ALU.subtract).then_inc(q_lo_done, 1)
                    if not static or s >= 2:
                        dve.wait_ge(spt_ready, s - 1)
                    add_halves(s, u, 0)
                for hg in range(8):
                    if not static or s < N_SAMPLE - (1 if hg == 7 else 0):
                        turn_lo(s * 8 + (hg + 1), (hg + 1) % 8)
                    if hg == 0 and (not static or s >= 2):
                        sum_latent(s - 2, u)
                    if hg == 0 and (not static or s >= 1):
                        dve.wait_ge(spt_hi_done, s)
                        tt(p_t[:, 0:N_PAGES, 32:40], gemm[1][:, 0:P].rearrange("p (j h) -> p j h", h=N_HEADS),
                           p_t[:, 0:N_PAGES, 0:N_HEADS].bitcast(F32), ALU.subtract)
                        tt(p_t[0:N_SAMPLE, N_PAGES, 32:40], gemm[1][0:N_SAMPLE, P:P + N_HEADS],
                           p_t[0:N_SAMPLE, N_PAGES, 0:N_HEADS].bitcast(F32), ALU.subtract).then_inc(spt_lo_done, 1)
                    if hg == 2 and (not static or s >= 2):
                        copy_ot(s - 2)
                    if hg % 2 and (not static or s < N_SAMPLE):
                        add_halves(s, u, (hg + 1) // 2)

            dve.wait_ge(wuk_t_copied, 9)
            turn_lo(0, 0)
            samples(dve, sample_dve)
            sum_latent(7, 1)
            copy_ot(7)

            for half in range(2):
                dve.wait_ge(os_step, half + 1)
                dve.tensor_copy(oh[0:N_SAMPLE, half * 512:(half + 1) * 512], gemm[half][0:N_SAMPLE, :]).then_inc(oh_copied, 1)
            dve.wait_ge(res_loaded, 16 * 7)
            dve.wait_ge(os_step, 3)
            tt(oz[:], misc[0][:, 0:64].rearrange("p (h b) -> p h b", h=8), zas[:], ALU.mult).then_inc(os_step, 3)
            dve.wait_ge(os_step, 7)
            tt(comb_lo[:, 8:16, T_PROMPT:T], oz[:], comb_hi[:, 8:16, T_PROMPT:T].bitcast(F32), ALU.subtract).then_inc(os_step, 1)

            def out_lo(j, slot):
                dve.wait_ge(w_hi_ready, j + (B_OUT + 1))
                tt(w_lo[:, slot, :], w_raw[:, slot, :], w_hi[:, slot, :].bitcast(F32), ALU.subtract).then_inc(w_lo_ready, 1)

            def out_add(j, slot):
                dve.wait_ge(out_t_ready, j + 3)
                cols = yt[:, :, ds(j * P, P)]
                tt(cols, cols, misc[slot][:].rearrange("p (t n) -> p t n", t=4), ALU.add)
                cols = ysm[0:N_SAMPLE, ds(j * P, P)]
                tt(cols, cols, misc[2 + slot][0:N_SAMPLE, 0:P], ALU.add).then_inc(out_added, 1)

            dve.sem_inc(out_added, 2)
            out_lo(0, 0)
            out_lo(1, 1)
            with dve.Fori(0, 7) as i:
                for u in range(2):
                    out_lo(i * 2 + (2 + u), u)
                    out_add(i * 2 + u, u)
            out_add(14, 0)
            out_add(15, 1)
            for t in range(5):
                y, rows = (yt[:, t], P) if t < 4 else (ysm[0:N_SAMPLE], N_SAMPLE)
                dve.wait_ge(x_squared, t + 6)
                dve.tensor_scalar(stat[0:rows, 8 + t:9 + t], stat[0:rows, t:t + 1], 1.0 / D_MODEL, EPS, ALU.mult, ALU.add).then_inc(var_ready, 1)
                dve.wait_ge(std_ready, t + 8)
                dve.reciprocal(stat[0:rows, 24 + t:25 + t], stat[0:rows, 16 + t:17 + t]).then_inc(rstd_ready, 1)
                dve.wait_ge(rstd_ready, t + 8)
                dve.scalar_tensor_tensor(out=y, in0=y, scalar=stat[0:rows, 24 + t:25 + t], in1=gfin[0:rows],
                                         op0=ALU.mult, op1=ALU.mult).then_inc(x_scaled, 1)

        @block.tensor
        def _(pe):
            pe.wait_ge(const_ready, 5)
            for g in range(20):
                t, q = divmod(g, 4)
                t0, rows = TILES[t]
                pe.wait_ge(x_scaled, t + 1)
                if g >= 4:
                    pe.wait_ge(xl_done, g - 3)
                for k in range(4):
                    last = pe.transpose(misc[g % 4][:, k * P:k * P + rows],
                                        xtok[0:rows, t, (4 * q + k) * P:(4 * q + k + 1) * P], ident[0:rows, 0:rows])
                last.then_inc(xt_ready, 1)

            pe.wait_ge(xl_done, 20)
            pe.wait_ge(ldt_spread, 1)
            for a in range(3):
                pe.transpose(misc[0][:, a * PAIRS:(a + 1) * PAIRS], anat[0:PAIRS, a, :], ident[0:PAIRS, 0:PAIRS])
            pe.transpose(misc[0][:, P:P + 26], vnat[0:26, :], ident[0:26, 0:26]).then_inc(prep_t_ready, 1)
            for h in range(2):
                for c in range(2):
                    last = pe.transpose(misc[1][:, (2 * h + c) * P:(2 * h + c + 1) * P], snat[:, h, c, :], ident[:])
            last.then_inc(prep_t_ready, 1)
            pe.wait_ge(cnat_loaded, 16 * 16)
            for b in range(4):
                for c in range(2):
                    last = pe.transpose(misc[2 + c][:, b * P:(b + 1) * P], cnat[:, b, c, :], ident[:])
            last.then_inc(prep_t_ready, 1)

            def multiply(n, slot, k_tiles, hi, lo):
                pe.wait_ge(w_lo_ready, n + 1)
                pe.wait_ge(gemm_read, n + 1)
                for h, (h0, hw) in enumerate(HALVES):
                    acc = gemm[2 * slot + h][:, 0:hw]
                    for k in range(k_tiles):
                        a, b = w_hi[:, slot, k * P:(k + 1) * P], w_lo[:, slot, k * P:(k + 1) * P]
                        xa, xb = hi[:, k, h0:h0 + hw], lo[:, k, h0:h0 + hw]
                        pe.matmul(acc, a, xa, start=k == 0, stop=False)
                        pe.matmul(acc, a, xb, start=False, stop=False)
                        last = pe.matmul(acc, b, xa, start=False, stop=k == k_tiles - 1)
                last.then_inc(gemm_done, 1)

            def project(n, r, slot, ahead):
                multiply(n, slot, KD, xh, xl)

            blocks(pe, B_LAT, 11, project)
            blocks(pe, B_U, 8, project)

            def first_pass(b):
                pe.wait_ge(wst_built, b + 1)
                pe.wait_ge(s_re_copied, b + 1)
                pe.wait_ge(s_im_copied, b + 1)
                pe.wait_ge(k_copied, b + 1)
                w = [wst[:, b % 2, c].rearrange("p q l c -> p q (l c)") for c in range(2)]
                for c in range(2):
                    for q in range(4):
                        last = pe.transpose(misc[c][:, q * P:(q + 1) * P], w[c][:, q], ident[:])
                last.then_inc(bt_ready, 1)
                for q in range(4):
                    for c in range(2):
                        last = pe.matmul(misc[2][:, q * 32:(q + 1) * 32], w[c][:, q],
                                         cbd[:, c, 4 * b + q].rearrange("p t c -> p (t c)"), start=c == 0, stop=c == 1)
                last.then_inc(k_ready, 1)
                pe.wait_ge(bt_re_copied, b + 1)
                pe.wait_ge(bt_im_copied, b + 1)
                for c in range(2):
                    acc = (misc[3], misc[0])[c]
                    for q in range(4):
                        for t in range(2):
                            rows = slice(t * N_STATE, (t + 1) * N_STATE)
                            last = pe.matmul(acc[rows, q * YCOLS:(q + 1) * YCOLS], bst[:, c, q, rows],
                                             xgrp[:, 8 * b + 2 * q + t, N_SAMPLE:82], start=True, stop=True)
                last.then_inc(s_ready, 1)

            for n in (B_ZS, B_ZS + 1):
                project(n, n // 2, n % 2, None)
            pe.wait_ge(prep_t_read, 11)
            pe.wait_ge(xgrp_loaded, 160)
            for b in range(8):
                first_pass(b)
                if b < 6:
                    n = B_ZS + 2 + b
                    project(n, n // 2, n % 2, None)
            blocks(pe, B_ZA, 8, project)

            pe.wait_ge(scan_step, 3 * N_CHUNK)
            pe.wait_ge(sample_step, 3)
            pe.wait_ge(toep_loaded, 16 * CHUNK)

            def transpose_out(b):
                pe.wait_ge(y_copied, 2 * b + 2)
                for h in range(2):
                    if b:
                        pe.wait_ge(yt_added, 2 * b - 1 + h)
                    for j in range(4):
                        last = pe.transpose(misc[2 + h][:, j * YCOLS:(j + 1) * YCOLS],
                                            ychunk[0:YCOLS, b % 2, 4 * h + j, :], ident[0:YCOLS, 0:YCOLS])
                    last.then_inc(yt_ready, 1)

            for b in range(8):
                pe.wait_ge(ca_built, b + 1)
                pe.wait_ge(ca_built_pool, 2 * b + 2)
                for h in range(2):
                    if b:
                        pe.wait_ge(y_copied, 2 * b)
                    for q in range(2):
                        p = 4 * b + 2 * h + q
                        acc = misc[h][0:YCOLS, q * 256:(q + 1) * 256]
                        for c in range(2):
                            pe.matmul(acc, states[:, 0:YCOLS, c, p], cast[:, b % 2, c, 2 * h + q].rearrange("p t l c -> p (t l c)"),
                                      start=c == 0, stop=False)
                        for t in range(2):
                            g = 2 * p + t
                            last = pe.matmul(acc[:, t * P:(t + 1) * P].rearrange("p (l c) -> p l c", c=GROUP),
                                             xgrp[:, g, 0:YCOLS], toep[:, :, g * GROUP:(g + 1) * GROUP],
                                             start=False, stop=t == 1)
                    last.then_inc(y_ready, 1)
                if b:
                    transpose_out(b - 1)
            transpose_out(7)
            pe.wait_ge(y_copied, 16)
            for h in range(2):
                for c in range(2):
                    last = pe.transpose(misc[0][:, (2 * h + c) * P:(2 * h + c + 1) * P], snew[:, c, 4 * h:4 * h + 4].rearrange("p b q -> p (b q)"), ident[:])
            last.then_inc(state_t_ready, 1)
            for c in range(2):
                last = pe.transpose(misc[1][0:PAIRS, c * P:(c + 1) * P], states[:, ENTRIES - N_SAMPLE - 1, c, :], ident[:])
            last.then_inc(state_t_ready, 1)

            def mix(n, r, slot, ahead):
                multiply(n, slot, D_SSM // P, ys_hi, ys_lo)

            def sum_squares():
                pe.wait_ge(pool_step, 32 + SQ_STEPS)
                for i in range(2):
                    for h, (h0, hw) in enumerate(HALVES):
                        last = pe.matmul(misc[2 * i + h][:, 0:hw], ones[:], sq[:, i, h0:h0 + hw], start=True, stop=True)
                    last.then_inc(sums_ready, 1)

            pe.wait_ge(ys_lo_done, 8)
            blocks(pe, B_GLU, 8, mix, sum_squares)

            pe.wait_ge(n_lo_done, 6)
            blocks(pe, B_QN, 8, lambda n, r, slot, ahead: multiply(n, slot, 6, qn_hi, qn_lo))
            blocks(pe, B_QR, 4, lambda n, r, slot, ahead: multiply(n, slot, 6, qn_hi, qn_lo))
            pe.wait_ge(n_lo_done, 10)
            blocks(pe, B_K, 8, lambda n, r, slot, ahead: multiply(n, slot, 4, cn_hi, cn_lo))
            pe.wait_ge(gemm_read, B_V + 2)
            pe.wait_ge(rope_loaded, 64)
            for v in range(10):
                j, t = divmod(v, 5)
                t0, rows = TILES[t]
                n = B_V + j
                if t == 0:
                    pe.wait_ge(w_lo_ready, n + 1)
                if v >= 4:
                    pe.wait_ge(v_copied, v - 3)
                acc = gemm[v % 4][0:rows, :]
                for k in range(4):
                    wh, wl = w_hi[:, n % 2, k * 512:(k + 1) * 512], w_lo[:, n % 2, k * 512:(k + 1) * 512]
                    ch, cl = cn_hi[:, k, t0:t0 + rows], cn_lo[:, k, t0:t0 + rows]
                    pe.matmul(acc, ch, wh, start=k == 0, stop=False)
                    pe.matmul(acc, ch, wl, start=False, stop=False)
                    last = pe.matmul(acc, cl, wh, start=False, stop=k == 3)
                last.then_inc(v_ready, 1)
                if v < 5:
                    if v:
                        pe.wait_ge(rope_done, v)
                    for h, (h0, hw) in enumerate(HALVES):
                        last = pe.matmul(misc[2 + h][:, 0:hw], rot[:], rp[:, v, h0:h0 + hw], start=True, stop=True)
                    last.then_inc(rotated, 1)
                else:
                    if t >= 2:
                        pe.wait_ge(c_t_copied, t - 1)
                    for k in range(4):
                        last = pe.transpose(misc[t % 2][0:rows, k * P:(k + 1) * P], latc[:, k, t0:t0 + rows], ident[:])
                    last.then_inc(c_t_ready, 1)
            pe.wait_ge(rope_done, 5)
            pe.wait_ge(c_t_copied, 5)
            for t, (t0, rows) in enumerate(TILES):
                last = pe.transpose(misc[0][0:rows, t * QK_ROPE:(t + 1) * QK_ROPE], ev[0:QK_ROPE, 0, t0:t0 + rows], ident[0:QK_ROPE, 0:QK_ROPE])
            last.then_inc(c_t_ready, 1)

            def scores(n, m, head):
                i = m % 5
                u = (m // 5) % 2
                if i == 0:
                    pe.wait_ge(head_lo_done, head * 2 + 1)
                if i == 4:
                    pe.wait_ge(o_gated, head + 1)
                if not isinstance(n, int) or n >= 3:
                    pe.wait_ge(exp_done, n - 2)
                q0, rows = i * P, (P if i < 4 else N_META)
                width = P * max(min(i + 1, 4), 2)
                parts = ((hh, hh, kp_hi), (hh, hl, kp_lo), (hl, hh, kp_hi))
                for a, (qq, kk, kp) in enumerate(parts):
                    pe.matmul(SBANK[m][0:rows, 0:width], qq[:, u, 0, q0:q0 + rows], kk[:, u, 1, 0:width], start=a == 0, stop=False)
                    last = pe.matmul(SBANK[m][0:rows, 0:width], qq[0:QK_ROPE, u, 2, q0:q0 + rows], kp[0:QK_ROPE, 0:width],
                                     start=False, stop=a == 2)
                if i == 4:
                    for a, (qq, kk, kp) in enumerate(parts):
                        pe.matmul(misc[0][0:rows, EXTRA], qq[:, u, 0, q0:q0 + rows], kk[:, u, 1, q0:q0 + rows], start=a == 0, stop=False)
                        last = pe.matmul(misc[0][0:rows, EXTRA], qq[0:QK_ROPE, u, 2, q0:q0 + rows], kp[0:QK_ROPE, q0:q0 + rows],
                                         start=False, stop=a == 2)
                last.then_inc(scores_ready, 1)

            def await_p(n, i):
                pe.wait_ge(prob_ready, n + 1)
                if i >= 2:
                    pe.wait_ge(pt_lo_done, n - 1)

            def transpose_p(n, m, waited=False):
                i = m % 5
                rows = P if i < 4 else N_META
                if not waited:
                    await_p(n, i)
                bank = misc[2 + m % 2]
                for j in range(i + 1):
                    keys = P if j < 4 else N_META
                    last = pe.transpose(bank[0:keys, j * rows:(j + 1) * rows], prob[0:rows, m % 2, j * P:j * P + keys], ident[0:rows, 0:rows])
                last.then_inc(pt_ready, 1)

            def weigh_values(h, u):
                pe.wait_ge(head_lo_done, h * 2 + 2)
                pe.wait_ge(pt_lo_done, h * 5 + 5)
                pe.wait_ge(o_gated, h + 1)
                for acc, q0, q1, tiles in ((gemm[3][:, 0:256], 0, 256, 2), (misc[0][:, 0:272], 256, T_PROMPT, 5)):
                    for j in range(tiles):
                        keys = slice(0, P if j < 4 else N_META)
                        a0 = q0 if j < 4 else 512
                        out = acc[:, a0 - q0:q1 - q0]
                        for a, (vv, pp) in enumerate(((vh, pt_hi), (vh, pt_lo), (vl, pt_hi))):
                            last = pe.matmul(out, vv[keys, u, j], pp[keys, j, a0:q1], start=j == 0 and a == 0,
                                             stop=j == tiles - 1 and a == 2)
                last.then_inc(pv_done, 1)

            pe.sem_inc(pv_done, 1)
            pe.sem_inc(pt_ready, 1)
            pe.sem_inc(ot_ready, 1)
            pe.wait_ge(kp_lo_done, 1)
            pe.wait_ge(filled, 7)
            for t in range(3):
                scores(t, t, 0)

            def head_pe(pair, u, last):
                for i in range(5):
                    m = 5 * u + i
                    if i == 4:
                        await_p(pair * 10 + m, 4)
                    if i > 0 and not (last and m >= 8):
                        scores(pair * 10 + (m + 2), (m + 2) % 10, pair * 2 + (m + 2) // 5)
                    transpose_p(pair * 10 + m, m, i == 4)
                if not (last and u == 1):
                    scores(pair * 10 + (5 * u + 7), (5 * u + 7) % 10, pair * 2 + (5 * u + 7) // 5)
                weigh_values(pair * 2 + u, u)

            head_pairs(pe, head_pe)

            pe.wait_ge(sample_loaded, 16 * 6)
            pe.wait_ge(comb_lo_done, 18)
            for h in range(N_HEADS):
                if h >= 4:
                    pe.wait_ge(wuk_t_copied, h - 3)
                for k in range(4):
                    last = pe.transpose(misc[h % 4][:, k * P:(k + 1) * P], wuk[:, k, h * P:(h + 1) * P], ident[:])
                last.then_inc(wuk_t_ready, 1)
            pe.wait_ge(wuk_t_copied, 8)
            for k in range(4):
                for h in range(N_HEADS):
                    last = pe.matmul(gemm[3][:, (k * 8 + h) * 8:(k * 8 + h + 1) * 8], wuk_t[:, h, k * P:(k + 1) * P], qs[:, h, :],
                                     start=True, stop=True)
            last.then_inc(qa_ready, 1)
            pe.wait_ge(cnt_saved, 1)
            pe.wait_ge(new_lo_done, 1)
            pe.wait_ge(wuk_t_copied, 9)

            def turn_pages(g, hg, u, half):
                if hg % 2 == 0:
                    pe.wait_ge(page_loaded[u][hg // 2], (half + 1) * 128)
                if not isinstance(g, int) or g >= 2:
                    pe.wait_ge(t_lo_done, g - 1)
                k = u * N_PAGES + 2 * hg
                for j in range(2):
                    for r in range(4):
                        pe.transpose(misc[(hg % 2) * 2 + j][:, r * P:(r + 1) * P], ckv[:, k + j, r * P:(r + 1) * P], ident[:])
                if not isinstance(g, int) or g >= 1:
                    pe.wait_ge(t_lo_done, g)
                pe.transpose(gemm[0][:, 0:P], kpe[:, k:k + 2].rearrange("p a e -> p (a e)"), ident[:]).then_inc(t_ready, 1)

            def new_scores(s):
                pe.wait_ge(q_lo_done, s + 1)
                pe.wait_ge(sc_added, s * 5)
                out = gemm[2][0:40, 0:N_SAMPLE]
                for r in range(4):
                    pe.matmul(out, q_st[:, r, :], cnt_hi[:, r, :], start=r == 0, stop=False)
                    pe.matmul(out, q_st[:, r, :], cnt_lo[:, r, :], start=False, stop=False)
                pe.matmul(out, q_st[0:QK_ROPE, 4, :], kpn_hi[0:QK_ROPE, :], start=False, stop=False)
                pe.matmul(out, q_st[0:QK_ROPE, 4, :], kpn_lo[0:QK_ROPE, :], start=False, stop=True).then_inc(sc_ready, 1)

            def page_scores(s, hg, before_last=None):
                pe.wait_ge(t_lo_done, s * 8 + (hg + 1))
                if hg % 2 == 0:
                    pe.wait_ge(sc_added, s * 5 + (hg // 2 + 1))
                c0 = hg % 2 * 256
                out = gemm[2][0:40, c0:c0 + 256]
                for r in range(4):
                    pe.matmul(out, q_st[:, r, :], ct_hi[:, hg % 2, r, :], start=r == 0, stop=False)
                    pe.matmul(out, q_st[:, r, :], ct_lo[:, hg % 2, r, :], start=False, stop=False)
                for j in range(2):
                    pe.matmul(out[:, j * P:(j + 1) * P], q_st[:, 4 + j, :], kt_hi[:, hg % 2, :], start=False, stop=False)
                    if j == 1 and before_last:
                        before_last()
                    last = pe.matmul(out[:, j * P:(j + 1) * P], q_st[:, 4 + j, :], kt_lo[:, hg % 2, :], start=False, stop=j == 1)
                if hg % 2:
                    last.then_inc(sc_ready, 1)

            def turn_weights(b, v):
                for j in range(N_PAGES):
                    pe.transpose(gemm[1][:, j * N_HEADS:(j + 1) * N_HEADS], sc[v][0:N_HEADS, j * P:(j + 1) * P], ident[0:N_HEADS, 0:N_HEADS])
                pe.transpose(gemm[1][0:N_SAMPLE, P:P + N_HEADS], sc[v][0:N_HEADS, PAST:KEYS], ident[0:N_HEADS, 0:N_HEADS]).then_inc(spt_ready, 1)

            def weigh(b, hg, before_last=None):
                pe.wait_ge(p_lo_done, b * 8 + (hg + 1))
                if hg == 0:
                    pe.wait_ge(spt_lo_done, b + 1)
                    pe.wait_ge(olat_step, b * 3)
                out = gemm[3][0:40, :]
                for j in range(2):
                    pe.matmul(out, p_t[:, 2 * hg + j, :], cp_hi[:, hg % 2, j, :], start=hg == 0 and j == 0, stop=False)
                    if j == 1 and before_last:
                        before_last()
                    last = pe.matmul(out, p_t[:, 2 * hg + j, :], cp_lo[:, hg % 2, j, :], start=False, stop=False)
                last.then_inc(pv_pair_done, 1)
                if hg == 7:
                    pe.matmul(out, p_t[0:N_SAMPLE, N_PAGES, :], cnew_hi[0:N_SAMPLE, :], start=False, stop=False)
                    pe.matmul(out, p_t[0:N_SAMPLE, N_PAGES, :], cnew_lo[0:N_SAMPLE, :], start=False, stop=True).then_inc(opv_done, 1)

            def turn_latent(b):
                for k in range(4):
                    last = pe.transpose(gemm[1][:, 256 + k * 8:256 + (k + 1) * 8], olat[0:N_HEADS, k * P:(k + 1) * P], ident[0:N_HEADS, 0:N_HEADS])
                last.then_inc(ot_ready, 1)

            def sample_pe(s, u, half):
                static = isinstance(s, int)
                run, weighs, turns = not static or s < N_SAMPLE, not static or s >= 1, not static or s >= 2

                def await_exp():
                    pe.wait_ge(sexp_done, s)
                    if turns:
                        pe.wait_ge(ot_copied, s - 1)

                if run:
                    new_scores(s)
                for hg in range(8):
                    if run and not (static and s == N_SAMPLE - 1 and hg == 7):
                        nu, nhalf = (u, half) if hg < 7 else (1 - u, half + u)
                        turn_pages(s * 8 + (hg + 1), (hg + 1) % 8, nu, nhalf)
                    if run:
                        page_scores(s, hg, await_exp if hg == 0 and weighs else None)
                    elif hg == 0:
                        await_exp()
                    if weighs:
                        if hg == 0:
                            turn_weights(s - 1, 1 - u)
                        if hg == 2 and turns:
                            weigh(s - 1, hg, lambda: (pe.wait_ge(olat_step, s * 3 - 3), pe.wait_ge(spt_lo_done, s)))
                            turn_latent(s - 2)
                        else:
                            weigh(s - 1, hg)

            turn_pages(0, 0, 0, 0)
            samples(pe, sample_pe)
            pe.wait_ge(olat_step, 3 * 8)
            turn_latent(7)

            pe.wait_ge(ot_copied, 9)
            pe.wait_ge(wuv_loaded, 16)
            for half in range(2):
                for h in range(4 * half, 4 * half + 4):
                    for k in range(4):
                        last = pe.matmul(gemm[half][0:N_SAMPLE, (h % 4) * P:(h % 4 + 1) * P], olat_t[:, k, h, :], wuv[:, k, h * P:(h + 1) * P],
                                         start=k == 0, stop=k == 3)
                last.then_inc(os_step, 1)
            pe.wait_ge(oh_copied, 2)
            for h in range(N_HEADS):
                last = pe.transpose(misc[0][:, h * 8:(h + 1) * 8], oh[0:N_SAMPLE, h * P:(h + 1) * P], ident[0:N_SAMPLE, 0:N_SAMPLE])
            last.then_inc(os_step, 1)
            pe.wait_ge(os_step, 8)

            def out_multiply(j, slot):
                pe.wait_ge(w_lo_ready, j + (B_OUT + 1))
                if not isinstance(j, int) or j >= 2:
                    pe.wait_ge(gemm_read, j + (B_V + 1))
                for h in range(2):
                    acc = gemm[2 * slot + h][:, 0:260]
                    c = slice(N_META + h * 260, N_META + (h + 1) * 260)
                    for k in range(KD):
                        a, b = w_hi[:, slot, k * P:(k + 1) * P], w_lo[:, slot, k * P:(k + 1) * P]
                        pe.matmul(acc, a, comb_hi[:, k, c], start=k == 0, stop=False)
                        pe.matmul(acc, a, comb_lo[:, k, c], start=False, stop=False)
                        last = pe.matmul(acc, b, comb_hi[:, k, c], start=False, stop=k == KD - 1)
                last.then_inc(gemm_done, 1)

            def out_turn(j, slot):
                pe.wait_ge(gemm_read, j + (B_V + 3))
                pe.wait_ge(out_added, j + 1)
                for t in range(4):
                    pe.transpose(misc[slot][:, t * P:(t + 1) * P], yb[:, slot, t * P:(t + 1) * P], ident[:])
                pe.transpose(misc[2 + slot][0:N_SAMPLE, 0:P], yb[:, slot, SEQ:SEQ + N_SAMPLE], ident[:]).then_inc(out_t_ready, 1)

            pe.sem_inc(out_t_ready, 2)
            out_multiply(0, 0)
            with pe.Fori(0, 7) as i:
                for u in range(2):
                    out_multiply(i * 2 + (1 + u), 1 - u)
                    out_turn(i * 2 + u, u)
            out_multiply(15, 1)
            out_turn(14, 0)
            out_turn(15, 1)


OUTPUTS = (
    ("o_y_p", (1, SEQ, D_MODEL)), ("o_y_s", (N_SAMPLE, 1, D_MODEL)),
    ("o_ckv_p", (1, 1, T_PROMPT, KV_LORA)), ("o_kpe_p", (1, 1, T_PROMPT, QK_ROPE)),
    ("o_ssm_re_p", (1, 1, N_GROUPS, N_STATE)), ("o_ssm_im_p", (1, 1, N_GROUPS, N_STATE)),
    ("o_ckv_s", (1, N_SAMPLE, 1, KV_LORA)), ("o_kpe_s", (1, N_SAMPLE, 1, QK_ROPE)),
    ("o_ssm_re_s", (1, N_SAMPLE, N_GROUPS, N_STATE)), ("o_ssm_im_s", (1, N_SAMPLE, N_GROUPS, N_STATE)),
)
SCRATCH = (
    ("lat_d", (Q_LORA + KV_LORA + P, T)),
    ("u_d", (D_SSM, T)), ("z_d", (2 * D_SSM, T)),
    ("q_d", (N_HEADS * QK_NOPE, T)), ("k_d", (N_HEADS * QK_NOPE, T)), ("v_d", (T, N_HEADS * V_HEAD)),
    ("qp_d", (N_HEADS * QK_ROPE + P, T)),
)


def rope_tables():
    half = QK_ROPE // 2
    inv = (ROPE_THETA ** (-np.arange(half) / half)).astype(np.float32)
    pos = np.concatenate([np.arange(T_PROMPT), np.full(N_SAMPLE, PAST)]).astype(np.float32)
    angle = (inv[:, None] * pos[None, :]).astype(np.float64)
    cos, sin = np.cos(angle).astype(np.float32), np.sin(angle).astype(np.float32)
    return np.concatenate([cos] * 4), np.concatenate([-sin, sin] * 2)


def kernel(**inputs):
    import concourse.bacc as bacc
    from concourse.bass_utils import run_bass_kernel_spmd

    nc = bacc.Bacc("TRN2", target_bir_lowering=False, num_devices=1)
    cos, sin = rope_tables()
    arrays = {name: np.ascontiguousarray(a) for name, a in inputs.items()}
    arrays.update(rope_cos=cos, rope_sin=sin)
    d = {name: nc.dram_tensor(name, a.shape, mybir.dt.from_np(a.dtype), kind="ExternalInput").ap() for name, a in arrays.items()}
    for name, shape in OUTPUTS:
        d[name] = nc.dram_tensor(name, shape, F32, kind="ExternalOutput").ap()
    for name, shape in SCRATCH:
        d[name] = nc.dram_tensor(name, shape, F32).ap()
    build(nc, d)
    r = run_bass_kernel_spmd(nc, [arrays], core_ids=[0])
    return tuple(r.results[0][name] for name, _ in OUTPUTS)
```

```python
import math
from contextlib import ExitStack

import numpy as np

import concourse.bass as bass
from concourse import mybir

F32 = mybir.dt.float32
F32R = mybir.dt.float32r
ALU = mybir.AluOpType
ACT = mybir.ActivationFunctionType
AX = mybir.AxisListType
ds = bass.ds

P = 128
D_MODEL, SEQ, N_META, N_SAMPLE = 2048, 512, 16, 8
D_SSM, GROUP, N_STATE = 1024, 16, 64
N_GROUPS = D_SSM // GROUP
N_HEADS, V_HEAD, QK_NOPE, QK_ROPE = 8, 128, 128, 64
KV_LORA, Q_LORA = 512, 768
PAGE, PAST = 128, 2048
N_PAGES = PAST // PAGE
ROPE_THETA = 10000.0
EPS = 1e-6
SCALE = (QK_NOPE + QK_ROPE) ** -0.5
NEG = -1.0e30

T_PROMPT = N_META + SEQ
T = T_PROMPT + N_SAMPLE
HALVES = ((0, 264), (264, 272))
TILES = tuple((t, min(P, T - t)) for t in range(0, T, P))
KD = D_MODEL // P
CHUNK = P // GROUP
N_CHUNK = T_PROMPT // CHUNK
YCOLS = N_SAMPLE + N_CHUNK
PAIRS = N_GROUPS // 2
ENTRIES = N_SAMPLE + 1 + N_CHUNK + N_SAMPLE
COL_ZS, COL_LAT = D_SSM, 2 * D_SSM
COL_ZA = 2 * D_SSM + Q_LORA + KV_LORA + QK_ROPE

B_LAT, B_U, B_ZS, B_ZA, B_GLU, B_QN, B_QR, B_K, B_V, B_OUT, B_END = 0, 11, 19, 27, 35, 43, 51, 55, 63, 65, 81




def block_width(n):
    if n < B_GLU:
        return KD * P
    if n < B_QN:
        return D_SSM
    if n < B_K:
        return Q_LORA
    if n < B_V:
        return KV_LORA
    return KV_LORA // P * 512 if n < B_OUT else KD * P


def build(nc, d):
    es = ExitStack()
    base = 16512

    def at(name, offset, shape, dt=F32):
        assert base + offset + math.prod(shape[1:]) * 4 <= 229344, name
        return nc.alloc_sbuf_tensor_at(name, shape, dt, offset=base + offset)

    with es:
        def sem(name):
            return es.enter_context(nc.semaphore(name))

        ROW = T * 4
        xh = at("xh", 0, [P, KD, T], F32R)
        xl = at("xl", KD * ROW, [P, KD, T], F32R)
        o = 2 * KD * ROW
        w_raw = at("w_raw", o, [P, 2, 2048])
        w_hi = at("w_hi", o + 16384, [P, 2, 2048], F32R)
        w_lo = at("w_lo", o + 32768, [P, 2, 2048], F32R)
        W_AREA = o
        o += 49152
        ident = at("ident", o, [P, P])
        ones = at("ones", o + 512, [P, P])
        causal = at("causal", o + 1024, [P, P])
        rot = at("rot", o + 1536, [P, P])
        vecs = at("vecs", o + 2048, [P, 64])
        stat = at("stat", o + 2304, [P, 64])
        o += 4096
        ev = at("ev", o, [P, 2, T])
        o += 2 * ROW
        A0 = o

        xtok = at("xtok", A0, [P, 5, D_MODEL])
        gbc = at("gbc", A0 + 40960, [P, D_MODEL])
        junk = at("junk", A0 + 49152, [P, D_MODEL])
        states = at("states", A0, [P, ENTRIES, 2, PAIRS])
        XA = A0 + ENTRIES * 256
        xgrp = at("xgrp", XA, [P, N_GROUPS, 82])
        o = XA + N_GROUPS * 82 * 4
        tmp = at("tmp", o, [P, 4, 512])
        o += 8192
        wst = at("wst", o, [P, 2, 2, 4, CHUNK, GROUP])
        bst = at("bst", o + 8192, [P, 2, 4, P])
        kall = at("kall", o + 12288, [P, D_SSM])
        cast = at("cast", o, [P, 2, 2, 4, 2, CHUNK, GROUP])
        o += 16384
        powers = at("powers", o, [P, 2, 9, PAIRS])
        coef = at("coef", o + 2304, [P, 24, PAIRS])
        bbar = at("bbar", o + 5376, [P, 2, PAIRS, GROUP])
        cbd = at("cbd", o + 9472, [P, 2, PAIRS, 2, GROUP])
        snew = at("snew", o + 17664, [P, 2, N_SAMPLE, PAIRS])
        o += 17664 + 2048
        anat = at("anat", A0 + 57344, [P, 3, P])
        snat = at("snat", A0 + 58880, [P, 2, 2, P])
        cnat = at("cnat", A0 + 60928, [P, 4, 2, P])
        vnat = at("vnat", A0 + 65024, [P, P])
        ldt = at("ldt", A0 + 65536, [P, 2])
        ychunk = at("ychunk", 0, [P, 2, CHUNK, P])
        ug = at("ug", 8192, [P, 2, T])
        yg = at("yg", 8192 + 2 * ROW, [P, 2, T])
        ys = at("ys", 8 * ROW, [P, 8, T])
        ys_hi = at("ys_hi", A0, [P, 8, T], F32R)
        ys_lo = at("ys_lo", A0 + 8 * ROW, [P, 8, T], F32R)
        ptmp = at("ptmp", 2 * KD * ROW + 49152 + 4096, [P, 4, 256])
        gate = at("gate", A0 + 16 * ROW, [P, 2, T])
        sig = at("sig", A0 + 18 * ROW, [P, 2, T])
        comb_hi, comb_lo = xh, xl
        sout = at("sout", A0 + 20 * ROW, [P, 6, P])
        A1 = A0 + 46592
        latq = at("latq", A1, [P, 6, T])
        latc = at("latc", A1 + 6 * ROW, [P, 4, T])
        sq = at("sq", A1 + 10 * ROW, [P, 2, T])
        rs = at("rs", A1 + 12 * ROW, [P, 2, T])
        vout = at("vout", A1 + 14 * ROW, [P, 2, 512])
        cos = at("cos", A1 + 14 * ROW + 4096, [P, T])
        sin = at("sin", A1 + 15 * ROW + 4096, [P, T])
        rp = at("rp", A1, [P, 5, T])
        cout = at("cout", A1 + 10 * ROW, [P, 2, KV_LORA])
        kout = at("kout", A0 + 42880, [P, 5, QK_ROPE])
        qn_hi = at("qn_hi", A0, [P, 6, T], F32R)
        qn_lo = at("qn_lo", A0 + 6 * ROW, [P, 6, T], F32R)
        cn_hi = at("cn_hi", A0 + 12 * ROW, [P, 4, T], F32R)
        cn_lo = at("cn_lo", A0 + 16 * ROW, [P, 4, T], F32R)
        hraw = at("hraw", A0, [P, 2, 3, T])
        hh = at("hh", A0 + 6 * ROW, [P, 2, 3, T], F32R)
        hl = at("hl", A0 + 12 * ROW, [P, 2, 3, T], F32R)
        kp_hi = at("kp_hi", A0 + 18 * ROW, [P, T], F32R)
        kp_lo = at("kp_lo", A0 + 19 * ROW, [P, T], F32R)
        o = A0 + 20 * ROW
        vraw = at("vraw", o, [P, 2, 5, V_HEAD])
        vh = at("vh", o + 5120, [P, 2, 5, V_HEAD], F32R)
        vl = at("vl", o + 10240, [P, 2, 5, V_HEAD], F32R)
        pt_hi = at("pt_hi", o + 15360, [P, 5, T_PROMPT], F32R)
        pt_lo = at("pt_lo", o + 15360 + 5 * T_PROMPT * 4, [P, 5, T_PROMPT], F32R)
        za = at("za", W_AREA, [P, 2, T])
        otmp = at("otmp", W_AREA + 2 * ROW, [P, T])
        prob = at("prob", W_AREA + 3 * ROW, [P, 4, T_PROMPT])
        kp_raw = at("kp_raw", W_AREA + 3 * ROW + 3 * T_PROMPT * 4, [P, T])
        ckv = at("ckv", A0, [P, 2 * N_PAGES, KV_LORA])
        kpe = at("kpe", A0 + 65536, [P, 2 * N_PAGES, QK_ROPE])
        KEYS = PAST + N_SAMPLE
        sc = [at("sc0", A0 + 73728, [P, KEYS]), at("sc1", W_AREA + 40704, [P, KEYS])]
        kt_hi = at("kt_hi", A0 + 81952, [P, 2, P], F32R)
        kt_lo = at("kt_lo", A0 + 82976, [P, 2, P], F32R)
        half2 = at("half2", A0 + 84000, [P, 512])
        ct_hi = at("ct_hi", W_AREA, [P, 2, 4, 2 * P], F32R)
        ct_lo = at("ct_lo", W_AREA + 8192, [P, 2, 4, 2 * P], F32R)
        cp_hi = at("cp_hi", W_AREA + 16384, [P, 2, 2, KV_LORA], F32R)
        cp_lo = at("cp_lo", W_AREA + 24576, [P, 2, 2, KV_LORA], F32R)
        wuk = at("wuk", W_AREA + 16384, [P, 4, N_HEADS * QK_NOPE])
        wuk_t = at("wuk_t", W_AREA, [P, N_HEADS, KV_LORA])
        cnew_hi = at("cnew_hi", W_AREA + 32768, [P, KV_LORA], F32R)
        cnew_lo = at("cnew_lo", W_AREA + 34816, [P, KV_LORA], F32R)
        olat = at("olat", W_AREA + 36864, [P, KV_LORA])
        olat_t = at("olat_t", W_AREA + 38912, [P, 4, N_HEADS, N_SAMPLE])
        qs = at("qs", W_AREA + 39936, [P, N_HEADS, N_SAMPLE])
        qps = at("qps", W_AREA + 40192, [P, N_HEADS, N_SAMPLE])
        kpn_raw = at("kpn_raw", W_AREA + 40448, [P, N_SAMPLE])
        EV0 = 2 * KD * ROW + 49152 + 4096
        p_t = at("p_t", EV0, [P, N_PAGES + 1, 40], F32R)
        qa = at("qa", EV0 + 2720, [P, 6, N_SAMPLE, N_HEADS])
        C0 = 2 * KD * ROW + 49152
        ptab = nc.alloc_sbuf_tensor_at("ptab", [1, N_SAMPLE * N_PAGES], mybir.dt.int32, offset=base + C0 + 1536)
        q_st = [at("q_st0", C0 + 2560, [P, 6, 40], F32R), at("q_st1", C0 + 512, [P, 6, 40], F32R)]
        cnt_hi = at("cnt_hi", C0 + 3520, [P, 4, N_SAMPLE], F32R)
        cnt_lo = at("cnt_lo", C0 + 3648, [P, 4, N_SAMPLE], F32R)
        not_own = at("not_own", C0 + 3776, [N_SAMPLE, N_SAMPLE, N_SAMPLE])
        kpn_hi = at("kpn_hi", C0 + 4032, [P, N_SAMPLE], F32R)
        kpn_lo = at("kpn_lo", C0 + 4064, [P, N_SAMPLE], F32R)
        wuv = at("wuv", A0, [P, 4, N_HEADS * V_HEAD])
        yt = at("yt", A0 + 16384, [P, 4, D_MODEL])
        ysm = at("ysm", A0 + 49152, [P, D_MODEL])
        gfin = at("gfin", A0 + 57344, [P, D_MODEL])
        yb = at("yb", A0 + 65536, [P, 2, SEQ + N_SAMPLE])
        junk2 = at("junk2", A0 + 69696, [P, D_MODEL])
        oh = at("oh", A0 + 77888, [P, N_HEADS * V_HEAD])
        zas = at("zas", A0 + 81984, [P, N_HEADS, N_SAMPLE])
        oz = at("oz", A0 + 82240, [P, N_HEADS, N_SAMPLE])
        toep = at("toep", KD * ROW, [P, CHUNK, D_SSM])

        def psum(name):
            return es.enter_context(nc.psum_tensor(name, [P, 512], F32))

        gemm = [psum(f"gemm{i}") for i in range(4)]
        misc = [psum(f"misc{i}") for i in range(4)]

        x_loaded = [sem(f"x_loaded{t}") for t in range(5)]
        g_loaded = sem("g_loaded")
        prep_loaded = sem("prep_loaded")
        cnat_loaded = sem("cnat_loaded")
        filled = sem("filled")
        const_ready = sem("const_ready")
        x_squared = sem("x_squared")
        var_ready = sem("var_ready")
        std_ready = sem("std_ready")
        rstd_ready = sem("rstd_ready")
        x_scaled = sem("x_scaled")
        xt_ready = sem("xt_ready")
        xh_done = sem("xh_done")
        xl_done = sem("xl_done")
        w_loaded = [sem("w_loaded0"), sem("w_loaded1")]
        w_hi_ready = sem("w_hi_ready")
        w_lo_ready = sem("w_lo_ready")
        gemm_done = sem("gemm_done")
        gemm_read = sem("gemm_read")
        ev_stored = [sem("ev_stored0"), sem("ev_stored1")]
        ldt_spread = sem("ldt_spread")
        prep_t_ready = sem("prep_t_ready")
        prep_t_read = sem("prep_t_read")
        dve_step = sem("dve_step")
        dt_ready = sem("dt_ready")
        mag_ready = sem("mag_ready")
        angle_ready = sem("angle_ready")
        sin_ready = sem("sin_ready")
        coef_ready = sem("coef_ready")
        xgrp_loaded = sem("xgrp_loaded")
        wst_built = sem("wst_built")
        mul_done = sem("mul_done")
        bt_ready = sem("bt_ready")
        k_ready = sem("k_ready")
        bt_re_copied = sem("bt_re_copied")
        bt_im_copied = sem("bt_im_copied")
        k_copied = sem("k_copied")
        s_ready = sem("s_ready")
        s_re_copied = sem("s_re_copied")
        s_im_copied = sem("s_im_copied")
        scan_step = sem("scan_step")
        sample_step = sem("sample_step")
        toep_loaded = [sem("toep_loaded0"), sem("toep_loaded1")]
        ca_built = sem("ca_built")
        ca_built_pool = sem("ca_built_pool")
        pool_step = sem("pool_step")
        y_ready = sem("y_ready")
        y_copied = sem("y_copied")
        yt_ready = sem("yt_ready")
        yt_added = sem("yt_added")
        ug_loaded = [sem("ug_loaded0"), sem("ug_loaded1")]
        gelu_done = sem("gelu_done")
        ys_hi_done = sem("ys_hi_done")
        ys_lo_done = sem("ys_lo_done")
        state_t_ready = sem("state_t_ready")
        state_copied = sem("state_copied")
        state_stored = sem("state_stored")
        gate_loaded = [sem("gate_loaded0"), sem("gate_loaded1")]
        sig_done = sem("sig_done")
        gated = sem("gated")
        lat_loaded = sem("lat_loaded")
        rope_loaded = sem("rope_loaded")
        sums_ready = sem("sums_ready")
        squared = sem("squared")
        c_scaled = sem("c_scaled")
        normed = sem("normed")
        n_hi_done = sem("n_hi_done")
        n_lo_done = sem("n_lo_done")
        c_t_ready = sem("c_t_ready")
        c_t_copied = sem("c_t_copied")
        c_stored = [sem("c_stored0"), sem("c_stored1")]
        rotated = sem("rotated")
        rope_step = sem("rope_step")
        rope_done = sem("rope_done")
        kpe_copied = sem("kpe_copied")
        kpe_stored = sem("kpe_stored")
        v_ready = sem("v_ready")
        v_copied = sem("v_copied")
        v_stored = [sem("v_stored0"), sem("v_stored1")]
        kp_loaded = sem("kp_loaded")
        kp_hi_done = sem("kp_hi_done")
        kp_lo_done = sem("kp_lo_done")
        v_loaded = [sem("v_loaded0"), sem("v_loaded1")]
        head_loaded = [sem("head_loaded0"), sem("head_loaded1")]
        head_hi_done = sem("head_hi_done")
        head_lo_done = sem("head_lo_done")
        scores_ready = sem("scores_ready")
        max_ready = sem("max_ready")
        max_step = sem("max_step")
        sum_step = sem("sum_step")
        exp_done = sem("exp_done")
        prob_ready = sem("prob_ready")
        pt_ready = sem("pt_ready")
        pt_hi_done = sem("pt_hi_done")
        pt_lo_done = sem("pt_lo_done")
        pv_done = sem("pv_done")
        o_gated = sem("o_gated")
        cnt_saved = sem("cnt_saved")
        table_loaded = sem("table_loaded")
        page_loaded = [[sem(f"page_loaded{u}{g}") for g in range(4)] for u in range(2)]
        sample_loaded = sem("sample_loaded")
        wuk_t_ready = sem("wuk_t_ready")
        wuk_t_copied = sem("wuk_t_copied")
        qa_ready = sem("qa_ready")
        new_hi_done = sem("new_hi_done")
        new_lo_done = sem("new_lo_done")
        q_hi_done = sem("q_hi_done")
        q_lo_done = sem("q_lo_done")
        t_ready = sem("t_ready")
        t_hi_done = sem("t_hi_done")
        t_lo_done = sem("t_lo_done")
        p_hi_done = sem("p_hi_done")
        p_lo_done = sem("p_lo_done")
        pv_pair_done = sem("pv_pair_done")
        sc_ready = sem("sc_ready")
        half_copied = sem("half_copied")
        sc_added = sem("sc_added")
        sc_step = sem("sc_step")
        smax_ready = sem("smax_ready")
        sexp_done = sem("sexp_done")
        spt_ready = sem("spt_ready")
        spt_hi_done = sem("spt_hi_done")
        spt_lo_done = sem("spt_lo_done")
        opv_done = sem("opv_done")
        ohalf_copied = sem("ohalf_copied")
        olat_step = sem("olat_step")
        ot_ready = sem("ot_ready")
        ot_copied = sem("ot_copied")
        wuv_loaded = sem("wuv_loaded")
        os_step = sem("os_step")
        oh_copied = sem("oh_copied")
        res_loaded = sem("res_loaded")
        out_t_ready = sem("out_t_ready")
        out_added = sem("out_added")
        y_stored = sem("y_stored")
        comb_hi_done = sem("comb_hi_done")
        comb_lo_done = sem("comb_lo_done")

        lat_d, u_d, z_d = d["lat_d"], d["u_d"], d["z_d"]
        w_in = d["w_in"].rearrange("l (k p) n -> p (l k) n", p=P)
        w_glu = d["w_glu"].rearrange("l (k p) n -> p (l k) n", p=P)
        w_uq = d["w_uq"].rearrange("l (k p) n -> p (l k) n", p=P)
        w_uk = d["w_uk"].rearrange("l (k p) h n -> p (l k) (h n)", p=P)
        w_uv = d["w_uv"].rearrange("l (k p) h n -> p (l k) (h n)", p=P)
        q_d, qp_d, k_d, v_d = d["q_d"], d["qp_d"], d["k_d"], d["v_d"]
        x_prompt = d["x_prompt"].rearrange("b s m -> (b s) m")
        x_sample = d["x_sample"].rearrange("b s m -> (b s) m")

        def blocks(eng, first, count, body, between=None):
            alike = block_width(first + count) == block_width(first) and first + count not in (B_QR, B_OUT, B_END)
            looped = (count if alike else count - 2) // 2
            with eng.Fori(0, looped) as i:
                for n in (first, first + 1):
                    body(i * 2 + n, i + n // 2, n % 2, first)
            if between is not None:
                between()
            for n in range(first + 2 * looped, first + count):
                body(n, n // 2, n % 2, n + 2 if n + 2 < B_OUT or B_OUT <= n < B_END - 2 else None)

        def with_first_pass(eng, body, first_pass):
            for n in (B_ZS, B_ZS + 1):
                body(n, n // 2, n % 2, B_ZS)
            with eng.Fori(0, 3) as i:
                for u in range(2):
                    n = B_ZS + 2 + u
                    first_pass(i * 2 + u)
                    body(i * 2 + n, i + n // 2, n % 2, B_ZS)
            for b in (6, 7):
                first_pass(b)

        def glu_blocks(eng, body, norms):
            with eng.Fori(0, 2) as i:
                for n in (B_GLU, B_GLU + 1):
                    body(i * 2 + n, i + n // 2, n % 2, B_GLU)
            norms()
            for n in range(B_GLU + 4, B_GLU + 8):
                body(n, n // 2, n % 2, B_GLU if n < B_GLU + 6 else n + 2)

        bias_glu = vecs[:, 10:18]
        EV_STORES = (18 + 4 + 4, 17 + 4 + 4)
        SQ_STEPS = 5 + 3
        NORM_OUT = (d["o_ckv_p"].rearrange("l b t r -> (l b t) r"), d["o_ckv_s"].rearrange("l b t r -> (l b t) r"))
        KPE_OUT = (d["o_kpe_p"].rearrange("l b t r -> (l b t) r"), d["o_kpe_s"].rearrange("l b t r -> (l b t) r"))

        def gate_count(n, r, slot):
            return (r - (B_GLU + 1 - slot) // 2 + 1) * 16 if slot == 0 else (r - B_GLU // 2 + 1) * 16

        SLOT = (0, 1, 2, 0, 1, 2, 0, 1, 2, 3)
        SBANK = [(gemm[0], gemm[1], gemm[2], misc[1])[k] for k in SLOT]
        EXTRA = slice(272, 288)
        N_TILES = 5 * N_HEADS

        def query_tiles(eng, step):
            for n in range(2):
                step(n, 0, n)
            with eng.Fori(0, N_HEADS // 2 - 1) as i:
                for k in range(2, 12):
                    step(i * 10 + k, i, k)
            for k in range(2, 12):
                step(N_TILES - 10 + k, N_HEADS // 2 - 1, k)

        def exists(n):
            return not isinstance(n, int) or 0 <= n < N_TILES

        def samples(eng, step):
            step(0, 0, 0)
            step(1, 1, 0)
            with eng.Fori(0, N_SAMPLE // 2 - 2) as i:
                for u in range(2):
                    step(i * 2 + (2 + u), u, i + 1)
            for s in range(N_SAMPLE - 2, N_SAMPLE + 1):
                step(s, s % 2, s // 2)

        block = es.enter_context(nc.Block())

        @block.sync
        def _(sp):
            for t, (t0, rows) in enumerate(TILES):
                if t == 0:
                    sp.dma_start(xtok[0:N_META, 0, :], d["meta_tokens"]).then_inc(x_loaded[0], 16)
                    sp.dma_start(xtok[N_META:P, 0, :], x_prompt[0:P - N_META, :]).then_inc(x_loaded[0], 16)
                elif t < 4:
                    if t == 2:
                        sp.dma_start(gbc[:], d["g_norm"].partition_broadcast(P).rearrange("p l m -> p (l m)")).then_inc(g_loaded, 16)
                    sp.dma_start(xtok[:, t, :], x_prompt[t0 - N_META:t0 - N_META + P, :]).then_inc(x_loaded[t], 16)
                else:
                    sp.dma_start(xtok[0:N_META, t, :], x_prompt[t0 - N_META:SEQ, :]).then_inc(x_loaded[t], 16)
                    sp.dma_start(xtok[N_META:rows, t, :], x_sample).then_inc(x_loaded[t], 16)

            def load(n, slot, col):
                sp.dma_start(w_raw[:, slot, :].rearrange("p (k n) -> p k n", k=KD),
                             w_in[:, :, ds(col, P)]).then_inc(w_loaded[slot], 16)

            for n in range(2):
                load(n, n, COL_LAT + n * P)

            sp.dma_start(anat[0:PAIRS, 0, :], d["ssm_a_re"].rearrange("l (q t) n -> (l q) (t n)", t=2)).then_inc(prep_loaded, 16)
            sp.dma_start(anat[0:PAIRS, 1, :], d["ssm_a_im"].rearrange("l (q t) n -> (l q) (t n)", t=2)).then_inc(prep_loaded, 16)
            sp.dma_start(ldt[0:PAIRS, :], d["ssm_log_dt"].rearrange("l (q t) -> (l q) t", t=2)).then_inc(prep_loaded, 16)
            for c, s in enumerate((d["state_ssm_re"], d["state_ssm_im"])):
                rows = s.rearrange("l b (q t) n -> (l b q) (t n)", t=2)
                for h in range(2):
                    sp.dma_start(snat[:, h, c, :], rows[h * P:(h + 1) * P, :]).then_inc(prep_loaded, 16)
            for c, b in enumerate((d["ssm_b_re"], d["ssm_b_im"])):
                sp.dma_start(bbar[:, c], b.rearrange("l (q t) n c -> (l t n) q c", t=2)).then_inc(prep_loaded, 16)
            row = 0
            for v in (d["g_q_norm"], d["g_kv_norm"], d["b_glu"], d["ssm_d"]):
                v = v.rearrange("l (k p) -> (l k) p", p=P)
                sp.dma_start(vnat[row:row + v.shape[0], :], v).then_inc(prep_loaded, 16)
                row += v.shape[0]
            for c, cc in enumerate((d["ssm_c_re"], d["ssm_c_im"])):
                v = cc.rearrange("l (b q t) c n -> t (l b) q c n", b=4, t=2)
                for b in range(4):
                    for t in range(2):
                        sp.dma_start(cnat[:, b, c, t * N_STATE:(t + 1) * N_STATE],
                                      v[t, b]).then_inc(cnat_loaded, 16)

            def run(first, count, col):
                with sp.Fori(0, count // 2) as i:
                    for u in range(2):
                        sp.wait_ge(w_lo_ready, i * 2 + (first + u - 1))
                        load(None, (first + u) % 2, i * (2 * P) + (col + u * P))
                if count % 2:
                    n = first + count - 1
                    sp.wait_ge(w_lo_ready, n - 1)
                    load(n, n % 2, col + (count - 1) * P)

            run(2, B_U - 2, COL_LAT + 2 * P)
            run(B_U, 8, 0)
            run(B_ZS, 8, COL_ZS)
            run(B_ZA, 8, COL_ZA)

            def load_glu(n, slot, col):
                sp.dma_start(w_raw[:, slot, 0:D_SSM].rearrange("p (k n) -> p k n", k=8),
                             w_glu[:, :, ds(col, P)]).then_inc(w_loaded[slot], 16)

            for n in (B_GLU, B_GLU + 1):
                sp.wait_ge(w_lo_ready, n - 1)
                load_glu(n, n % 2, (n - B_GLU) * P)
            sp.wait_ge(coef_ready, 5)
            sp.wait_ge(k_copied, 9)
            for h in range(2):
                cols = slice(h * (D_SSM // 2), (h + 1) * (D_SSM // 2))
                for i in range(CHUNK):
                    sp.dma_start(toep[(CHUNK - 1 - i) * GROUP:P, i, cols], kall[0:(i + 1) * GROUP, cols]).then_inc(toep_loaded[h], 16)
            for b in range(8):
                if b >= 2:
                    sp.wait_ge(yt_added, 2 * (b - 1))
                sp.dma_start(ug[:, b % 2, :], u_d[b * P:(b + 1) * P, :]).then_inc(ug_loaded[b % 2], 16)
            sp.wait_ge(y_ready, 16)

            def load_gate(n, slot):
                sp.dma_start(gate[:, slot, :], z_d[ds((n - B_GLU) * P, P), :]).then_inc(gate_loaded[slot], 16)
            load_gate(B_GLU, B_GLU % 2)
            load_gate(B_GLU + 1, (B_GLU + 1) % 2)

            def next_glu(k, ku):
                sp.wait_ge(w_lo_ready, k + (B_GLU + 2))
                load_glu(None, (B_GLU + 3 + ku) % 2, k * P + 3 * P)

            def next_gate(k, ku):
                sp.wait_ge(comb_lo_done, k + 3)
                load_gate(k + (B_GLU + 2), (B_GLU + ku) % 2)

            next_glu(-1, -1)
            with sp.Fori(0, 2) as i:
                for u in range(2):
                    next_glu(i * 2 + u, u)
                    next_gate(i * 2 + u, u)
            def load_w(n, slot, src, width):
                sp.dma_start(w_raw[:, slot, 0:width].rearrange("p (k n) -> p k n", k=src.shape[1]), src).then_inc(w_loaded[slot], 16)

            HD = QK_NOPE + QK_ROPE

            def load_qn(k, u):
                sp.wait_ge(w_lo_ready, k + (B_QN - 1))
                load_w(None, (B_QN + u) % 2, w_uq[:, :, ds(k * HD, P)], Q_LORA)

            next_glu(4, 4)
            load_qn(0, 0)
            next_gate(4, 4)
            load_qn(1, 1)
            next_gate(5, 5)
            with sp.Fori(0, 3) as i:
                for u in range(2):
                    load_qn(i * 2 + (2 + u), u)
            sp.wait_ge(state_copied, 6)
            for c, o_d in enumerate((d["o_ssm_re_s"], d["o_ssm_im_s"])):
                rows = o_d.rearrange("l b (q t) n -> (l b q) (t n)", t=2)
                for h in range(2):
                    sp.dma_start(rows[h * P:(h + 1) * P, :], sout[:, 2 * h + c, :]).then_inc(state_stored, 16)
            for c, o_d in enumerate((d["o_ssm_re_p"], d["o_ssm_im_p"])):
                sp.dma_start(o_d.rearrange("l b (q t) n -> (l b q) (t n)", t=2), sout[0:PAIRS, 4 + c, :]).then_inc(state_stored, 16)
            with sp.Fori(0, 2) as i:
                for u in range(2):
                    sp.wait_ge(w_lo_ready, i * 2 + (B_QR + u - 1))
                    slot = (B_QR + u) % 2
                    dst = w_raw[:, slot, 0:Q_LORA].rearrange("p (k n) -> p k n", k=Q_LORA // P)
                    for t in range(2):
                        c0 = i * (4 * HD) + ((2 * u + t) * HD + QK_NOPE)
                        sp.dma_start(dst[:, :, t * QK_ROPE:(t + 1) * QK_ROPE], w_uq[:, :, ds(c0, QK_ROPE)]).then_inc(w_loaded[slot], 16)
            with sp.Fori(0, 4) as i:
                for u in range(2):
                    sp.wait_ge(w_lo_ready, i * 2 + (B_K + u - 1))
                    load_w(None, (B_K + u) % 2, w_uk[:, :, ds(i * (2 * P) + u * P, P)], KV_LORA)
            for u in range(2):
                sp.wait_ge(w_lo_ready, B_V + u - 1)
                load_w(None, (B_V + u) % 2, w_uv[:, :, u * 512:(u + 1) * 512], 2048)
            sp.wait_ge(state_stored, 16 * 6)
            def load_qk(h, slot):
                sp.dma_start(hraw[:, slot, 0, :], q_d[ds(h * P, P), :]).then_inc(head_loaded[slot], 16)
                sp.dma_start(hraw[:, slot, 1, :], k_d[ds(h * P, P), :]).then_inc(head_loaded[slot], 16)

            def load_qp(h, slot):
                sp.dma_start(hraw[0:QK_ROPE, slot, 2, :], qp_d[ds(h * QK_ROPE, QK_ROPE), :]).then_inc(head_loaded[slot], 16)

            def load_v(h, slot):
                sp.dma_start(vraw[:, slot, 0:4, :], v_d[0:SEQ, ds(h * V_HEAD, V_HEAD)].rearrange("(t p) c -> p t c", p=P)
                             ).then_inc(v_loaded[slot], 16)
                sp.dma_start(vraw[0:N_META, slot, 4, :], v_d[SEQ:T_PROMPT, ds(h * V_HEAD, V_HEAD)]).then_inc(v_loaded[slot], 16)

            def load_za(h, slot):
                sp.dma_start(za[:, slot, :], z_d[ds(h * P + D_SSM, P), :]).then_inc(ug_loaded[slot], 16)

            sp.wait_ge(gemm_done, B_V)
            for u in range(2):
                sp.wait_ge(ev_stored[u], 16 * (1 + EV_STORES[u]))
            for u in range(2):
                load_qk(u, u)
            for u in range(2):
                sp.wait_ge(ev_stored[u], 16 * (1 + EV_STORES[u] + 3 - u))
            sp.wait_ge(w_lo_ready, B_V + 2)
            sp.dma_start(kp_raw[0:QK_ROPE, :], qp_d[4 * P:4 * P + QK_ROPE, :]).then_inc(kp_loaded, 16)
            for u in range(2):
                load_qp(u, u)
            for u in range(2):
                sp.wait_ge(v_stored[u], 16 * 5)
            sp.wait_ge(kpe_stored, 16 * 3)
            for u in range(2):
                load_v(u, u)
                load_za(u, u)
            for u in range(2):
                sp.wait_ge(c_stored[u], 16 * (4 - 2 * u))
            sp.wait_ge(rotated, 5)
            sp.dma_start(ptab[:], d["page_table"].rearrange("b j -> (b j)").unsqueeze(0)).then_inc(table_loaded, 16)
            sp.dma_start(wuk[:], w_uk).then_inc(sample_loaded, 16)
            sp.dma_start(qs[:], q_d.rearrange("(h e) t -> e h t", e=QK_NOPE)[:, :, T_PROMPT:T]).then_inc(sample_loaded, 16)
            for half in range(2):
                sp.dma_start(qps[half * QK_ROPE:(half + 1) * QK_ROPE],
                             qp_d[0:4 * P, :].rearrange("(h e) t -> e h t", e=QK_ROPE)[:, :, T_PROMPT:T]).then_inc(sample_loaded, 16)
            sp.dma_start(kpn_raw[0:QK_ROPE], qp_d[4 * P:4 * P + QK_ROPE, T_PROMPT:T]).then_inc(sample_loaded, 16)
            sp.dma_start(half2[0:N_SAMPLE], NORM_OUT[1]).then_inc(sample_loaded, 16)
            with sp.Fori(0, N_HEADS // 2 - 1) as i:
                for u in range(2):
                    sp.wait_ge(head_lo_done, i * 4 + (2 * u + 2))
                    load_qk(i * 2 + (u + 2), u)
                    load_qp(i * 2 + (u + 2), u)
                    load_v(i * 2 + (u + 2), u)
                    sp.wait_ge(o_gated, i * 2 + (u + 2))
                    load_za(i * 2 + (u + 2), u)
            sp.wait_ge(table_loaded, 16)
            sp.wait_ge(comb_lo_done, 18)

            def load_pages(s, u, g):
                pages = [sp.value_load(ptab[0:1, ds(s * N_PAGES + (4 * g + j), 1)], min_val=0, max_val=d["cache_ckv"].shape[1] - 1)
                         for j in range(4)]
                if not isinstance(s, int):
                    sp.wait_ge(p_lo_done, s * 8 + (2 * g + 2 - 16))
                for j, page in enumerate(pages):
                    k = u * N_PAGES + 4 * g + j
                    sp.dma_start(ckv[:, k, :], d["cache_ckv"][0, ds(page, 1)].rearrange("a k r -> (a k) r")).then_inc(page_loaded[u][g], 16)
                    sp.dma_start(kpe[:, k, :], d["cache_kpe"][0, ds(page, 1)].rearrange("a k r -> (a k) r")).then_inc(page_loaded[u][g], 16)

            for b in range(2):
                for g in range(4):
                    load_pages(b, b, g)
            with sp.Fori(0, N_SAMPLE // 2 - 1) as i:
                for u in range(2):
                    for g in range(4):
                        load_pages(i * 2 + (2 + u), u, g)
            sp.wait_ge(p_lo_done, 8 * 7)
            sp.dma_start(wuv[:], w_uv).then_inc(wuv_loaded, 16)

            w_out = d["w_out"].rearrange("l (k p) n -> p (l k) n", p=P)

            def load_out(j, slot):
                sp.dma_start(w_raw[:, slot, :].rearrange("p (k n) -> p k n", k=KD),
                             w_out[:, :, ds(j * P, P)]).then_inc(w_loaded[slot], 16)

            sp.wait_ge(sc_ready, 5 * 8)
            for j in range(2):
                load_out(j, j)
            sp.wait_ge(p_lo_done, 8 * 8)
            sp.wait_ge(ot_copied, 9)
            sp.dma_start(zas[:], z_d[D_SSM:2 * D_SSM, :].rearrange("(h e) t -> e h t", e=P)[:, :, T_PROMPT:T]).then_inc(g_loaded, 16)
            for t in range(4):
                sp.dma_start(yt[:, t, :], x_prompt[t * P:(t + 1) * P, :]).then_inc(res_loaded, 16)
            sp.dma_start(ysm[0:N_SAMPLE, :], x_sample).then_inc(res_loaded, 16)
            sp.dma_start(gfin[:], d["g_final"].partition_broadcast(P)).then_inc(res_loaded, 16)
            with sp.Fori(0, 7) as i:
                for u in range(2):
                    sp.wait_ge(w_lo_ready, i * 2 + (B_OUT + 1 + u))
                    load_out(i * 2 + (2 + u), u)
            for t in range(4):
                sp.wait_ge(x_scaled, t + 6)
                sp.dma_start(d["o_y_p"].rearrange("b s m -> (b s) m")[t * P:(t + 1) * P, :], yt[:, t, :]).then_inc(y_stored, 16)
            sp.wait_ge(x_scaled, 10)
            sp.dma_start(d["o_y_s"].rearrange("b s m -> (b s) m"), ysm[0:N_SAMPLE, :]).then_inc(y_stored, 16)
            sp.wait_ge(y_stored, 16 * 5)

        @block.gpsimd
        def _(pool):
            pool.memset(ident[:], 0.0).then_inc(filled, 1)
            pool.memset(rot[:], 0.0).then_inc(filled, 1)
            pool.memset(causal[:], 0.0).then_inc(filled, 1)
            pool.memset(ones[:], 1.0).then_inc(const_ready, 1)
            pool.wait_ge(filled, 3)
            pool.affine_select(out=ident[:], in_=ident[:], compare_op=ALU.not_equal, fill=1.0, base=0,
                               pattern=[[-1, P]], channel_multiplier=1).then_inc(const_ready, 1)
            pool.affine_select(out=causal[:], in_=causal[:], compare_op=ALU.is_ge, fill=NEG, base=0,
                               pattern=[[-1, P]], channel_multiplier=1).then_inc(const_ready, 1)
            rv = rot[:].rearrange("p (a h i) -> p a h i", a=2, h=2)
            for h, off in ((0, -32), (1, 0)):
                v = rv[:, :, h, :]
                pool.affine_select(out=v, in_=v, compare_op=ALU.not_equal, fill=1.0, base=off,
                                   pattern=[[-64, 2], [-1, 32]], channel_multiplier=1).then_inc(const_ready, 1)

            def build_out(b):
                if b >= 2:
                    pool.wait_ge(y_ready, 2 * b - 2)
                for q in (2, 3):
                    g = 4 * b + q
                    n = 2 * b + q - 2
                    for c in range(2):
                        t2 = [ptmp[:, 2 * c + i].rearrange("p (t l c) -> p t l c", t=2, l=CHUNK) for i in range(2)]
                        for i in range(2):
                            pw = powers[:, (c + i) % 2, 1:9, g].unsqueeze(1).to_broadcast([P, 2, CHUNK])
                            pw = pw.unsqueeze(3).to_broadcast([P, 2, CHUNK, GROUP])
                            cc = cbd[:, i, g].unsqueeze(2).to_broadcast([P, 2, CHUNK, GROUP])
                            last = pool.tensor_tensor(t2[i], pw, cc, ALU.mult)
                        last.then_inc(pool_step, 1)
                    for c in range(2):
                        t2 = [ptmp[:, 2 * c + i].rearrange("p (t l c) -> p t l c", t=2, l=CHUNK) for i in range(2)]
                        pool.wait_ge(pool_step, 2 * n + 1 + c)
                        if c == 0:
                            last = pool.tensor_tensor(cast[:, b % 2, c, q], t2[0], t2[1], ALU.add)
                        else:
                            last = pool.tensor_tensor(cast[:, b % 2, c, q], t2[1], t2[0], ALU.subtract)
                    last.then_inc(ca_built_pool, 1)
                    pool.wait_ge(ca_built_pool, n + 1)

            pool.wait_ge(gemm_done, B_GLU)
            pool.memset(toep[:, 0:4], 0.0).then_inc(coef_ready, 1)
            pool.wait_ge(ev_stored[0], 16 * 19)
            pool.wait_ge(ev_stored[1], 16 * 18)
            build_out(0)
            for h in range(2):
                pool.wait_ge(toep_loaded[h], 16 * CHUNK)
            for b in range(1, 8):
                build_out(b)
            pool.wait_ge(state_t_ready, 2)
            pool.dma_start(latq[:], lat_d[0:Q_LORA, :].rearrange("(k p) t -> p k t", p=P)).then_inc(lat_loaded, 16)
            pool.dma_start(latc[:], lat_d[Q_LORA:Q_LORA + KV_LORA, :].rearrange("(k p) t -> p k t", p=P)).then_inc(lat_loaded, 16)
            pool.dma_start(cos[:], d["rope_cos"]).then_inc(rope_loaded, 16)
            pool.dma_start(sin[:], d["rope_sin"]).then_inc(rope_loaded, 16)
            for k in range(1, 10):
                if k == 6:
                    continue
                pool.wait_ge(squared, k + 1)
                i = k // 6
                pool.tensor_tensor(sq[:, i], sq[:, i], rs[:, k % 2], ALU.add).then_inc(pool_step, 1)
                pool.wait_ge(pool_step, 32 + k - i)
            for k in range(10):
                if k in (0, 6):
                    pool.wait_ge(rstd_ready, 6 + k // 6)
                buf = latq[:, k] if k < 6 else latc[:, k - 6]
                pool.tensor_tensor(buf, buf, rs[:, k // 6], ALU.mult).then_inc(normed, 1)
            pool.wait_ge(n_lo_done, 6)
            for h in range(2):
                pool.dma_start(rp[h * QK_ROPE:(h + 1) * QK_ROPE, 4, :],
                               lat_d[Q_LORA + KV_LORA:Q_LORA + KV_LORA + QK_ROPE, :]).then_inc(rope_loaded, 16)

            pool.wait_ge(c_t_ready, 6)
            for u in range(2):
                pool.wait_ge(c_stored[u], 16 * (4 - 2 * u))
            for z in (pt_hi, pt_lo):
                pool.memset(z[:, 1, 0:P].bitcast(F32), 0.0).then_inc(filled, 1)
                pool.memset(z[:, 3, 2 * P:3 * P].bitcast(F32), 0.0).then_inc(filled, 1)

            def head_lo(h, u):
                pool.wait_ge(head_hi_done, h * 2 + 1)
                pool.tensor_tensor(hl[:, u, 0:2], hraw[:, u, 0:2], hh[:, u, 0:2].bitcast(F32), ALU.subtract)
                pool.tensor_tensor(hl[0:QK_ROPE, u, 2], hraw[0:QK_ROPE, u, 2], hh[0:QK_ROPE, u, 2].bitcast(F32), ALU.subtract).then_inc(head_lo_done, 1)

            def values_lo(h, u):
                pool.wait_ge(head_hi_done, h * 2 + 2)
                pool.tensor_tensor(vl[0:N_META, u, 4], vraw[0:N_META, u, 4], vh[0:N_META, u, 4].bitcast(F32), ALU.subtract)
                pool.tensor_tensor(vl[:, u, 0:4], vraw[:, u, 0:4], vh[:, u, 0:4].bitcast(F32), ALU.subtract).then_inc(head_lo_done, 1)

            pool.wait_ge(head_lo_done, 1)
            values_lo(0, 0)
            head_lo(1, 1)
            values_lo(1, 1)
            with pool.Fori(0, N_HEADS // 2 - 1) as i:
                for u in range(2):
                    head_lo(i * 2 + (2 + u), u)
                    values_lo(i * 2 + (2 + u), u)

            pool.memset(not_own[:], NEG).then_inc(filled, 1)
            pool.wait_ge(filled, 8)
            pool.affine_select(out=not_own[:], in_=not_own[:], compare_op=ALU.not_equal, fill=0.0, base=0,
                               pattern=[[1, N_SAMPLE], [-1, N_SAMPLE]], channel_multiplier=0).then_inc(filled, 1)
            pool.memset(q_st[0][:].bitcast(F32), 0.0).then_inc(filled, 1)
            pool.memset(p_t[:].bitcast(F32), 0.0).then_inc(filled, 1)
            pool.memset(qa[:, 4:6], 0.0).then_inc(filled, 1)
            pool.wait_ge(comb_lo_done, 18)
            pool.memset(q_st[1][:].bitcast(F32), 0.0).then_inc(filled, 1)

            def page_lo(b, u, hg):
                pool.wait_ge(p_hi_done, b * 8 + (hg + 1))
                k = u * N_PAGES + 2 * hg
                pool.tensor_tensor(cp_lo[:, hg % 2], ckv[:, k:k + 2], cp_hi[:, hg % 2].bitcast(F32), ALU.subtract).then_inc(p_lo_done, 1)

            with pool.Fori(0, N_SAMPLE // 2) as i:
                for u in range(2):
                    for hg in range(8):
                        page_lo(i * 2 + u, u, hg)

        @block.scalar
        def _(act):
            def square(t):
                t0, rows = TILES[t]
                act.wait_ge(x_loaded[t], 32 if t in (0, 4) else 16)
                act.activation(junk[0:rows], xtok[0:rows, t], ACT.Square,
                               accum_out=stat[0:rows, t:t + 1]).then_inc(x_squared, 1)
                act.wait_ge(var_ready, t + 1)
                act.activation(stat[0:rows, 16 + t:17 + t], stat[0:rows, 8 + t:9 + t],
                               ACT.Sqrt).then_inc(std_ready, 1)

            def split_hi(n, r, slot, ahead):
                if ahead is not None:
                    width = block_width(ahead)
                    more = 0 if ahead < B_QR else r + 2 - (B_QR + 1 - slot) // 2 if ahead < B_K else 2
                    act.wait_ge(w_loaded[slot], (r + 2 + more) * 16)
                    act.wait_ge(gemm_done, n + 1)
                    act.activation(w_hi[:, slot, 0:width], w_raw[:, slot, 0:width], ACT.Copy).then_inc(w_hi_ready, 1)

            square(0)
            square(1)
            for g in range(20):
                t, q = divmod(g, 4)
                t0, rows = TILES[t]
                act.wait_ge(xt_ready, g + 1)
                act.activation(xh[:, 4 * q:4 * q + 4, t0:t0 + rows],
                               misc[g % 4][:].rearrange("p (k t) -> p k t", k=4)[:, :, 0:rows],
                               ACT.Copy).then_inc(xh_done, 1)
                if q == 3 and t < 3:
                    square(t + 2)
                if q == 3 and t in (2, 3):
                    act.wait_ge(w_loaded[t - 2], 16)
                    act.activation(w_hi[:, t - 2, :], w_raw[:, t - 2, :], ACT.Copy).then_inc(w_hi_ready, 1)

            act.wait_ge(prep_t_read, 1)
            act.activation(coef[:, 3], coef[:, 2], ACT.Exp).then_inc(dt_ready, 1)
            act.wait_ge(dve_step, 1)
            act.activation(coef[:, 5], coef[:, 4], ACT.Exp).then_inc(mag_ready, 1)
            act.wait_ge(angle_ready, 1)
            act.activation(coef[:, 10:12], coef[:, 8:10], ACT.Sin).then_inc(sin_ready, 1)

            def store(dst):
                def body(n, r, slot, ahead):
                    split_hi(n, r, slot, ahead)
                    act.wait_ge(gemm_read, n + 3)
                    act.dma_start(dst(n), ev[:, slot, :]).then_inc(ev_stored[slot], 16)
                return body

            blocks(act, B_LAT, 11, store(lambda n: lat_d[ds(n * P, P), :]))
            blocks(act, B_U, 8, store(lambda n: u_d[ds((n - B_U) * P, P), :]))

            act.wait_ge(coef_ready, 3)
            act.wait_ge(ev_stored[0], 16 + 16 * (B_ZS // 2 + B_ZS % 2))
            act.wait_ge(ev_stored[1], 16 + 16 * (B_ZS // 2))
            for lag in range(CHUNK):
                j = CHUNK - 1 - lag
                rows = xgrp[lag * GROUP:(lag + 1) * GROUP]
                act.dma_start(rows[:, :, N_SAMPLE:YCOLS],
                              u_d.rearrange("(g c) t -> c g t", c=GROUP)[:, :, j * N_CHUNK:(j + 1) * N_CHUNK]
                              ).then_inc(xgrp_loaded, 16)
            for lag, col in ((0, YCOLS), (CHUNK - 1, 0)):
                act.dma_start(xgrp[lag * GROUP:(lag + 1) * GROUP, :, col:col + N_SAMPLE],
                              u_d.rearrange("(g c) t -> c g t", c=GROUP)[:, :, T_PROMPT:T]).then_inc(xgrp_loaded, 16)

            def first_pass(b):
                act.wait_ge(bt_ready, b + 1)
                act.activation(bst[:, 0], misc[0][:].rearrange("p (q m) -> p q m", q=4), ACT.Copy).then_inc(bt_re_copied, 1)
                act.wait_ge(k_ready, b + 1)
                act.activation(kall[:, ds(b * P, P)], misc[2][:, 0:P], ACT.Copy).then_inc(k_copied, 1)
                act.wait_ge(s_ready, b + 1)
                act.activation(states[:, N_SAMPLE + 1:ENTRIES, 0, ds(b * 4, 4)],
                               misc[3][:, 0:4 * YCOLS].rearrange("p (q e) -> p e q", q=4), ACT.Copy).then_inc(s_re_copied, 1)

            def silu_store(first):
                def body(n, r, slot, ahead):
                    split_hi(n, r, slot, ahead)
                    act.wait_ge(gemm_done, n + 1)
                    act.wait_ge(ev_stored[slot], (r + 1) * 16)
                    for h, (h0, hw) in enumerate(HALVES):
                        last = act.activation(ev[:, slot, h0:h0 + hw], gemm[2 * slot + h][:, 0:hw], ACT.Silu)
                    last.then_inc(gemm_read, 1)
                    act.wait_ge(gemm_read, n + 3)
                    act.dma_start(z_d[ds((n - B_ZS) * P, P), :], ev[:, slot, :]).then_inc(ev_stored[slot], 16)
                return body

            with_first_pass(act, silu_store(B_ZS), first_pass)
            blocks(act, B_ZA, 8, silu_store(B_ZA))

            act.wait_ge(gemm_done, B_GLU)
            def gelu(b):
                act.wait_ge(yt_added, 2 * b + 2)
                act.activation(ys[:, b], yg[:, b % 2], ACT.Gelu_apprx_tanh).then_inc(gelu_done, 1)

            for b in range(8):
                act.wait_ge(y_ready, 2 * b + 1)
                if b >= 2:
                    act.wait_ge(yt_ready, 2 * b - 2)
                act.activation(ychunk[0:YCOLS, b % 2, :, 0:64].rearrange("p i (g c) -> p g i c", c=GROUP),
                               misc[0][0:YCOLS, :].rearrange("p (g i c) -> p g i c", g=4, c=GROUP), ACT.Copy).then_inc(y_copied, 1)
                if b >= 1:
                    gelu(b - 1)
            gelu(7)

            act.wait_ge(state_t_ready, 2)
            act.wait_ge(gelu_done, 8)
            for k in range(8):
                act.activation(ys_hi[:, k], ys[:, k], ACT.Copy).then_inc(ys_hi_done, 1)

            def glu(n, r, slot, ahead):
                split_hi(n, r, slot, ahead)
                act.wait_ge(gemm_done, n + 1)
                act.wait_ge(comb_lo_done, n - (B_GLU - 1))
                for h, (h0, hw) in enumerate(HALVES):
                    last = act.activation(sig[:, slot, h0:h0 + hw], gemm[2 * slot + h][:, 0:hw], ACT.Sigmoid,
                                          bias=bias_glu[:, ds(n - B_GLU, 1)])
                last.then_inc(sig_done, 1)
                act.wait_ge(gated, n - (B_GLU - 1))
                act.activation(comb_hi[:, ds(n - B_GLU, 1), :].rearrange("p a t -> p (a t)"), gate[:, slot], ACT.Copy).then_inc(comb_hi_done, 1)

            def square(k):
                if k >= 3 and k != 6:
                    act.wait_ge(pool_step, 32 + (k - 2 if k < 8 else k - 3))
                src = latq[:, k] if k < 6 else latc[:, k - 6]
                act.activation(sq[:, k // 6] if k in (0, 6) else rs[:, k % 2], src, ACT.Square).then_inc(squared, 1)

            act.wait_ge(lat_loaded, 32)
            for k in range(6):
                square(k)
            for n in range(B_GLU, B_GLU + 8):
                if n == B_GLU + 2:
                    for k in range(6, 10):
                        square(k)
                if n == B_GLU + 4:
                    for i in range(2):
                        act.wait_ge(var_ready, i + 6)
                        act.activation(rs[:, i], rs[:, i], ACT.Sqrt).then_inc(std_ready, 1)
                glu(n, n // 2, n % 2, B_GLU if n < B_GLU + 6 else n + 2)

            act.wait_ge(comb_lo_done, 10)
            for k in range(6):
                act.wait_ge(normed, k + 1)
                act.activation(qn_hi[:, k], latq[:, k], ACT.Copy, scale=vecs[:, k:k + 1]).then_inc(n_hi_done, 1)

            def kv_high():
                for k in range(4):
                    act.wait_ge(c_scaled, k + 1)
                    act.activation(cn_hi[:, k], latc[:, k], ACT.Copy).then_inc(n_hi_done, 1)

            def store_rows(dst, first):
                def body(n, r, slot, ahead):
                    split_hi(n, r, slot, ahead)
                    act.wait_ge(gemm_read, n + 3)
                    act.dma_start(dst[ds((n - first) * P, P), :], ev[:, slot, :]).then_inc(ev_stored[slot], 16)
                return body

            blocks(act, B_QN, 8, store_rows(q_d, B_QN))

            def store_c(t):
                act.wait_ge(c_t_copied, t + 1)
                t0, rows = TILES[t]
                if t < 4:
                    act.dma_start(NORM_OUT[0][t0:t0 + P, :], cout[:, t % 2, :]).then_inc(c_stored[t % 2], 16)
                else:
                    act.dma_start(NORM_OUT[0][t0:T_PROMPT, :], cout[0:N_META, 0, :]).then_inc(c_stored[0], 16)
                    act.dma_start(NORM_OUT[1], cout[N_META:rows, 0, :]).then_inc(c_stored[0], 16)

            blocks(act, B_QR, 4, split_hi, kv_high)
            blocks(act, B_K, 8, store_rows(k_d, B_K))
            def head_hi(u, count):
                act.wait_ge(head_loaded[u], (count + 1) * 48)
                act.activation(hh[:, u, 0:2], hraw[:, u, 0:2], ACT.Copy)
                act.activation(hh[0:QK_ROPE, u, 2], hraw[0:QK_ROPE, u, 2], ACT.Copy).then_inc(head_hi_done, 1)

            for v in range(10):
                j, t = divmod(v, 5)
                t0, rows = TILES[t]
                act.wait_ge(v_copied, v + 1)
                act.dma_start(v_d[t0:t0 + rows, j * 512:(j + 1) * 512], vout[0:rows, v % 2, :]).then_inc(v_stored[v % 2], 16)
                if v < 5:
                    act.wait_ge(rope_done, v + 1)
                    act.dma_start(qp_d[v * P:(v + 1) * P, :], ev[:, v % 2, :]).then_inc(ev_stored[v % 2], 16)
                else:
                    act.wait_ge(c_t_ready, t + 1)
                    if t >= 2:
                        act.wait_ge(c_stored[t % 2], 16 * (t // 2))
                    act.activation(cout[0:rows, t % 2, :], misc[t % 2][0:rows, :], ACT.Copy).then_inc(c_t_copied, 1)
                    store_c(t)
                if v == 8:
                    head_hi(0, 0)
            act.wait_ge(n_lo_done, 10)
            act.wait_ge(v_ready, 10)
            act.activation(cnt_hi[:], cn_hi[:, :, T_PROMPT:T].bitcast(F32), ACT.Copy)
            act.activation(cnt_lo[:], cn_lo[:, :, T_PROMPT:T].bitcast(F32), ACT.Copy).then_inc(cnt_saved, 1)
            act.wait_ge(cnt_saved, 1)
            act.wait_ge(kp_loaded, 16)
            act.activation(kp_hi[0:QK_ROPE], kp_raw[0:QK_ROPE], ACT.Copy).then_inc(kp_hi_done, 1)
            act.wait_ge(kpe_copied, 1)
            kv = kout[:]
            act.dma_start(KPE_OUT[0][0:512, :].rearrange("(t p) r -> p t r", p=P), kv[:, 0:4, :]).then_inc(kpe_stored, 16)
            act.dma_start(KPE_OUT[0][512:T_PROMPT, :], kv[0:N_META, 4, :]).then_inc(kpe_stored, 16)
            act.dma_start(KPE_OUT[1], kv[N_META:N_META + N_SAMPLE, 4, :]).then_inc(kpe_stored, 16)

            NM, SM, RS = 0, 12, 24
            def values_hi(u, count):
                act.wait_ge(v_loaded[u], (count + 1) * 32)
                act.activation(vh[:, u, 0:4], vraw[:, u, 0:4], ACT.Copy)
                act.activation(vh[0:N_META, u, 4], vraw[0:N_META, u, 4], ACT.Copy).then_inc(head_hi_done, 1)

            def exponential(n, m):
                i = m % 5
                rows = P if i < 4 else N_META
                width = P * min(i + 1, 4)
                act.wait_ge(max_ready, n + 1)
                if not isinstance(n, int) or n >= 3:
                    act.wait_ge(pt_ready, n - 1)
                last = act.activation(prob[0:rows, SLOT[m], 0:width], SBANK[m][0:rows, 0:width], ACT.Exp, scale=SCALE,
                                      bias=stat[0:rows, NM + m:NM + m + 1], accum_out=stat[0:rows, SM + m:SM + m + 1])
                if i == 4:
                    last = act.activation(prob[0:rows, SLOT[m], width:T_PROMPT], misc[0][0:rows, EXTRA], ACT.Exp, scale=SCALE,
                                          bias=stat[0:rows, NM + m:NM + m + 1], accum_out=stat[0:rows, 40 + m // 5:41 + m // 5])
                last.then_inc(exp_done, 1)

            def pt_high(n, m):
                i = m % 5
                rows = P if i < 4 else N_META
                act.wait_ge(pt_ready, n + 2)
                q0 = i * P
                src = misc[2 + m % 2][:, 0:5 * rows if i == 4 else (i + 1) * P].rearrange("p (j q) -> p j q", q=rows)
                last = act.activation(pt_hi[:, 0:min(i + 1, 4), q0:q0 + rows], src[:, 0:min(i + 1, 4)], ACT.Copy)
                if i == 4:
                    last = act.activation(pt_hi[0:rows, 4, q0:q0 + rows], src[0:rows, 4], ACT.Copy)
                last.then_inc(pt_hi_done, 1)

            def comb_high(h):
                act.wait_ge(o_gated, h + 2)
                act.activation(comb_hi[:, ds(h + 8, 1), 0:T_PROMPT].rearrange("p a t -> p (a t)"), otmp[:, 0:T_PROMPT], ACT.Copy).then_inc(comb_hi_done, 1)

            exponential(0, 0)
            values_hi(0, 0)
            head_hi(1, 0)

            def tile_act(n, pair, k):
                m, i, u = k % 10, k % 5, k // 5 % 2
                head = pair * 2 + k // 5
                if exists(n + 1):
                    exponential(n + 1, (k + 1) % 10)
                if i == 1 and k > 1:
                    comb_high(head - 1)
                if exists(n - 1):
                    pt_high(n - 1, (k - 1) % 10)
                if i == 2 and exists(n + 3):
                    act.wait_ge(pv_done, head + 1)
                    values_hi(1 - u, pair + u)
                if i == 3 and exists(n + 7):
                    act.wait_ge(scores_ready, n + 2)
                    head_hi(u, pair + 1)

            query_tiles(act, tile_act)

            SUM, RSUM, PART, SMAX = 48, 50, 52, 58
            act.wait_ge(filled, 13)
            act.wait_ge(sample_loaded, 16 * 6)
            act.activation(kpn_hi[0:QK_ROPE], kpn_raw[0:QK_ROPE], ACT.Copy)
            act.activation(cnew_hi[0:N_SAMPLE], half2[0:N_SAMPLE], ACT.Copy).then_inc(new_hi_done, 1)
            for h in range(N_HEADS):
                act.wait_ge(wuk_t_ready, h + 1)
                act.activation(wuk_t[:, h], misc[h % 4][:], ACT.Copy).then_inc(wuk_t_copied, 1)
            act.wait_ge(qa_ready, 1)
            act.activation(qa[:, 0:4].rearrange("p k b h -> p k h b"), gemm[3][:, 0:256].rearrange("p (k h b) -> p k h b", k=4, h=8), ACT.Copy)
            for half in range(2):
                rows = slice(half * QK_ROPE, (half + 1) * QK_ROPE)
                last = act.activation(qa[rows, 4 + half].rearrange("p b h -> p h b"), qps[rows], ACT.Copy)
            last.then_inc(wuk_t_copied, 1)
            act.wait_ge(wuk_t_copied, 9)

            def turn_hi(g, hg):
                act.wait_ge(t_ready, g + 1)
                for j in range(2):
                    act.activation(ct_hi[:, hg % 2, :, j * P:(j + 1) * P], misc[(hg % 2) * 2 + j][:].rearrange("p (k c) -> p k c", k=4), ACT.Copy)
                act.activation(kt_hi[:, hg % 2], gemm[0][:, 0:P], ACT.Copy).then_inc(t_hi_done, 1)

            def second_half(s, k):
                width = 512 if k else N_SAMPLE
                act.wait_ge(sc_ready, s * 5 + (k + 1))
                act.wait_ge(sc_added, s * 5 + k)
                act.activation(half2[0:N_HEADS, 0:width], gemm[2][32:40, 0:width], ACT.Copy).then_inc(half_copied, 1)

            def last_half(b):
                act.wait_ge(opv_done, b + 1)
                act.activation(half2[0:N_HEADS, 0:KV_LORA], gemm[3][32:40, :], ACT.Copy).then_inc(ohalf_copied, 1)

            def page_hi(hg, v):
                k = v * N_PAGES + 2 * hg
                act.activation(cp_hi[:, hg % 2], ckv[:, k:k + 2], ACT.Copy).then_inc(p_hi_done, 1)

            def query_hi(s, u):
                act.activation(q_st[u][:, :, 0:N_HEADS], qa[:, :, ds(s, 1), :].rearrange("p k b h -> p k (b h)"), ACT.Copy).then_inc(q_hi_done, 1)

            def sample_act(s, u, half):
                static = isinstance(s, int)
                run, weighs, turns = not static or s < N_SAMPLE, not static or s >= 1, not static or s >= 2
                v = 1 - u
                for hg in range(8):
                    if not static or s < N_SAMPLE - (1 if hg == 7 else 0):
                        turn_hi(s * 8 + (hg + 1), (hg + 1) % 8)
                    if hg == 0 and run:
                        second_half(s, 0)
                    if hg == 0 and weighs:
                        act.wait_ge(smax_ready, s)
                        act.activation(sc[v][0:N_HEADS, :], sc[v][0:N_HEADS, :], ACT.Exp, scale=SCALE, bias=stat[0:N_HEADS, SMAX + v:SMAX + v + 1],
                                       accum_out=stat[0:N_HEADS, SUM + v:SUM + v + 1]).then_inc(sexp_done, 1)
                    if hg == 1 and turns:
                        act.wait_ge(sc_added, s * 5 + 1 if run else s * 5)
                        last_half(s - 2)
                    if hg == 1 and weighs:
                        act.wait_ge(spt_ready, s)
                        act.activation(p_t[:, 0:N_PAGES, 0:N_HEADS], gemm[1][:, 0:P].rearrange("p (j h) -> p j h", h=N_HEADS), ACT.Copy)
                        act.activation(p_t[0:N_SAMPLE, N_PAGES, 0:N_HEADS], gemm[1][0:N_SAMPLE, P:P + N_HEADS], ACT.Copy).then_inc(spt_hi_done, 1)
                    if weighs:
                        if not (static and s == 1 and hg < 2):
                            act.wait_ge(pv_pair_done, s * 8 + (hg - 9))
                        page_hi(hg, v)
                    if hg == 4 and (not static or s < N_SAMPLE - 1):
                        if not static or s >= 1:
                            act.wait_ge(sc_ready, s * 5)
                        query_hi(s + 1, v)
                    if hg % 2 and run:
                        if hg == 1 and turns:
                            act.wait_ge(olat_step, s * 3 - 4)
                        second_half(s, (hg + 1) // 2)

            query_hi(0, 0)
            turn_hi(0, 0)
            samples(act, sample_act)
            act.wait_ge(olat_step, 3 * 7)
            last_half(7)


            def out_hi(j, slot, r):
                act.wait_ge(w_loaded[slot], (r + (B_OUT + 1 - slot) // 2 + 3) * 16)
                if not isinstance(j, int) or j >= 2:
                    act.wait_ge(gemm_done, j + (B_V - 1))
                act.activation(w_hi[:, slot, :], w_raw[:, slot, :], ACT.Copy).then_inc(w_hi_ready, 1)

            def out_copy(j, slot):
                act.wait_ge(gemm_done, j + (B_V + 1))
                act.wait_ge(out_t_ready, j + 1)
                for h in range(2):
                    last = act.activation(yb[:, slot, h * 260:(h + 1) * 260], gemm[2 * slot + h][:, 0:260], ACT.Copy)
                last.then_inc(gemm_read, 1)

            out_hi(0, 0, 0)
            out_hi(1, 1, 0)
            act.wait_ge(os_step, 6)
            act.activation(comb_hi[:, 8:16, T_PROMPT:T], oz[:], ACT.Copy).then_inc(os_step, 1)
            with act.Fori(0, 7) as i:
                for u in range(2):
                    out_copy(i * 2 + u, u)
                    out_hi(i * 2 + (2 + u), u, i + 1)
            out_copy(14, 0)
            out_copy(15, 1)
            for t in range(5):
                y, rows = (yt[:, t], P) if t < 4 else (ysm[0:N_SAMPLE], N_SAMPLE)
                act.wait_ge(out_added, 18)
                act.activation(junk2[0:rows], y, ACT.Square, accum_out=stat[0:rows, t:t + 1]).then_inc(x_squared, 1)
                act.wait_ge(var_ready, t + 8)
                act.activation(stat[0:rows, 16 + t:17 + t], stat[0:rows, 8 + t:9 + t], ACT.Sqrt).then_inc(std_ready, 1)

        @block.vector
        def _(dve):
            dve.sem_inc(gemm_read, 2)
            dve.sem_inc(ev_stored[0], 16)
            dve.sem_inc(ev_stored[1], 16)

            def scale(t):
                t0, rows = TILES[t]
                dve.wait_ge(x_squared, t + 1)
                dve.tensor_scalar(stat[0:rows, 8 + t:9 + t], stat[0:rows, t:t + 1], 1.0 / D_MODEL, EPS,
                                  ALU.mult, ALU.add).then_inc(var_ready, 1)
                dve.wait_ge(std_ready, t + 1)
                dve.reciprocal(stat[0:rows, 24 + t:25 + t], stat[0:rows, 16 + t:17 + t]).then_inc(rstd_ready, 1)
                dve.wait_ge(rstd_ready, t + 1)
                if t == 0:
                    dve.wait_ge(g_loaded, 16)
                dve.scalar_tensor_tensor(out=xtok[0:rows, t], in0=xtok[0:rows, t], scalar=stat[0:rows, 24 + t:25 + t],
                                         in1=gbc[0:rows], op0=ALU.mult, op1=ALU.mult).then_inc(x_scaled, 1)

            def split_lo(n, slot, ahead):
                if ahead is not None:
                    width = block_width(ahead)
                    dve.wait_ge(w_hi_ready, n + 3)
                    dve.tensor_tensor(w_lo[:, slot, 0:width], w_raw[:, slot, 0:width],
                                      w_hi[:, slot, 0:width].bitcast(F32), ALU.subtract).then_inc(w_lo_ready, 1)

            scale(0)
            scale(1)
            for g in range(20):
                t, q = divmod(g, 4)
                t0, rows = TILES[t]
                dve.wait_ge(xh_done, g + 1)
                dve.tensor_tensor(xl[:, 4 * q:4 * q + 4, t0:t0 + rows],
                                  misc[g % 4][:].rearrange("p (k t) -> p k t", k=4)[:, :, 0:rows],
                                  xh[:, 4 * q:4 * q + 4, t0:t0 + rows].bitcast(F32), ALU.subtract).then_inc(xl_done, 1)
                if q == 3 and t < 3:
                    scale(t + 2)
                if q == 3 and t in (2, 3):
                    split_lo(t - 4, t - 2, B_LAT)
            dve.wait_ge(prep_loaded, 16 * 13)
            dve.tensor_copy(anat[0:PAIRS, 2, :].rearrange("p (t n) -> p t n", t=2),
                            ldt[0:PAIRS, :].unsqueeze(2).to_broadcast([PAIRS, 2, N_STATE])).then_inc(ldt_spread, 1)

            dve.wait_ge(prep_t_ready, 1)
            dve.tensor_copy(coef[:, 0:3], misc[0][:, 0:3 * PAIRS].rearrange("p (a q) -> p a q", a=3)).then_inc(prep_t_read, 1)
            dve.tensor_copy(vecs[:, 0:26], misc[0][:, P:P + 26]).then_inc(prep_t_read, 1)
            dve.wait_ge(prep_t_ready, 2)
            for h in range(2):
                for c in range(2):
                    dve.tensor_copy(states[:, 4 * h:4 * h + 4, c, :],
                                    misc[1][:].rearrange("p (h c b q) -> p h c b q", h=2, c=2, b=4)[:, h, c]).then_inc(prep_t_read, 1)
            dve.memset(cbd[:], 0.0).then_inc(prep_t_read, 1)
            dve.wait_ge(prep_t_read, 7)
            dve.wait_ge(prep_t_ready, 3)
            for c in range(2):
                for t in range(2):
                    rows = slice(t * N_STATE, (t + 1) * N_STATE)
                    dve.tensor_scalar(cbd[rows, c, :, t, :], misc[2 + c][rows, :].rearrange("p (q c) -> p q c", c=GROUP),
                                      -1.0 if c else 1.0, None, ALU.mult).then_inc(prep_t_read, 1)

            step = [0]

            def link(ins):
                step[0] += 1
                ins.then_inc(dve_step, 1)
                dve.wait_ge(dve_step, step[0])

            AR, AI, DT, XR, MAG, TH, ROT, R, SN, CS, DEN, NR, FR, FI, U1, U2 = 0, 1, 3, 4, 5, 8, 12, 8, 10, 11, 6, 7, 16, 17, 18, 19
            c_ = lambda k: coef[:, k]
            tt = dve.tensor_tensor
            dve.wait_ge(dt_ready, 1)
            link(tt(c_(XR), c_(DT), c_(AR), ALU.mult))
            link(tt(c_(TH), c_(DT), c_(AI), ALU.mult))
            link(dve.tensor_scalar(c_(TH + 1), c_(TH), math.pi / 2, None, ALU.add))
            big_ = float(3 << 22)
            c1 = 6.28125
            c2 = 2 * math.pi - c1
            link(dve.tensor_scalar(coef[:, ROT:ROT + 2], coef[:, TH:TH + 2], 1 / (2 * math.pi), big_, ALU.mult, ALU.add))
            link(dve.tensor_scalar(coef[:, ROT:ROT + 2], coef[:, ROT:ROT + 2], -big_, None, ALU.add))
            link(dve.scalar_tensor_tensor(out=coef[:, R:R + 2], in0=coef[:, ROT:ROT + 2], scalar=-c1, in1=coef[:, R:R + 2],
                                          op0=ALU.mult, op1=ALU.add))
            link(dve.scalar_tensor_tensor(out=coef[:, R:R + 2], in0=coef[:, ROT:ROT + 2], scalar=-c2, in1=coef[:, R:R + 2],
                                          op0=ALU.mult, op1=ALU.add))
            dve.tensor_scalar(coef[:, R:R + 2], coef[:, R:R + 2], 3.1415925, -3.1415925, ALU.min, ALU.max).then_inc(angle_ready, 1)
            dve.wait_ge(sin_ready, 1)
            dve.wait_ge(mag_ready, 1)
            re, im = powers[:, 0], powers[:, 1]
            link(dve.memset(re[:, 0], 1.0))
            link(dve.memset(im[:, 0], 0.0))
            link(tt(re[:, 1], c_(MAG), c_(CS), ALU.mult))
            link(tt(im[:, 1], c_(MAG), c_(SN), ALU.mult))
            for k in (1, 2, 4):
                by = lambda z: z[:, k:k + 1].to_broadcast([P, k, PAIRS])
                t = [tmp[:, i, 0:k * PAIRS].rearrange("p (k q) -> p k q", k=k) for i in range(4)]
                link(tt(t[0], re[:, 1:k + 1], by(re), ALU.mult))
                link(tt(t[1], im[:, 1:k + 1], by(im), ALU.mult))
                link(tt(t[2], re[:, 1:k + 1], by(im), ALU.mult))
                link(tt(t[3], im[:, 1:k + 1], by(re), ALU.mult))
                link(tt(re[:, k + 1:2 * k + 1], t[0], t[1], ALU.subtract))
                link(tt(im[:, k + 1:2 * k + 1], t[2], t[3], ALU.add))
            link(tt(c_(U1), c_(AR), c_(AR), ALU.mult))
            link(tt(c_(U2), c_(AI), c_(AI), ALU.mult))
            link(tt(c_(DEN), c_(U1), c_(U2), ALU.add))
            link(dve.reciprocal(c_(DEN), c_(DEN)))
            link(dve.tensor_scalar(c_(NR), re[:, 1], -1.0, None, ALU.add))
            link(tt(c_(U1), c_(NR), c_(AR), ALU.mult))
            link(tt(c_(U2), im[:, 1], c_(AI), ALU.mult))
            link(tt(c_(U1), c_(U1), c_(U2), ALU.add))
            link(tt(c_(FR), c_(U1), c_(DEN), ALU.mult))
            link(tt(c_(U1), im[:, 1], c_(AR), ALU.mult))
            link(tt(c_(U2), c_(NR), c_(AI), ALU.mult))
            link(tt(c_(U1), c_(U1), c_(U2), ALU.subtract))
            link(tt(c_(FI), c_(U1), c_(DEN), ALU.mult))
            t = [tmp[:, i, :].rearrange("p (q c) -> p q c", c=GROUP) for i in range(4)]
            wide = lambda z: z.unsqueeze(2).to_broadcast([P, PAIRS, GROUP])
            link(tt(t[0], bbar[:, 0], wide(c_(FR)), ALU.mult))
            link(tt(t[1], bbar[:, 1], wide(c_(FI)), ALU.mult))
            link(tt(t[2], bbar[:, 1], wide(c_(FR)), ALU.mult))
            link(tt(t[3], bbar[:, 0], wide(c_(FI)), ALU.mult))
            link(tt(bbar[:, 0], t[0], t[1], ALU.subtract))
            link(tt(bbar[:, 1], t[2], t[3], ALU.add))
            dve.memset(xgrp[:, :, 0:N_SAMPLE], 0.0).then_inc(coef_ready, 1)
            dve.memset(xgrp[:, :, YCOLS:82], 0.0).then_inc(coef_ready, 1)
            dve.memset(states[:, N_SAMPLE], 0.0).then_inc(coef_ready, 1)

            def copy_out(n, r, slot, ahead):
                split_lo(n, slot, ahead)
                dve.wait_ge(gemm_done, n + 1)
                dve.wait_ge(ev_stored[slot], (r + 1) * 16)
                for h, (h0, hw) in enumerate(HALVES):
                    last = dve.tensor_copy(ev[:, slot, h0:h0 + hw], gemm[2 * slot + h][:, 0:hw])
                last.then_inc(gemm_read, 1)

            def copy_u(n, r, slot, ahead):
                split_lo(n, slot, ahead)
                dve.wait_ge(gemm_done, n + 1)
                dve.wait_ge(ev_stored[slot], (r + 1) * 16)
                out = ev[:, slot, 0:T_PROMPT].rearrange("p (j k) -> p k j", k=N_CHUNK)
                for h in range(2):
                    dve.tensor_copy(out[:, 33 * h:33 * h + 33],
                                    gemm[2 * slot + h][:, 0:264].rearrange("p (k j) -> p k j", j=CHUNK))
                dve.tensor_copy(ev[:, slot, T_PROMPT:T], gemm[2 * slot + 1][:, 264:272]).then_inc(gemm_read, 1)

            blocks(dve, B_LAT, 11, copy_out)
            blocks(dve, B_U, 8, copy_u)

            dve.sem_inc(s_im_copied, 1)
            dve.sem_inc(s_re_copied, 1)
            dve.sem_inc(k_copied, 1)
            dve.wait_ge(coef_ready, 3)
            def build(b, slot):
                t4 = [tmp[:, i].rearrange("p (q l c) -> p q l c", q=4, l=CHUNK) for i in range(4)]
                for i, (pc, bc) in enumerate(((0, 0), (1, 1), (0, 1), (1, 0))):
                    pw = powers[:, pc, 0:CHUNK, ds(b * 4, 4)].rearrange("p l q -> p q l").unsqueeze(3).to_broadcast([P, 4, CHUNK, GROUP])
                    bb = bbar[:, bc, ds(b * 4, 4), :].unsqueeze(2).to_broadcast([P, 4, CHUNK, GROUP])
                    last = tt(t4[i], pw, bb, ALU.mult)
                last.then_inc(mul_done, 1)
                dve.wait_ge(mul_done, b + 1)
                tt(wst[:, slot, 0], t4[0], t4[1], ALU.subtract)
                tt(wst[:, slot, 1], t4[2], t4[3], ALU.add).then_inc(wst_built, 1)
                dve.wait_ge(wst_built, b + 1)

            def first_pass(b):
                dve.wait_ge(bt_ready, b + 1)
                dve.tensor_copy(bst[:, 1], misc[1][:].rearrange("p (q m) -> p q m", q=4)).then_inc(bt_im_copied, 1)
                dve.wait_ge(s_ready, b + 1)
                dve.tensor_copy(states[:, N_SAMPLE + 1:ENTRIES, 1, ds(b * 4, 4)],
                                misc[0][:, 0:4 * YCOLS].rearrange("p (q e) -> p e q", q=4)).then_inc(s_im_copied, 1)

            for b in range(2):
                build(b, b)
            for n in (B_ZS, B_ZS + 1):
                split_lo(n, n % 2, B_ZS)
            with dve.Fori(0, 3) as i:
                for u in range(2):
                    first_pass(i * 2 + u)
                    build(i * 2 + (2 + u), u)
                    split_lo(i * 2 + (B_ZS + 2 + u), (B_ZS + u) % 2, B_ZS)
            for b in (6, 7):
                first_pass(b)

            a8 = [powers[:, c, 8].unsqueeze(1).to_broadcast([P, 2, PAIRS]) for c in range(2)]
            m1, m2 = [tmp[:, i, 0:2 * PAIRS].rearrange("p (c q) -> p c q", c=2) for i in range(2)]

            def scan(k):
                prev = states[:, ds(k + N_SAMPLE, 1)].rearrange("p e c q -> p (e c) q")
                new = states[:, ds(k + (N_SAMPLE + 1), 1)].rearrange("p e c q -> p (e c) q")
                tt(m1, prev, a8[0], ALU.mult)
                tt(m2, prev, a8[1], ALU.mult).then_inc(scan_step, 1)
                dve.wait_ge(scan_step, k * 3 + 1)
                tt(new, new, m1, ALU.add).then_inc(scan_step, 1)
                dve.wait_ge(scan_step, k * 3 + 2)
                tt(new[:, 0], new[:, 0], m2[:, 1], ALU.subtract)
                tt(new[:, 1], new[:, 1], m2[:, 0], ALU.add).then_inc(scan_step, 1)
                dve.wait_ge(scan_step, k * 3 + 3)

            dve.wait_ge(s_re_copied, 9)
            dve.wait_ge(s_im_copied, 9)
            h0, hs = states[:, 0:N_SAMPLE], states[:, ENTRIES - N_SAMPLE:ENTRIES]
            a1 = [powers[:, c, 1].unsqueeze(1).to_broadcast([P, N_SAMPLE, PAIRS]) for c in range(2)]
            m = [tmp[:, i, 0:256].rearrange("p (b q) -> p b q", q=PAIRS) for i in range(4)]
            for i, (c, e) in enumerate(((0, 0), (1, 1), (0, 1), (1, 0))):
                last = tt(m[i], h0[:, :, c], a1[e], ALU.mult)
            last.then_inc(sample_step, 1)
            dve.wait_ge(sample_step, 1)
            tt(m[0], m[0], m[1], ALU.subtract)
            tt(m[2], m[2], m[3], ALU.add).then_inc(sample_step, 1)
            dve.wait_ge(sample_step, 2)
            tt(snew[:, 0], hs[:, :, 0], m[0], ALU.add)
            tt(snew[:, 1], hs[:, :, 1], m[2], ALU.add).then_inc(sample_step, 1)
            dve.wait_ge(sample_step, 3)

            def build_out(b):
                if b >= 2:
                    dve.wait_ge(y_ready, 2 * b - 2)
                for q in range(2):
                    g = 4 * b + q
                    for c in range(2):
                        out = cast[:, b % 2, c, q]
                        t2 = [tmp[:, 2 * c + i, 0:256].rearrange("p (t l c) -> p t l c", t=2, l=CHUNK) for i in range(2)]
                        for i in range(2):
                            pw = powers[:, (c + i) % 2, 1:9, g].unsqueeze(1).to_broadcast([P, 2, CHUNK])
                            pw = pw.unsqueeze(3).to_broadcast([P, 2, CHUNK, GROUP])
                            cc = cbd[:, i, g].unsqueeze(2).to_broadcast([P, 2, CHUNK, GROUP])
                            last = tt(t2[i], pw, cc, ALU.mult)
                        last.then_inc(mul_done, 1)
                        dve.wait_ge(mul_done, 8 + 4 * b + 2 * q + c + 1)
                        if c == 0:
                            last = tt(out, t2[0], t2[1], ALU.add)
                        else:
                            last = tt(out, t2[1], t2[0], ALU.subtract)
                last.then_inc(ca_built, 1)

            dve.wait_ge(k_ready, 8)
            build_out(0)
            SCAN_FIRST = N_CHUNK % 8
            for k in range(SCAN_FIRST):
                scan(k)

            def split_and_scan(n, r, slot, ahead):
                for j in range(8):
                    if isinstance(n, int) and n == B_GLU - 1 and j == 4:
                        dve.wait_ge(gemm_done, B_GLU)
                        dve.memset(toep[:, 4:CHUNK - 1], 0.0).then_inc(coef_ready, 1)
                    scan((n - B_ZA) * 8 + (SCAN_FIRST + j))
                split_lo(n, slot, ahead)

            blocks(dve, B_ZA, 8, split_and_scan)

            def add_skip(b):
                dve.wait_ge(ug_loaded[b % 2], 16 * (b // 2 + 1))
                if b >= 2:
                    dve.wait_ge(gelu_done, b - 1)
                for h in range(2):
                    dve.wait_ge(yt_ready, 2 * b + h + 1)
                    out = yg[:, b % 2, 0:T_PROMPT].rearrange("p (k j) -> p j k", j=CHUNK)[:, 4 * h:4 * h + 4]
                    src = misc[2 + h][:, 0:4 * YCOLS].rearrange("p (j k) -> p j k", j=4)
                    uu = ug[:, b % 2, 0:T_PROMPT].rearrange("p (j k) -> p j k", j=CHUNK)[:, 4 * h:4 * h + 4]
                    last = dve.scalar_tensor_tensor(out=out, in0=uu, scalar=vecs[:, 18 + b:19 + b],
                                                    in1=src[:, :, N_SAMPLE:], op0=ALU.mult, op1=ALU.add)
                    if h == 0:
                        last = dve.scalar_tensor_tensor(out=yg[:, b % 2, T_PROMPT:T], in0=ug[:, b % 2, T_PROMPT:T],
                                                        scalar=vecs[:, 18 + b:19 + b], in1=src[:, 0, 0:N_SAMPLE],
                                                        op0=ALU.mult, op1=ALU.add)
                    last.then_inc(yt_added, 1)

            for h in range(2):
                dve.wait_ge(toep_loaded[h], 16 * CHUNK)
            build_out(1)
            for b in range(8):
                dve.wait_ge(y_ready, 2 * b + 2)
                if b >= 2:
                    dve.wait_ge(yt_ready, 2 * b - 2)
                dve.tensor_copy(ychunk[0:YCOLS, b % 2, :, 64:P].rearrange("p i (g c) -> p g i c", c=GROUP),
                                misc[1][0:YCOLS, :].rearrange("p (g i c) -> p g i c", g=4, c=GROUP)).then_inc(y_copied, 1)
                if b < 6:
                    build_out(b + 2)
                add_skip(b)
            dve.wait_ge(state_t_ready, 1)
            dve.tensor_copy(sout[:, 0:4, :], misc[0][:].rearrange("p (a m) -> p a m", a=4)).then_inc(state_copied, 4)
            dve.wait_ge(state_t_ready, 2)
            dve.tensor_copy(sout[0:PAIRS, 4:6, :], misc[1][0:PAIRS, 0:2 * P].rearrange("p (a m) -> p a m", a=2)).then_inc(state_copied, 2)
            for k in range(8):
                dve.wait_ge(ys_hi_done, k + 1)
                tt(ys_lo[:, k], ys[:, k], ys_hi[:, k].bitcast(F32), ALU.subtract).then_inc(ys_lo_done, 1)
            dve.sem_inc(comb_lo_done, 2)

            def glu(n, r, slot, ahead):
                split_lo(n, slot, ahead)
                dve.wait_ge(sig_done, n - (B_GLU - 1))
                dve.wait_ge(gate_loaded[slot], gate_count(n, r, slot))
                y = ys[:, ds(n - B_GLU, 1), :].rearrange("p a t -> p (a t)")
                tt(sig[:, slot], sig[:, slot], y, ALU.mult).then_inc(gemm_read, 1)
                dve.wait_ge(gemm_read, n + 3)
                tt(gate[:, slot], gate[:, slot], sig[:, slot], ALU.mult).then_inc(gated, 1)
                dve.wait_ge(comb_hi_done, n - (B_GLU - 1))
                lo = comb_lo[:, ds(n - B_GLU, 1), :].rearrange("p a t -> p (a t)")
                hi = comb_hi[:, ds(n - B_GLU, 1), :].rearrange("p a t -> p (a t)")
                tt(lo, gate[:, slot], hi.bitcast(F32), ALU.subtract).then_inc(comb_lo_done, 1)

            def norms():
                for i, width in enumerate((Q_LORA, KV_LORA)):
                    dve.wait_ge(sums_ready, i + 1)
                    for h, (h0, hw) in enumerate(HALVES):
                        last = dve.tensor_scalar(rs[:, i, h0:h0 + hw], misc[2 * i + h][:, 0:hw], 1.0 / width, EPS, ALU.mult, ALU.add)
                    last.then_inc(var_ready, 1)
                dve.wait_ge(std_ready, 6)
                dve.reciprocal(rs[:, 0], rs[:, 0]).then_inc(rstd_ready, 1)

            def norm_kv():
                dve.wait_ge(std_ready, 7)
                dve.reciprocal(rs[:, 1], rs[:, 1]).then_inc(rstd_ready, 1)

            glu_blocks(dve, glu, norms)

            dve.wait_ge(comb_lo_done, 10)
            for k in range(6):
                dve.wait_ge(n_hi_done, k + 1)
                dve.scalar_tensor_tensor(out=qn_lo[:, k], in0=latq[:, k], scalar=vecs[:, k:k + 1], in1=qn_hi[:, k].bitcast(F32),
                                         op0=ALU.mult, op1=ALU.subtract).then_inc(n_lo_done, 1)

            def kv_low():
                for k in range(4):
                    dve.wait_ge(normed, k + 7)
                    dve.tensor_scalar(latc[:, k], latc[:, k], vecs[:, 6 + k:7 + k], None, ALU.mult).then_inc(c_scaled, 1)
                for k in range(4):
                    dve.wait_ge(n_hi_done, k + 7)
                    tt(cn_lo[:, k], latc[:, k], cn_hi[:, k].bitcast(F32), ALU.subtract).then_inc(n_lo_done, 1)

            def copy_q(stores):
                def body(n, r, slot, ahead):
                    if ahead not in (B_V, B_V + 1):
                        split_lo(n, slot, ahead)
                    dve.wait_ge(gemm_done, n + 1)
                    dve.wait_ge(ev_stored[slot], (stores(r, slot) + 1) * 16)
                    for h, (h0, hw) in enumerate(HALVES):
                        last = dve.tensor_copy(ev[:, slot, h0:h0 + hw], gemm[2 * slot + h][:, 0:hw])
                    last.then_inc(gemm_read, 1)
                    if ahead in (B_V, B_V + 1):
                        split_lo(n, slot, ahead)
                return body

            blocks(dve, B_QN, 8, copy_q(lambda r, slot: r - 4), norm_kv)

            def keep_rotary(n, r, slot, ahead):
                split_lo(n, slot, ahead)
                dve.wait_ge(gemm_done, n + 1)
                for h, (h0, hw) in enumerate(HALVES):
                    last = dve.tensor_copy(rp[:, ds(n - B_QR, 1), h0:h0 + hw].rearrange("p a t -> p (a t)"), gemm[2 * slot + h][:, 0:hw])
                last.then_inc(gemm_read, 1)

            blocks(dve, B_QR, 4, keep_rotary, kv_low)
            blocks(dve, B_K, 8, copy_q(lambda r, slot: r - 6))

            dve.wait_ge(rope_loaded, 64)
            for v in range(10):
                rows = TILES[v % 5][1]
                dve.wait_ge(v_ready, v + 1)
                if v >= 2:
                    dve.wait_ge(v_stored[v % 2], 16 * (v // 2))
                dve.tensor_copy(vout[0:rows, v % 2, :], gemm[v % 4][0:rows, :]).then_inc(v_copied, 1)
                if v < 5:
                    dve.wait_ge(rotated, v + 1)
                    dve.wait_ge(ev_stored[v % 2], 16 * (1 + EV_STORES[v % 2] + v // 2))
                    for h, (h0, hw) in enumerate(HALVES):
                        last = tt(ev[:, v % 2, h0:h0 + hw], misc[2 + h][:, 0:hw], sin[:, h0:h0 + hw], ALU.mult)
                    last.then_inc(rope_step, 1)
                    tt(rp[:, v], rp[:, v], cos[:], ALU.mult).then_inc(rope_step, 1)
                    dve.wait_ge(rope_step, 2 * v + 2)
                    tt(ev[:, v % 2], ev[:, v % 2], rp[:, v], ALU.add).then_inc(rope_done, 1)
            dve.wait_ge(cnt_saved, 1)
            tt(hl[:, 0, 0:2], hraw[:, 0, 0:2], hh[:, 0, 0:2].bitcast(F32), ALU.subtract)
            tt(hl[0:QK_ROPE, 0, 2], hraw[0:QK_ROPE, 0, 2], hh[0:QK_ROPE, 0, 2].bitcast(F32), ALU.subtract).then_inc(head_lo_done, 1)
            dve.wait_ge(kp_hi_done, 1)
            tt(kp_lo[0:QK_ROPE], kp_raw[0:QK_ROPE], kp_hi[0:QK_ROPE].bitcast(F32), ALU.subtract).then_inc(kp_lo_done, 1)
            dve.wait_ge(c_t_ready, 6)
            dve.wait_ge(state_stored, 16 * 6)
            dve.tensor_copy(kout[:], misc[0][:, 0:5 * QK_ROPE].rearrange("p (t r) -> p t r", t=5)).then_inc(kpe_copied, 1)

            NM, SM, RS = 0, 12, 24
            dve.sem_inc(o_gated, 1)
            dve.sem_inc(ot_copied, 1)

            def maximum(n, m, head):
                i = m % 5
                rows = P if i < 4 else N_META
                width = P * min(i + 1, 4)
                bank = SBANK[m]
                dve.wait_ge(scores_ready, n + 1)
                diag = bank[:, i * P:(i + 1) * P] if i < 4 else misc[0][0:rows, EXTRA]
                tt(diag, diag, causal[0:rows, 0:rows], ALU.add).then_inc(max_step, 1)
                dve.wait_ge(max_step, head * 11 + (2 * i + 1))
                nm = stat[0:rows, NM + m:NM + m + 1]
                if i < 4:
                    dve.reduce_max(nm, bank[0:rows, 0:width], axis=AX.X).then_inc(max_step, 1)
                else:
                    parts = stat[0:rows, 42 + 2 * (m // 5):44 + 2 * (m // 5)]
                    dve.reduce_max(parts[:, 0:1], bank[0:rows, 0:width], axis=AX.X)
                    dve.reduce_max(parts[:, 1:2], misc[0][0:rows, EXTRA], axis=AX.X).then_inc(max_step, 1)
                    dve.wait_ge(max_step, head * 11 + 10)
                    tt(nm, parts[:, 0:1], parts[:, 1:2], ALU.max).then_inc(max_step, 1)
                dve.wait_ge(max_step, head * 11 + (2 * i + 2 if i < 4 else 11))
                dve.tensor_scalar(nm, nm, -SCALE, None, ALU.mult).then_inc(max_ready, 1)

            def normalise(n, m, head):
                i = m % 5
                rows = P if i < 4 else N_META
                width = P * (i + 1) if i < 4 else T_PROMPT
                sm, r = stat[0:rows, SM + m:SM + m + 1], stat[0:rows, RS + m:RS + m + 1]
                dve.wait_ge(exp_done, n + 1)
                if i == 4:
                    tt(sm, sm, stat[0:rows, 40 + m // 5:41 + m // 5], ALU.add).then_inc(sum_step, 1)
                    dve.wait_ge(sum_step, head * 6 + 5)
                dve.reciprocal(r, sm).then_inc(sum_step, 1)
                dve.wait_ge(sum_step, head * 6 + (i + 1 if i < 4 else 6))
                p = prob[0:rows, SLOT[m], 0:width]
                dve.tensor_scalar(p, p, r, None, ALU.mult).then_inc(prob_ready, 1)

            def pt_low(n, m):
                i = m % 5
                rows = P if i < 4 else N_META
                q0 = i * P
                dve.wait_ge(pt_hi_done, n + 1)
                src = misc[2 + m % 2][:, 0:5 * rows if i == 4 else (i + 1) * P].rearrange("p (j q) -> p j q", q=rows)
                w = min(i + 1, 4)
                last = tt(pt_lo[:, 0:w, q0:q0 + rows], src[:, 0:w], pt_hi[:, 0:w, q0:q0 + rows].bitcast(F32), ALU.subtract)
                if i == 4:
                    last = tt(pt_lo[0:rows, 4, q0:q0 + rows], src[0:rows, 4], pt_hi[0:rows, 4, q0:q0 + rows].bitcast(F32), ALU.subtract)
                last.then_inc(pt_lo_done, 1)

            def gate_o(h, u, count):
                dve.wait_ge(ug_loaded[u], (count + 5) * 16)
                dve.wait_ge(pv_done, h + 2)
                tt(otmp[:, 0:256], gemm[3][:, 0:256], za[:, u, 0:256], ALU.mult)
                tt(otmp[:, 256:T_PROMPT], misc[0][:, 0:272], za[:, u, 256:T_PROMPT], ALU.mult).then_inc(o_gated, 1)

            def comb_low(h):
                dve.wait_ge(comb_hi_done, h + 9)
                tt(comb_lo[:, ds(h + 8, 1), 0:T_PROMPT].rearrange("p a t -> p (a t)"), otmp[:, 0:T_PROMPT],
                   comb_hi[:, ds(h + 8, 1), 0:T_PROMPT].rearrange("p a t -> p (a t)").bitcast(F32), ALU.subtract).then_inc(comb_lo_done, 1)

            maximum(0, 0, 0)
            normalise(0, 0, 0)
            maximum(1, 1, 0)

            def tile_dve(n, pair, k):
                i, u = k % 5, k // 5 % 2
                tile = lambda j: (n + j, (k + j) % 10, pair * 2 + (k + j) // 5)
                if exists(n + 1):
                    normalise(*tile(1))
                if exists(n + 2):
                    maximum(*tile(2))
                if i == 1 and k > 1:
                    gate_o(pair * 2 + k // 5 - 1, 1 - u, pair + (k // 5 - 1) // 2)
                    comb_low(pair * 2 + k // 5 - 1)
                if exists(n - 1):
                    pt_low(n - 1, (k - 1) % 10)

            query_tiles(dve, tile_dve)

            SUM, RSUM, PART, SMAX = 48, 50, 52, 58
            dve.wait_ge(new_hi_done, 1)
            tt(kpn_lo[0:QK_ROPE], kpn_raw[0:QK_ROPE], kpn_hi[0:QK_ROPE].bitcast(F32), ALU.subtract)
            tt(cnew_lo[0:N_SAMPLE], half2[0:N_SAMPLE], cnew_hi[0:N_SAMPLE].bitcast(F32), ALU.subtract).then_inc(new_lo_done, 1)

            def turn_lo(g, hg):
                dve.wait_ge(t_hi_done, g + 1)
                for j in range(2):
                    tt(ct_lo[:, hg % 2, :, j * P:(j + 1) * P], misc[(hg % 2) * 2 + j][:].rearrange("p (k c) -> p k c", k=4),
                       ct_hi[:, hg % 2, :, j * P:(j + 1) * P].bitcast(F32), ALU.subtract)
                tt(kt_lo[:, hg % 2], gemm[0][:, 0:P], kt_hi[:, hg % 2].bitcast(F32), ALU.subtract).then_inc(t_lo_done, 1)

            def add_halves(s, u, k):
                width = 512 if k else N_SAMPLE
                out = sc[u][0:N_HEADS, (k - 1) * 512:k * 512] if k else sc[u][0:N_HEADS, PAST:KEYS]
                dve.wait_ge(half_copied, s * 5 + (k + 1))
                tt(out, gemm[2][0:N_HEADS, 0:width], half2[0:N_HEADS, 0:width], ALU.add).then_inc(sc_added, 1)
                dve.wait_ge(sc_added, s * 5 + (k + 1))
                if k == 0:
                    tt(out, out, not_own[:, ds(s, 1), :].rearrange("p a b -> p (a b)"), ALU.add).then_inc(sc_step, 1)
                    dve.wait_ge(sc_step, s * 3 + 1)
                last = dve.reduce_max(stat[0:N_HEADS, PART + k:PART + k + 1], out, axis=AX.X)
                if k == 4:
                    last.then_inc(sc_step, 1)
                    dve.wait_ge(sc_step, s * 3 + 2)
                    nm = stat[0:N_HEADS, SMAX + u:SMAX + u + 1]
                    dve.reduce_max(nm, stat[0:N_HEADS, PART:PART + 5], axis=AX.X).then_inc(sc_step, 1)
                    dve.wait_ge(sc_step, s * 3 + 3)
                    dve.tensor_scalar(nm, nm, -SCALE, None, ALU.mult).then_inc(smax_ready, 1)

            def sum_latent(b, u):
                dve.wait_ge(sexp_done, b + 1)
                dve.wait_ge(ohalf_copied, b + 1)
                dve.wait_ge(ot_ready, b + 1)
                dve.reciprocal(stat[0:N_HEADS, RSUM + u:RSUM + u + 1], stat[0:N_HEADS, SUM + u:SUM + u + 1]).then_inc(olat_step, 1)
                tt(olat[0:N_HEADS], gemm[3][0:N_HEADS, :], half2[0:N_HEADS], ALU.add).then_inc(olat_step, 1)
                dve.wait_ge(olat_step, b * 3 + 2)
                dve.tensor_scalar(olat[0:N_HEADS], olat[0:N_HEADS], stat[0:N_HEADS, RSUM + u:RSUM + u + 1], None, ALU.mult).then_inc(olat_step, 1)

            def copy_ot(b):
                dve.wait_ge(ot_ready, b + 2)
                dve.tensor_copy(olat_t[:, :, :, ds(b, 1)].rearrange("p k h b -> p k (h b)"),
                                gemm[1][:, 256:288].rearrange("p (k h) -> p k h", k=4)).then_inc(ot_copied, 1)

            def query_lo(s, u):
                dve.wait_ge(q_hi_done, s + 1)
                tt(q_st[u][:, :, 32:40], qa[:, :, ds(s, 1), :].rearrange("p k b h -> p k (b h)"), q_st[u][:, :, 0:N_HEADS].bitcast(F32),
                   ALU.subtract).then_inc(q_lo_done, 1)

            def sample_dve(s, u, half):
                static = isinstance(s, int)
                run, weighs, turns = not static or s < N_SAMPLE, not static or s >= 1, not static or s >= 2
                for hg in range(8):
                    if not static or s < N_SAMPLE - (1 if hg == 7 else 0):
                        turn_lo(s * 8 + (hg + 1), (hg + 1) % 8)
                    if hg == 0 and run:
                        if turns:
                            dve.wait_ge(spt_ready, s - 1)
                        add_halves(s, u, 0)
                    if hg == 1 and turns:
                        sum_latent(s - 2, u)
                    if hg == 1 and weighs:
                        dve.wait_ge(spt_hi_done, s)
                        tt(p_t[:, 0:N_PAGES, 32:40], gemm[1][:, 0:P].rearrange("p (j h) -> p j h", h=N_HEADS),
                           p_t[:, 0:N_PAGES, 0:N_HEADS].bitcast(F32), ALU.subtract)
                        tt(p_t[0:N_SAMPLE, N_PAGES, 32:40], gemm[1][0:N_SAMPLE, P:P + N_HEADS],
                           p_t[0:N_SAMPLE, N_PAGES, 0:N_HEADS].bitcast(F32), ALU.subtract).then_inc(spt_lo_done, 1)
                    if hg == 3 and turns:
                        copy_ot(s - 2)
                    if hg == 4 and (not static or s < N_SAMPLE - 1):
                        query_lo(s + 1, 1 - u)
                    if hg % 2 and run:
                        add_halves(s, u, (hg + 1) // 2)

            dve.wait_ge(wuk_t_copied, 9)
            query_lo(0, 0)
            turn_lo(0, 0)
            samples(dve, sample_dve)
            sum_latent(7, 1)
            copy_ot(7)

            def out_lo(j, slot):
                dve.wait_ge(w_hi_ready, j + (B_OUT + 1))
                tt(w_lo[:, slot, :], w_raw[:, slot, :], w_hi[:, slot, :].bitcast(F32), ALU.subtract).then_inc(w_lo_ready, 1)

            def out_add(j, slot):
                dve.wait_ge(out_t_ready, j + 3)
                cols = yt[:, :, ds(j * P, P)]
                tt(cols, cols, misc[slot][:].rearrange("p (t n) -> p t n", t=4), ALU.add)
                cols = ysm[0:N_SAMPLE, ds(j * P, P)]
                tt(cols, cols, misc[2 + slot][0:N_SAMPLE, 0:P], ALU.add).then_inc(out_added, 1)

            for half in range(2):
                dve.wait_ge(os_step, half + 1)
                dve.tensor_copy(oh[0:N_SAMPLE, half * 512:(half + 1) * 512], gemm[half][0:N_SAMPLE, :]).then_inc(oh_copied, 1)
            out_lo(0, 0)
            dve.wait_ge(g_loaded, 32)
            dve.wait_ge(os_step, 3)
            tt(oz[:], misc[0][:, 0:64].rearrange("p (h b) -> p h b", h=8), zas[:], ALU.mult).then_inc(os_step, 3)
            dve.wait_ge(os_step, 7)
            tt(comb_lo[:, 8:16, T_PROMPT:T], oz[:], comb_hi[:, 8:16, T_PROMPT:T].bitcast(F32), ALU.subtract).then_inc(os_step, 1)

            dve.sem_inc(out_added, 2)
            out_lo(1, 1)
            dve.wait_ge(res_loaded, 16 * 6)
            with dve.Fori(0, 7) as i:
                for u in range(2):
                    out_lo(i * 2 + (2 + u), u)
                    out_add(i * 2 + u, u)
            out_add(14, 0)
            out_add(15, 1)
            for t in range(5):
                y, rows = (yt[:, t], P) if t < 4 else (ysm[0:N_SAMPLE], N_SAMPLE)
                dve.wait_ge(x_squared, t + 6)
                dve.tensor_scalar(stat[0:rows, 8 + t:9 + t], stat[0:rows, t:t + 1], 1.0 / D_MODEL, EPS, ALU.mult, ALU.add).then_inc(var_ready, 1)
                dve.wait_ge(std_ready, t + 8)
                dve.reciprocal(stat[0:rows, 24 + t:25 + t], stat[0:rows, 16 + t:17 + t]).then_inc(rstd_ready, 1)
                dve.wait_ge(rstd_ready, t + 8)
                dve.scalar_tensor_tensor(out=y, in0=y, scalar=stat[0:rows, 24 + t:25 + t], in1=gfin[0:rows],
                                         op0=ALU.mult, op1=ALU.mult).then_inc(x_scaled, 1)

        @block.tensor
        def _(pe):
            pe.wait_ge(const_ready, 5)
            for g in range(20):
                t, q = divmod(g, 4)
                t0, rows = TILES[t]
                pe.wait_ge(x_scaled, t + 1)
                if g >= 4:
                    pe.wait_ge(xl_done, g - 3)
                for k in range(4):
                    last = pe.transpose(misc[g % 4][:, k * P:k * P + rows],
                                        xtok[0:rows, t, (4 * q + k) * P:(4 * q + k + 1) * P], ident[0:rows, 0:rows])
                last.then_inc(xt_ready, 1)

            pe.wait_ge(xl_done, 20)
            pe.wait_ge(ldt_spread, 1)
            for a in range(3):
                pe.transpose(misc[0][:, a * PAIRS:(a + 1) * PAIRS], anat[0:PAIRS, a, :], ident[0:PAIRS, 0:PAIRS])
            pe.transpose(misc[0][:, P:P + 26], vnat[0:26, :], ident[0:26, 0:26]).then_inc(prep_t_ready, 1)
            for h in range(2):
                for c in range(2):
                    last = pe.transpose(misc[1][:, (2 * h + c) * P:(2 * h + c + 1) * P], snat[:, h, c, :], ident[:])
            last.then_inc(prep_t_ready, 1)
            pe.wait_ge(cnat_loaded, 16 * 16)
            for b in range(4):
                for c in range(2):
                    last = pe.transpose(misc[2 + c][:, b * P:(b + 1) * P], cnat[:, b, c, :], ident[:])
            last.then_inc(prep_t_ready, 1)

            def multiply(n, slot, k_tiles, hi, lo, between=None, ready=None):
                pe.wait_ge(w_lo_ready, n + 1)
                pe.wait_ge(gemm_read, n + 1)
                for h, (h0, hw) in enumerate(HALVES):
                    acc = gemm[2 * slot + h][:, 0:hw]
                    for k in range(k_tiles):
                        if ready is not None and h == 0:
                            pe.wait_ge(ready, k + 1)
                        a, b = w_hi[:, slot, k * P:(k + 1) * P], w_lo[:, slot, k * P:(k + 1) * P]
                        xa, xb = hi[:, k, h0:h0 + hw], lo[:, k, h0:h0 + hw]
                        pe.matmul(acc, a, xa, start=k == 0, stop=False)
                        pe.matmul(acc, a, xb, start=False, stop=False)
                        last = pe.matmul(acc, b, xa, start=False, stop=k == k_tiles - 1)
                    if between is not None and h == 0:
                        between()
                last.then_inc(gemm_done, 1)

            def project(n, r, slot, ahead):
                multiply(n, slot, KD, xh, xl)

            blocks(pe, B_LAT, 11, project)
            blocks(pe, B_U, 8, project)

            def response(b):
                pe.wait_ge(wst_built, b + 1)
                pe.wait_ge(s_re_copied, b + 1)
                pe.wait_ge(s_im_copied, b + 1)
                pe.wait_ge(k_copied, b + 1)
                w = [wst[:, b % 2, c].rearrange("p q l c -> p q (l c)") for c in range(2)]
                for c in range(2):
                    for q in range(4):
                        last = pe.transpose(misc[c][:, q * P:(q + 1) * P], w[c][:, q], ident[:])
                last.then_inc(bt_ready, 1)
                for q in range(4):
                    for c in range(2):
                        last = pe.matmul(misc[2][:, q * 32:(q + 1) * 32], w[c][:, q],
                                         cbd[:, c, 4 * b + q].rearrange("p t c -> p (t c)"), start=c == 0, stop=c == 1)
                last.then_inc(k_ready, 1)

            def chunk_sums(b):
                pe.wait_ge(bt_re_copied, b + 1)
                pe.wait_ge(bt_im_copied, b + 1)
                for c in range(2):
                    acc = (misc[3], misc[0])[c]
                    for q in range(4):
                        for t in range(2):
                            rows = slice(t * N_STATE, (t + 1) * N_STATE)
                            last = pe.matmul(acc[rows, q * YCOLS:(q + 1) * YCOLS], bst[:, c, q, rows],
                                             xgrp[:, 8 * b + 2 * q + t, N_SAMPLE:82], start=True, stop=True)
                last.then_inc(s_ready, 1)

            for n in (B_ZS, B_ZS + 1):
                project(n, n // 2, n % 2, None)
            pe.wait_ge(prep_t_read, 11)
            pe.wait_ge(xgrp_loaded, 160)
            for b in range(8):
                response(b)
                if b < 6:
                    n = B_ZS + 2 + b
                    multiply(n, n % 2, KD, xh, xl, lambda b=b: chunk_sums(b))
                else:
                    chunk_sums(b)
            blocks(pe, B_ZA, 8, project)

            pe.wait_ge(scan_step, 3 * N_CHUNK)
            pe.wait_ge(sample_step, 3)

            def transpose_out(b):
                pe.wait_ge(y_copied, 2 * b + 2)
                for h in range(2):
                    if b:
                        pe.wait_ge(yt_added, 2 * b - 1 + h)
                    for j in range(4):
                        last = pe.transpose(misc[2 + h][:, j * YCOLS:(j + 1) * YCOLS],
                                            ychunk[0:YCOLS, b % 2, 4 * h + j, :], ident[0:YCOLS, 0:YCOLS])
                    last.then_inc(yt_ready, 1)

            for b in range(8):
                pe.wait_ge(ca_built, b + 1)
                pe.wait_ge(ca_built_pool, 2 * b + 2)
                if b % 4 == 0:
                    pe.wait_ge(toep_loaded[b // 4], 16 * CHUNK)
                for h in range(2):
                    if b:
                        pe.wait_ge(y_copied, 2 * b)
                    for q in range(2):
                        p = 4 * b + 2 * h + q
                        acc = misc[h][0:YCOLS, q * 256:(q + 1) * 256]
                        for c in range(2):
                            pe.matmul(acc, states[:, 0:YCOLS, c, p], cast[:, b % 2, c, 2 * h + q].rearrange("p t l c -> p (t l c)"),
                                      start=c == 0, stop=False)
                        for t in range(2):
                            g = 2 * p + t
                            last = pe.matmul(acc[:, t * P:(t + 1) * P].rearrange("p (l c) -> p l c", c=GROUP),
                                             xgrp[:, g, 0:YCOLS], toep[:, :, g * GROUP:(g + 1) * GROUP],
                                             start=False, stop=t == 1)
                    last.then_inc(y_ready, 1)
                if b:
                    transpose_out(b - 1)
            transpose_out(7)
            pe.wait_ge(y_copied, 16)
            for h in range(2):
                for c in range(2):
                    last = pe.transpose(misc[0][:, (2 * h + c) * P:(2 * h + c + 1) * P], snew[:, c, 4 * h:4 * h + 4].rearrange("p b q -> p (b q)"), ident[:])
            last.then_inc(state_t_ready, 1)
            for c in range(2):
                last = pe.transpose(misc[1][0:PAIRS, c * P:(c + 1) * P], states[:, ENTRIES - N_SAMPLE - 1, c, :], ident[:])
            last.then_inc(state_t_ready, 1)

            def mix(n, r, slot, ahead):
                multiply(n, slot, D_SSM // P, ys_hi, ys_lo, ready=ys_lo_done if slot == B_GLU % 2 else None)

            def sum_squares():
                pe.wait_ge(pool_step, 32 + SQ_STEPS)
                for i in range(2):
                    for h, (h0, hw) in enumerate(HALVES):
                        last = pe.matmul(misc[2 * i + h][:, 0:hw], ones[:], sq[:, i, h0:h0 + hw], start=True, stop=True)
                    last.then_inc(sums_ready, 1)

            glu_blocks(pe, mix, sum_squares)

            for n in (B_QN, B_QN + 1):
                multiply(n, n % 2, 6, qn_hi, qn_lo, ready=n_lo_done if n == B_QN else None)
            blocks(pe, B_QN + 2, 6, lambda n, r, slot, ahead: multiply(n, slot, 6, qn_hi, qn_lo))
            blocks(pe, B_QR, 4, lambda n, r, slot, ahead: multiply(n, slot, 6, qn_hi, qn_lo))
            pe.wait_ge(n_lo_done, 10)
            blocks(pe, B_K, 8, lambda n, r, slot, ahead: multiply(n, slot, 4, cn_hi, cn_lo))
            pe.wait_ge(gemm_read, B_V + 2)
            pe.wait_ge(rope_loaded, 64)
            for v in range(10):
                j, t = divmod(v, 5)
                t0, rows = TILES[t]
                n = B_V + j
                if t == 0:
                    pe.wait_ge(w_lo_ready, n + 1)
                if v >= 4:
                    pe.wait_ge(v_copied, v - 3)
                acc = gemm[v % 4][0:rows, :]
                for k in range(4):
                    wh, wl = w_hi[:, n % 2, k * 512:(k + 1) * 512], w_lo[:, n % 2, k * 512:(k + 1) * 512]
                    ch, cl = cn_hi[:, k, t0:t0 + rows], cn_lo[:, k, t0:t0 + rows]
                    pe.matmul(acc, ch, wh, start=k == 0, stop=False)
                    pe.matmul(acc, ch, wl, start=False, stop=False)
                    last = pe.matmul(acc, cl, wh, start=False, stop=k == 3)
                last.then_inc(v_ready, 1)
                if v < 5:
                    if v:
                        pe.wait_ge(rope_done, v)
                    for h, (h0, hw) in enumerate(HALVES):
                        last = pe.matmul(misc[2 + h][:, 0:hw], rot[:], rp[:, v, h0:h0 + hw], start=True, stop=True)
                    last.then_inc(rotated, 1)
                else:
                    if t >= 2:
                        pe.wait_ge(c_t_copied, t - 1)
                    for k in range(4):
                        last = pe.transpose(misc[t % 2][0:rows, k * P:(k + 1) * P], latc[:, k, t0:t0 + rows], ident[:])
                    last.then_inc(c_t_ready, 1)
            pe.wait_ge(rope_done, 5)
            pe.wait_ge(c_t_copied, 5)
            for t, (t0, rows) in enumerate(TILES):
                last = pe.transpose(misc[0][0:rows, t * QK_ROPE:(t + 1) * QK_ROPE], ev[0:QK_ROPE, 0, t0:t0 + rows], ident[0:QK_ROPE, 0:QK_ROPE])
            last.then_inc(c_t_ready, 1)

            def scores(n, m, head, before_last=None):
                i = m % 5
                u = (m // 5) % 2
                if i == 0:
                    pe.wait_ge(head_lo_done, head * 2 + 1)
                if not isinstance(n, int) or n >= 3:
                    pe.wait_ge(exp_done, n - 2)
                q0, rows = i * P, (P if i < 4 else N_META)
                width = P * max(min(i + 1, 4), 2)
                parts = ((hh, hh, kp_hi), (hh, hl, kp_lo), (hl, hh, kp_hi))
                for a, (qq, kk, kp) in enumerate(parts):
                    pe.matmul(SBANK[m][0:rows, 0:width], qq[:, u, 0, q0:q0 + rows], kk[:, u, 1, 0:width], start=a == 0, stop=False)
                    if a == 2 and before_last:
                        before_last()
                    last = pe.matmul(SBANK[m][0:rows, 0:width], qq[0:QK_ROPE, u, 2, q0:q0 + rows], kp[0:QK_ROPE, 0:width],
                                     start=False, stop=a == 2)
                if i == 4:
                    pe.wait_ge(o_gated, head + 1)
                    for a, (qq, kk, kp) in enumerate(parts):
                        pe.matmul(misc[0][0:rows, EXTRA], qq[:, u, 0, q0:q0 + rows], kk[:, u, 1, q0:q0 + rows], start=a == 0, stop=False)
                        last = pe.matmul(misc[0][0:rows, EXTRA], qq[0:QK_ROPE, u, 2, q0:q0 + rows], kp[0:QK_ROPE, q0:q0 + rows],
                                         start=False, stop=a == 2)
                last.then_inc(scores_ready, 1)

            def await_p(n, i):
                pe.wait_ge(prob_ready, n + 1)
                if not isinstance(n, int) or n >= 2:
                    pe.wait_ge(pt_lo_done, n - 1)

            def transpose_p(n, m, waited=False):
                i = m % 5
                rows = P if i < 4 else N_META
                if not waited:
                    await_p(n, i)
                bank = misc[2 + m % 2]
                for j in range(i + 1):
                    keys = P if j < 4 else N_META
                    last = pe.transpose(bank[0:keys, j * rows:(j + 1) * rows], prob[0:rows, SLOT[m], j * P:j * P + keys], ident[0:rows, 0:rows])
                last.then_inc(pt_ready, 1)

            def weigh_values(h, u):
                pe.wait_ge(head_lo_done, h * 2 + 2)
                pe.wait_ge(pt_lo_done, h * 5 + 5)
                pe.wait_ge(o_gated, h + 1)
                for acc, q0, q1, tiles in ((gemm[3][:, 0:256], 0, 256, 2), (misc[0][:, 0:272], 256, T_PROMPT, 5)):
                    for j in range(tiles):
                        keys = slice(0, P if j < 4 else N_META)
                        a0 = q0 if j < 4 else 512
                        out = acc[:, a0 - q0:q1 - q0]
                        for a, (vv, pp) in enumerate(((vh, pt_hi), (vh, pt_lo), (vl, pt_hi))):
                            last = pe.matmul(out, vv[keys, u, j], pp[keys, j, a0:q1], start=j == 0 and a == 0,
                                             stop=j == tiles - 1 and a == 2)
                last.then_inc(pv_done, 1)

            pe.sem_inc(pv_done, 1)
            pe.sem_inc(pt_ready, 1)
            pe.sem_inc(ot_ready, 1)
            pe.wait_ge(kp_lo_done, 1)
            pe.wait_ge(filled, 7)
            for t in range(2):
                scores(t, t, 0)

            def tile_pe(n, pair, k):
                i = k % 5
                narrow = i == 0 and k > 0
                if exists(n + 2):
                    scores(n + 2, (k + 2) % 10, pair * 2 + (k + 2) // 5, (lambda: await_p(n - 1, 4)) if narrow else None)
                if i == 1 and k > 1:
                    weigh_values(pair * 2 + k // 5 - 1, (k // 5 - 1) % 2)
                if exists(n - 1):
                    transpose_p(n - 1, (k - 1) % 10, narrow and exists(n + 2))

            query_tiles(pe, tile_pe)

            pe.wait_ge(sample_loaded, 16 * 6)
            pe.wait_ge(comb_lo_done, 18)
            for h in range(N_HEADS):
                if h >= 4:
                    pe.wait_ge(wuk_t_copied, h - 3)
                for k in range(4):
                    last = pe.transpose(misc[h % 4][:, k * P:(k + 1) * P], wuk[:, k, h * P:(h + 1) * P], ident[:])
                last.then_inc(wuk_t_ready, 1)
            pe.wait_ge(wuk_t_copied, 8)
            for k in range(4):
                for h in range(N_HEADS):
                    last = pe.matmul(gemm[3][:, (k * 8 + h) * 8:(k * 8 + h + 1) * 8], wuk_t[:, h, k * P:(k + 1) * P], qs[:, h, :],
                                     start=True, stop=True)
            last.then_inc(qa_ready, 1)
            pe.wait_ge(cnt_saved, 1)
            pe.wait_ge(new_lo_done, 1)
            pe.wait_ge(wuk_t_copied, 9)

            def turn_pages(g, hg, u, half):
                if hg % 2 == 0:
                    pe.wait_ge(page_loaded[u][hg // 2], (half + 1) * 128)
                if not isinstance(g, int) or g >= 2:
                    pe.wait_ge(t_lo_done, g - 1)
                k = u * N_PAGES + 2 * hg
                for j in range(2):
                    for r in range(4):
                        pe.transpose(misc[(hg % 2) * 2 + j][:, r * P:(r + 1) * P], ckv[:, k + j, r * P:(r + 1) * P], ident[:])
                if not isinstance(g, int) or g >= 1:
                    pe.wait_ge(t_lo_done, g)
                pe.transpose(gemm[0][:, 0:P], kpe[:, k:k + 2].rearrange("p a e -> p (a e)"), ident[:]).then_inc(t_ready, 1)

            def new_scores(s, u):
                pe.wait_ge(q_lo_done, s + 1)
                pe.wait_ge(sc_added, s * 5)
                out = gemm[2][0:40, 0:N_SAMPLE]
                for r in range(4):
                    pe.matmul(out, q_st[u][:, r, :], cnt_hi[:, r, :], start=r == 0, stop=False)
                    pe.matmul(out, q_st[u][:, r, :], cnt_lo[:, r, :], start=False, stop=False)
                pe.matmul(out, q_st[u][0:QK_ROPE, 4, :], kpn_hi[0:QK_ROPE, :], start=False, stop=False)
                pe.matmul(out, q_st[u][0:QK_ROPE, 4, :], kpn_lo[0:QK_ROPE, :], start=False, stop=True).then_inc(sc_ready, 1)

            def page_scores(s, u, hg, before_last=None):
                pe.wait_ge(t_lo_done, s * 8 + (hg + 1))
                if hg % 2 == 0:
                    pe.wait_ge(sc_added, s * 5 + (hg // 2 + 1))
                c0 = hg % 2 * 256
                out = gemm[2][0:40, c0:c0 + 256]
                for r in range(4):
                    pe.matmul(out, q_st[u][:, r, :], ct_hi[:, hg % 2, r, :], start=r == 0, stop=False)
                    pe.matmul(out, q_st[u][:, r, :], ct_lo[:, hg % 2, r, :], start=False, stop=False)
                for j in range(2):
                    pe.matmul(out[:, j * P:(j + 1) * P], q_st[u][:, 4 + j, :], kt_hi[:, hg % 2, :], start=False, stop=False)
                    if j == 1 and before_last:
                        before_last()
                    last = pe.matmul(out[:, j * P:(j + 1) * P], q_st[u][:, 4 + j, :], kt_lo[:, hg % 2, :], start=False, stop=j == 1)
                if hg % 2:
                    last.then_inc(sc_ready, 1)

            def turn_weights(b, v):
                for j in range(N_PAGES):
                    pe.transpose(gemm[1][:, j * N_HEADS:(j + 1) * N_HEADS], sc[v][0:N_HEADS, j * P:(j + 1) * P], ident[0:N_HEADS, 0:N_HEADS])
                pe.transpose(gemm[1][0:N_SAMPLE, P:P + N_HEADS], sc[v][0:N_HEADS, PAST:KEYS], ident[0:N_HEADS, 0:N_HEADS]).then_inc(spt_ready, 1)

            def weigh(b, hg, before_last=None):
                pe.wait_ge(p_lo_done, b * 8 + (hg + 1))
                if hg == 0:
                    pe.wait_ge(spt_lo_done, b + 1)
                    pe.wait_ge(olat_step, b * 3)
                out = gemm[3][0:40, :]
                for j in range(2):
                    pe.matmul(out, p_t[:, 2 * hg + j, :], cp_hi[:, hg % 2, j, :], start=hg == 0 and j == 0, stop=False)
                    if j == 1 and before_last:
                        before_last()
                    last = pe.matmul(out, p_t[:, 2 * hg + j, :], cp_lo[:, hg % 2, j, :], start=False, stop=False)
                last.then_inc(pv_pair_done, 1)
                if hg == 7:
                    pe.matmul(out, p_t[0:N_SAMPLE, N_PAGES, :], cnew_hi[0:N_SAMPLE, :], start=False, stop=False)
                    pe.matmul(out, p_t[0:N_SAMPLE, N_PAGES, :], cnew_lo[0:N_SAMPLE, :], start=False, stop=True).then_inc(opv_done, 1)

            def turn_latent(b):
                for k in range(4):
                    last = pe.transpose(gemm[1][:, 256 + k * 8:256 + (k + 1) * 8], olat[0:N_HEADS, k * P:(k + 1) * P], ident[0:N_HEADS, 0:N_HEADS])
                last.then_inc(ot_ready, 1)

            def sample_pe(s, u, half):
                static = isinstance(s, int)
                run, weighs, turns = not static or s < N_SAMPLE, not static or s >= 1, not static or s >= 2

                def await_exp():
                    pe.wait_ge(sexp_done, s)
                    if turns:
                        pe.wait_ge(ot_copied, s - 1)

                for hg in range(8):
                    if run and not (static and s == N_SAMPLE - 1 and hg == 7):
                        nu, nhalf = (u, half) if hg < 7 else (1 - u, half + u)
                        turn_pages(s * 8 + (hg + 1), (hg + 1) % 8, nu, nhalf)
                    if hg == 0:
                        if run:
                            new_scores(s, u)
                        if turns:
                            weigh(s - 2, 7)
                    if run:
                        page_scores(s, u, hg, await_exp if hg == 1 and weighs else None)
                    elif hg == 1:
                        await_exp()
                    if hg >= 1 and weighs:
                        if hg == 1:
                            turn_weights(s - 1, 1 - u)
                        if hg == 3 and turns:
                            def before_weigh():
                                pe.wait_ge(olat_step, s * 3 - 3)
                                pe.wait_ge(spt_lo_done, s)
                            weigh(s - 1, 2, before_weigh)
                            turn_latent(s - 2)
                        else:
                            weigh(s - 1, hg - 1)

            turn_pages(0, 0, 0, 0)
            samples(pe, sample_pe)
            weigh(7, 7)
            pe.wait_ge(olat_step, 3 * 8)
            turn_latent(7)

            pe.wait_ge(ot_copied, 9)
            pe.wait_ge(wuv_loaded, 16)
            for half in range(2):
                for h in range(4 * half, 4 * half + 4):
                    for k in range(4):
                        last = pe.matmul(gemm[half][0:N_SAMPLE, (h % 4) * P:(h % 4 + 1) * P], olat_t[:, k, h, :], wuv[:, k, h * P:(h + 1) * P],
                                         start=k == 0, stop=k == 3)
                last.then_inc(os_step, 1)
            pe.wait_ge(oh_copied, 2)
            for h in range(N_HEADS):
                last = pe.transpose(misc[0][:, h * 8:(h + 1) * 8], oh[0:N_SAMPLE, h * P:(h + 1) * P], ident[0:N_SAMPLE, 0:N_SAMPLE])
            last.then_inc(os_step, 1)
            pe.wait_ge(os_step, 8)

            def out_multiply(j, slot):
                pe.wait_ge(w_lo_ready, j + (B_OUT + 1))
                if not isinstance(j, int) or j >= 2:
                    pe.wait_ge(gemm_read, j + (B_V + 1))
                for h in range(2):
                    acc = gemm[2 * slot + h][:, 0:260]
                    c = slice(N_META + h * 260, N_META + (h + 1) * 260)
                    for k in range(KD):
                        a, b = w_hi[:, slot, k * P:(k + 1) * P], w_lo[:, slot, k * P:(k + 1) * P]
                        pe.matmul(acc, a, comb_hi[:, k, c], start=k == 0, stop=False)
                        pe.matmul(acc, a, comb_lo[:, k, c], start=False, stop=False)
                        last = pe.matmul(acc, b, comb_hi[:, k, c], start=False, stop=k == KD - 1)
                last.then_inc(gemm_done, 1)

            def out_turn(j, slot):
                pe.wait_ge(gemm_read, j + (B_V + 3))
                pe.wait_ge(out_added, j + 1)
                for t in range(4):
                    pe.transpose(misc[slot][:, t * P:(t + 1) * P], yb[:, slot, t * P:(t + 1) * P], ident[:])
                pe.transpose(misc[2 + slot][0:N_SAMPLE, 0:P], yb[:, slot, SEQ:SEQ + N_SAMPLE], ident[:]).then_inc(out_t_ready, 1)

            pe.sem_inc(out_t_ready, 2)
            out_multiply(0, 0)
            with pe.Fori(0, 7) as i:
                for u in range(2):
                    out_multiply(i * 2 + (1 + u), 1 - u)
                    out_turn(i * 2 + u, u)
            out_multiply(15, 1)
            out_turn(14, 0)
            out_turn(15, 1)


OUTPUTS = (
    ("o_y_p", (1, SEQ, D_MODEL)), ("o_y_s", (N_SAMPLE, 1, D_MODEL)),
    ("o_ckv_p", (1, 1, T_PROMPT, KV_LORA)), ("o_kpe_p", (1, 1, T_PROMPT, QK_ROPE)),
    ("o_ssm_re_p", (1, 1, N_GROUPS, N_STATE)), ("o_ssm_im_p", (1, 1, N_GROUPS, N_STATE)),
    ("o_ckv_s", (1, N_SAMPLE, 1, KV_LORA)), ("o_kpe_s", (1, N_SAMPLE, 1, QK_ROPE)),
    ("o_ssm_re_s", (1, N_SAMPLE, N_GROUPS, N_STATE)), ("o_ssm_im_s", (1, N_SAMPLE, N_GROUPS, N_STATE)),
)
SCRATCH = (
    ("lat_d", (Q_LORA + KV_LORA + P, T)),
    ("u_d", (D_SSM, T)), ("z_d", (2 * D_SSM, T)),
    ("q_d", (N_HEADS * QK_NOPE, T)), ("k_d", (N_HEADS * QK_NOPE, T)), ("v_d", (T, N_HEADS * V_HEAD)),
    ("qp_d", (N_HEADS * QK_ROPE + P, T)),
)


def rope_tables():
    half = QK_ROPE // 2
    inv = (ROPE_THETA ** (-np.arange(half) / half)).astype(np.float32)
    pos = np.concatenate([np.arange(T_PROMPT), np.full(N_SAMPLE, PAST)]).astype(np.float32)
    angle = (inv[:, None] * pos[None, :]).astype(np.float64)
    cos, sin = np.cos(angle).astype(np.float32), np.sin(angle).astype(np.float32)
    return np.concatenate([cos] * 4), np.concatenate([-sin, sin] * 2)


def kernel(**inputs):
    import concourse.bacc as bacc
    from concourse.bass_utils import run_bass_kernel_spmd

    nc = bacc.Bacc("TRN2", target_bir_lowering=False, num_devices=1)
    cos, sin = rope_tables()
    arrays = {name: np.ascontiguousarray(a) for name, a in inputs.items()}
    arrays.update(rope_cos=cos, rope_sin=sin)
    d = {name: nc.dram_tensor(name, a.shape, mybir.dt.from_np(a.dtype), kind="ExternalInput").ap() for name, a in arrays.items()}
    for name, shape in OUTPUTS:
        d[name] = nc.dram_tensor(name, shape, F32, kind="ExternalOutput").ap()
    for name, shape in SCRATCH:
        d[name] = nc.dram_tensor(name, shape, F32).ap()
    build(nc, d)
    r = run_bass_kernel_spmd(nc, [arrays], core_ids=[0])
    return tuple(r.results[0][name] for name, _ in OUTPUTS)
```
